# Optimizing a Trainium2 kernel written in Bass

```python
import math
import jax, jax.numpy as jnp
from jax import lax
import numpy as np

D_MODEL = 1024
BATCH = 1
SEQ = 256
DEPTH = 2
DEC_BATCH = 8
DEC_SEQ = 1
PAST_LEN = 2048
PAGE_SIZE = 128

N_MIXERS = 2
N_A = (DEPTH + 1) // 2
N_B = DEPTH // 2

GDN_HEADS = 8
GDN_DK = 128
GDN_DV = 128
CONV_W = 4
GDN_CHUNK = 64
GDN_CONV_DIM = GDN_HEADS * (2 * GDN_DK + GDN_DV)
GDN_PROJ = GDN_CONV_DIM + GDN_HEADS * GDN_DV + 2 * GDN_HEADS

ATT_HEADS = 8
KV_HEADS = 4
GROUP = ATT_HEADS // KV_HEADS
HEAD_DIM = D_MODEL // ATT_HEADS
ROT_DIM = HEAD_DIM // 4
ROPE_THETA = 500000.0
MOBA_BLOCK = 256
MOBA_TOPK = 3
Q_CHUNK = 16
ATT_PROJ = (ATT_HEADS + 2 * KV_HEADS) * HEAD_DIM

D_FF = 3584
N_EXPERTS = 8
TOP_K = 2
EPS = 1e-6

kernel_name = "hybrid_gdn_moba_decode_step"

def rmsnorm(x, g):
    xf = x.astype(jnp.float32)
    y = xf * lax.rsqrt(jnp.mean(xf * xf, axis=-1, keepdims=True) + EPS)
    return (y * g.astype(jnp.float32)).astype(x.dtype)

def l2norm(x):
    return x * lax.rsqrt(jnp.sum(x * x, axis=-1, keepdims=True) + 1e-6)

def swiglu(h, w_gate, w_up, w_down):
    return (jax.nn.silu(h @ w_gate) * (h @ w_up)) @ w_down

def causal_short_conv(u, prev, w):
    L = u.shape[1]
    up = jnp.concatenate([prev.astype(jnp.float32), u], axis=1)
    wf = w.astype(jnp.float32)
    out = sum(up[:, j:j + L] * wf[j] for j in range(CONV_W))
    return jax.nn.silu(out), up[:, L:]

def _to_chunks(t, n, c):
    b, _, h = t.shape[:3]
    rest = t.shape[3:]
    t = t.reshape((b, n, c, h) + rest)
    return t.transpose((1, 0, 3, 2) + tuple(range(4, 4 + len(rest))))

def gated_delta_rule(q, k, v, g, beta, s0):
    b, L, h, dk = q.shape
    dv = v.shape[-1]
    c = math.gcd(L, GDN_CHUNK)
    n = L // c
    qc = _to_chunks(q * dk ** -0.5, n, c)
    kc = _to_chunks(k, n, c)
    vc = _to_chunks(v, n, c)
    gc = _to_chunks(g, n, c)
    bc = _to_chunks(beta, n, c)
    gam = jnp.cumsum(gc, axis=-1)
    tri = jnp.tril(jnp.ones((c, c), dtype=bool))
    strict = jnp.tril(jnp.ones((c, c), dtype=bool), -1)
    dmat = jnp.exp(jnp.where(tri, gam[..., :, None] - gam[..., None, :], -jnp.inf))
    kb = kc * bc[..., None]
    a = jnp.where(strict, jnp.einsum('nbhrk,nbhjk->nbhrj', kb, kc) * dmat, 0.0)
    m = a + jnp.eye(c, dtype=jnp.float32)
    rhs = jnp.concatenate([vc * bc[..., None], kb * jnp.exp(gam)[..., None]], axis=-1)
    sol = lax.linalg.triangular_solve(m, rhs, left_side=True, lower=True, unit_diagonal=True)
    u0, kcd = sol[..., :dv], sol[..., dv:]
    attn = jnp.einsum('nbhrk,nbhjk->nbhrj', qc, kc) * dmat
    q_dec = qc * jnp.exp(gam)[..., None]
    k_dec = kc * jnp.exp(gam[..., -1:] - gam)[..., None]
    g_end = jnp.exp(gam[..., -1])

    def step(s, xs):
        u0_i, kcd_i, attn_i, qd_i, kd_i, ge_i = xs
        u = u0_i - jnp.einsum('bhrk,bhkv->bhrv', kcd_i, s)
        o = jnp.einsum('bhrk,bhkv->bhrv', qd_i, s) + jnp.einsum('bhrj,bhjv->bhrv', attn_i, u)
        s = s * ge_i[..., None, None] + jnp.einsum('bhjk,bhjv->bhkv', kd_i, u)
        return s, o

    s_fin, o = lax.scan(step, s0, (u0, kcd, attn, q_dec, k_dec, g_end))
    o = o.transpose(1, 0, 3, 2, 4).reshape(b, L, h, dv)
    return o, s_fin

def gdn_mixer(h, conv_prev, s0, w_in, conv_w, a_log, dt_bias, o_gain, w_out):
    b, L, _ = h.shape
    hk = GDN_HEADS * GDN_DK
    hv = GDN_HEADS * GDN_DV
    proj = (h @ w_in).astype(jnp.float32)
    qkv, z, beta_raw, a_raw = jnp.split(
        proj, [GDN_CONV_DIM, GDN_CONV_DIM + hv, GDN_CONV_DIM + hv + GDN_HEADS], axis=-1)
    qkv, conv_state = causal_short_conv(qkv, conv_prev, conv_w)
    q, k, v = jnp.split(qkv, [hk, 2 * hk], axis=-1)
    q = l2norm(q.reshape(b, L, GDN_HEADS, GDN_DK))
    k = l2norm(k.reshape(b, L, GDN_HEADS, GDN_DK))
    v = v.reshape(b, L, GDN_HEADS, GDN_DV)
    beta = jax.nn.sigmoid(beta_raw)
    g = -jnp.exp(a_log.astype(jnp.float32)) * jax.nn.softplus(a_raw + dt_bias.astype(jnp.float32))
    o, s_fin = gated_delta_rule(q, k, v, g, beta, s0.astype(jnp.float32))
    o = rmsnorm(o, o_gain) * jax.nn.silu(z.reshape(b, L, GDN_HEADS, GDN_DV))
    y = o.reshape(b, L, hv).astype(h.dtype) @ w_out
    return y, conv_state.astype(h.dtype), s_fin

def partial_rope(x, pos):
    half = ROT_DIM // 2
    inv = jnp.power(ROPE_THETA, -jnp.arange(half, dtype=jnp.float32) * (2.0 / ROT_DIM))
    ang = pos.astype(jnp.float32)[:, None] * inv[None, :]
    cos = jnp.cos(ang)[None, :, None, :]
    sin = jnp.sin(ang)[None, :, None, :]
    x1, x2, rest = x[..., :half], x[..., half:ROT_DIM], x[..., ROT_DIM:]
    return jnp.concatenate([x1 * cos - x2 * sin, x2 * cos + x1 * sin, rest], axis=-1)

def moba_attend(q, k_all, v_all, q_pos):
    b, L = k_all.shape[:2]
    nq_tot = q.shape[1]
    nb = -(-L // MOBA_BLOCK)
    pad = ((0, 0), (0, nb * MOBA_BLOCK - L), (0, 0), (0, 0))
    kb = jnp.pad(k_all, pad).reshape(b, nb, MOBA_BLOCK, KV_HEADS, HEAD_DIM).transpose(0, 3, 1, 2, 4)
    vb = jnp.pad(v_all, pad).reshape(b, nb, MOBA_BLOCK, KV_HEADS, HEAD_DIM).transpose(0, 3, 1, 2, 4)
    k_mean = jnp.repeat(jnp.mean(kb, axis=3), GROUP, axis=1)
    ksel = min(MOBA_TOPK, nb)
    qc = math.gcd(nq_tot, Q_CHUNK)
    n_ch = nq_tot // qc
    q_ch = q.reshape(b, n_ch, qc, ATT_HEADS, HEAD_DIM).transpose(1, 0, 2, 3, 4)
    pos_ch = q_pos.reshape(n_ch, qc)
    b_idx = jnp.arange(b)[:, None, None, None]
    h_idx = (jnp.arange(ATT_HEADS) // GROUP)[None, None, :, None]
    scale = HEAD_DIM ** -0.5

    def one_chunk(args):
        qi, pi = args
        own = pi // MOBA_BLOCK
        gate = jnp.einsum('bqhd,bhnd->bqhn', qi, k_mean)
        eligible = jnp.arange(nb)[None, :] < own[:, None]
        gate = jnp.where(eligible[None, :, None, :], gate, -jnp.inf)
        _, top = lax.top_k(gate, ksel)
        sel_ok = jnp.arange(ksel)[None, :] < jnp.minimum(own, MOBA_TOPK)[:, None]
        blocks = jnp.concatenate(
            [top, jnp.broadcast_to(own[None, :, None, None], (b, qc, ATT_HEADS, 1))], axis=-1)
        ok = jnp.concatenate(
            [jnp.broadcast_to(sel_ok[None, :, None, :], (b, qc, ATT_HEADS, ksel)),
             jnp.ones((b, qc, ATT_HEADS, 1), dtype=bool)], axis=-1)
        kg = kb[b_idx, h_idx, blocks]
        vg = vb[b_idx, h_idx, blocks]
        kpos = blocks[..., None] * MOBA_BLOCK + jnp.arange(MOBA_BLOCK)
        mask = ok[..., None] & (kpos <= pi[None, :, None, None, None])
        logits = jnp.einsum('bqhd,bqhsjd->bqhsj', qi, kg) * scale
        logits = jnp.where(mask, logits, -jnp.inf).reshape(b, qc, ATT_HEADS, -1)
        p = jax.nn.softmax(logits, axis=-1).reshape(b, qc, ATT_HEADS, ksel + 1, MOBA_BLOCK)
        return jnp.einsum('bqhsj,bqhsjd->bqhd', p, vg)

    out = lax.map(one_chunk, (q_ch, pos_ch))
    return out.transpose(1, 0, 2, 3, 4).reshape(b, nq_tot, ATT_HEADS, HEAD_DIM)

def moba_mixer(h, pos, k_past, v_past, w_in, w_out):
    b, L, _ = h.shape
    nqd = ATT_HEADS * HEAD_DIM
    nkd = KV_HEADS * HEAD_DIM
    proj = (h @ w_in).astype(jnp.float32)
    q, k, v = jnp.split(proj, [nqd, nqd + nkd], axis=-1)
    q = partial_rope(q.reshape(b, L, ATT_HEADS, HEAD_DIM), pos)
    k = partial_rope(k.reshape(b, L, KV_HEADS, HEAD_DIM), pos)
    v = v.reshape(b, L, KV_HEADS, HEAD_DIM)
    if k_past is None:
        k_all, v_all = k, v
    else:
        k_all = jnp.concatenate([k_past.astype(jnp.float32), k], axis=1)
        v_all = jnp.concatenate([v_past.astype(jnp.float32), v], axis=1)
    o = moba_attend(q, k_all, v_all, pos)
    y = o.reshape(b, L, nqd).astype(h.dtype) @ w_out
    return y, k.astype(h.dtype), v.astype(h.dtype)

def moe_swiglu(h, w_router, w_gate, w_up, w_down):
    logits = (h @ w_router).astype(jnp.float32)
    top_val, top_idx = lax.top_k(logits, TOP_K)
    wts = jax.nn.softmax(top_val, axis=-1)
    gates = jnp.sum(jax.nn.one_hot(top_idx, N_EXPERTS, dtype=jnp.float32) * wts[..., None], axis=-2)
    y = jnp.zeros(h.shape, jnp.float32)
    for e in range(N_EXPERTS):
        y = y + gates[..., e:e + 1] * swiglu(h, w_gate[e], w_up[e], w_down[e]).astype(jnp.float32)
    return y.astype(h.dtype)

def setup_inputs(seed: int = 0) -> dict:
    key = jax.random.key(seed)
    ks = jax.random.split(key, 32)
    f32 = jnp.float32
    n_pages = PAST_LEN // PAGE_SIZE
    n_used = DEC_BATCH * n_pages
    n_pool = n_used + n_used // 4
    nrm = lambda k, s, sc: jax.random.normal(k, s, f32) * sc
    dt = jnp.exp(jax.random.uniform(ks[10], (N_A, GDN_HEADS), f32, math.log(1e-3), math.log(1e-1)))
    return {
        "x_prompt": nrm(ks[0], (BATCH, SEQ, D_MODEL), 1.0),
        "x_sample": nrm(ks[1], (DEC_BATCH, DEC_SEQ, D_MODEL), 1.0),
        "state_conv": nrm(ks[2], (N_A, DEC_BATCH, CONV_W - 1, GDN_CONV_DIM), 1.0),
        "state_delta": nrm(ks[3], (N_A, DEC_BATCH, GDN_HEADS, GDN_DK, GDN_DV), GDN_DK ** -0.5),
        "cache_k": nrm(ks[4], (N_B, n_pool, PAGE_SIZE, KV_HEADS, HEAD_DIM), 1.0),
        "cache_v": nrm(ks[5], (N_B, n_pool, PAGE_SIZE, KV_HEADS, HEAD_DIM), 1.0),
        "page_table": jax.random.permutation(ks[6], n_pool)[:n_used].reshape(DEC_BATCH, n_pages).astype(jnp.int32),
        "norm_mix": 1.0 + nrm(ks[7], (DEPTH, D_MODEL), 0.02),
        "norm_ffn": 1.0 + nrm(ks[8], (DEPTH, D_MODEL), 0.02),
        "norm_final": 1.0 + nrm(ks[9], (D_MODEL,), 0.02),
        "gdn_w_in": nrm(ks[11], (N_A, D_MODEL, GDN_PROJ), D_MODEL ** -0.5),
        "gdn_conv_w": nrm(ks[12], (N_A, CONV_W, GDN_CONV_DIM), CONV_W ** -0.5),
        "gdn_a_log": jnp.log(jax.random.uniform(ks[13], (N_A, GDN_HEADS), f32, 1.0, 16.0)),
        "gdn_dt_bias": dt + jnp.log(-jnp.expm1(-dt)),
        "gdn_o_norm": 1.0 + nrm(ks[14], (N_A, GDN_DV), 0.02),
        "gdn_w_out": nrm(ks[15], (N_A, GDN_HEADS * GDN_DV, D_MODEL), (GDN_HEADS * GDN_DV) ** -0.5),
        "att_w_in": nrm(ks[16], (N_B, D_MODEL, ATT_PROJ), D_MODEL ** -0.5),
        "att_w_out": nrm(ks[17], (N_B, ATT_HEADS * HEAD_DIM, D_MODEL), (ATT_HEADS * HEAD_DIM) ** -0.5),
        "ffn_w_gate": nrm(ks[18], (N_A, D_MODEL, D_FF), D_MODEL ** -0.5),
        "ffn_w_up": nrm(ks[19], (N_A, D_MODEL, D_FF), D_MODEL ** -0.5),
        "ffn_w_down": nrm(ks[20], (N_A, D_FF, D_MODEL), D_FF ** -0.5),
        "moe_router": nrm(ks[21], (N_B, D_MODEL, N_EXPERTS), D_MODEL ** -0.5),
        "moe_w_gate": nrm(ks[22], (N_B, N_EXPERTS, D_MODEL, D_FF), D_MODEL ** -0.5),
        "moe_w_up": nrm(ks[23], (N_B, N_EXPERTS, D_MODEL, D_FF), D_MODEL ** -0.5),
        "moe_w_down": nrm(ks[24], (N_B, N_EXPERTS, D_FF, D_MODEL), D_FF ** -0.5),
    }

def reference(x_prompt, x_sample, state_conv, state_delta, cache_k, cache_v, page_table,
              norm_mix, norm_ffn, norm_final,
              gdn_w_in, gdn_conv_w, gdn_a_log, gdn_dt_bias, gdn_o_norm, gdn_w_out,
              att_w_in, att_w_out,
              ffn_w_gate, ffn_w_up, ffn_w_down,
              moe_router, moe_w_gate, moe_w_up, moe_w_down):
    bp, seq, _ = x_prompt.shape
    db, dec_seq, _ = x_sample.shape
    n_pages = page_table.shape[1]
    past_len = n_pages * cache_k.shape[2]
    pos_p = jnp.arange(seq, dtype=jnp.int32)
    pos_s = past_len + jnp.arange(dec_seq, dtype=jnp.int32)
    hp, hs = x_prompt, x_sample
    conv_p, delta_p, k_p, v_p = [], [], [], []
    conv_s, delta_s, k_s, v_s = [], [], [], []
    for i in range(DEPTH):
        j = i // N_MIXERS
        if i % N_MIXERS == 0:
            zero_conv = jnp.zeros((bp, CONV_W - 1, GDN_CONV_DIM), hp.dtype)
            zero_s = jnp.zeros((bp, GDN_HEADS, GDN_DK, GDN_DV), jnp.float32)
            yp, cp, sp = gdn_mixer(rmsnorm(hp, norm_mix[i]), zero_conv, zero_s, gdn_w_in[j], gdn_conv_w[j],
                                   gdn_a_log[j], gdn_dt_bias[j], gdn_o_norm[j], gdn_w_out[j])
            ys, cs, ss = gdn_mixer(rmsnorm(hs, norm_mix[i]), state_conv[j], state_delta[j], gdn_w_in[j], gdn_conv_w[j],
                                   gdn_a_log[j], gdn_dt_bias[j], gdn_o_norm[j], gdn_w_out[j])
            hp = hp + yp
            hs = hs + ys
            conv_p.append(cp)
            delta_p.append(sp.astype(state_delta.dtype))
            conv_s.append(cs)
            delta_s.append(ss.astype(state_delta.dtype))
            hp = hp + swiglu(rmsnorm(hp, norm_ffn[i]), ffn_w_gate[j], ffn_w_up[j], ffn_w_down[j])
            hs = hs + swiglu(rmsnorm(hs, norm_ffn[i]), ffn_w_gate[j], ffn_w_up[j], ffn_w_down[j])
        else:
            k_past = cache_k[j][page_table].reshape(db, past_len, KV_HEADS, HEAD_DIM)
            v_past = cache_v[j][page_table].reshape(db, past_len, KV_HEADS, HEAD_DIM)
            yp, kp, vp = moba_mixer(rmsnorm(hp, norm_mix[i]), pos_p, None, None, att_w_in[j], att_w_out[j])
            ys, kn, vn = moba_mixer(rmsnorm(hs, norm_mix[i]), pos_s, k_past, v_past, att_w_in[j], att_w_out[j])
            hp = hp + yp
            hs = hs + ys
            k_p.append(kp)
            v_p.append(vp)
            k_s.append(kn)
            v_s.append(vn)
            hp = hp + moe_swiglu(rmsnorm(hp, norm_ffn[i]), moe_router[j], moe_w_gate[j], moe_w_up[j], moe_w_down[j])
            hs = hs + moe_swiglu(rmsnorm(hs, norm_ffn[i]), moe_router[j], moe_w_gate[j], moe_w_up[j], moe_w_down[j])
    y_prompt = rmsnorm(hp, norm_final)
    y_sample = rmsnorm(hs, norm_final)
    conv_prompt = jnp.stack(conv_p)
    delta_prompt = jnp.stack(delta_p)
    k_prompt = jnp.stack(k_p)
    v_prompt = jnp.stack(v_p)
    conv_sample = jnp.stack(conv_s)
    delta_sample = jnp.stack(delta_s)
    k_sample = jnp.stack(k_s)
    v_sample = jnp.stack(v_s)
    return (y_prompt, y_sample, conv_prompt, delta_prompt, k_prompt, v_prompt,
            conv_sample, delta_sample, k_sample, v_sample)


_drawn_inputs = setup_inputs


def setup_inputs(seed=0):
    import zlib

    import numpy as np

    out = dict(_drawn_inputs(seed))
    spreads = {}
    factors = {}
    for name, (base, spread) in spreads.items():
        noise = np.random.default_rng([zlib.crc32(name.encode()), seed]).standard_normal(out[name].shape)
        drawn = base * np.exp(spread * noise) if base else spread * noise
        out[name] = __import__('jax').numpy.asarray(drawn.astype(out[name].dtype))
    for name, factor in factors.items():
        out[name] = (out[name] * factor).astype(out[name].dtype)
    return out
```

```python
from contextlib import ExitStack

import numpy as np

import concourse.bass as bass
from concourse import mybir

F32 = mybir.dt.float32
I32 = mybir.dt.int32
ALU = mybir.AluOpType
ACT = mybir.ActivationFunctionType
AX = mybir.AxisListType.X

P = 128
D = 1024
KT = D // P
NPR = 256
NS = 8
T = NPR + NS
TOK_TILES = ((0, P), (P, P), (NPR, NS))
H = 8
KVH = 4
DK = 128
CONV_W = 4
QKV = 3 * H
CH = 2
NI = CH * H
GRP = 4
NG = NI // GRP
LEVELS = 7
FT = 3584 // P
NE = 8
N_PAGES = 16
PAGE = 128
PPC = 8
BLOCKS = N_PAGES * PAGE // 256
TOPK = 3
ROT = 32
POS0 = N_PAGES * PAGE
SCALE = DK ** -0.5
EPS = 1e-6
BIG = 1e30

SLOTS = 8
SLOT = 4096
C_IN = 0
C_STATE = C_IN + 8
C_OUT = C_STATE + 2
C_GU = C_OUT + 2
C_DOWN = C_GU + FT // 2
C_AIN = C_DOWN + KT
C_K = C_AIN + 4
C_V = C_K + 2 * NS
C_AOUT = C_V + 2 * NS
C_MOE = C_AOUT + 2
MOE_CHUNKS = FT // 2 + KT
STORES = 6
assert C_MOE % SLOTS == 0


def fills_per_chunk(n):
    return 16 * (PPC if C_K <= n < C_AOUT else 1)


def full_value(n):
    return sum(fills_per_chunk(m) for m in range(n % SLOTS, n + 1, SLOTS))


def moe_fills(slot):
    return 16 * len(range(slot, MOE_CHUNKS, SLOTS))


CST = {}
_at = 0
for _name, _n in (("ident", P), ("ones", P), ("upper", P), ("causal", P), ("before", 64), ("eps", 2)):
    CST[_name] = (_at, _n)
    _at += _n
CST_N = _at
PRM = {}
_at = 0
for _name, _n in (("gain", 5 * KT), ("o_gain", 1), ("conv_w", QKV * CONV_W), ("a_log", H), ("dt_bias", H),
                  ("router", KT * NE), ("w_small", KT * 2 * H)):
    PRM[_name] = (_at, _n)
    _at += _n
PRM_N = _at
ROPE_N = ROT + 2 * T


def program(nc, x_in, cst_in, lmask_in, rope_in, prm_in, conv_in, table_in, gdn_in_w, state_in, gdn_out_w,
            ffn_gu, ffn_down, att_in_w, k_pages, v_pages, att_out_w, moe_gu, moe_down,
            y_out, convp_out, convs_out, deltap_out, deltas_out, kv_out):
    with ExitStack() as ctx:
        def sb(name, shape, dt=F32):
            return ctx.enter_context(nc.sbuf_tensor(name, shape, dt))

        def sem(name):
            return ctx.enter_context(nc.semaphore(name))

        ring = sb("ring", [P, SLOTS, SLOT])
        xT = sb("xT", [P, KT, T])
        hT = sb("hT", [P, KT, T])
        scr = sb("scr", [P, 48 * T])
        cst = sb("cst", [P, CST_N])
        prm = sb("prm", [P, PRM_N])
        conv_prev = sb("conv_prev", [P, QKV, CONV_W - 1, NS])
        raw = sb("raw", [P, 2, CONV_W - 1 + T])
        conv_last = sb("conv_last", [P, QKV, CONV_W - 1])
        conv_new = sb("conv_new", [P, QKV, NS])
        small = sb("small", [P, 768])
        table = sb("table", [1, NS * N_PAGES], I32)
        bank = [ctx.enter_context(nc.psum_tensor(f"bank{i}", [P, 512], F32))[:, :] for i in range(8)]

        def c_(name):
            a, n = CST[name]
            return cst[:, a:a + n]

        def p_(name):
            a, n = PRM[name]
            return prm[:, a:a + n]

        ident, ones, upper, causal = c_("ident"), c_("ones"), c_("upper"), c_("causal")
        before = c_("before").rearrange("p (i j) -> p i j", i=8)
        eps, eps_q = cst[:, CST["eps"][0]:CST["eps"][0] + 1], cst[:, CST["eps"][0] + 1:CST["eps"][0] + 2]
        gain = p_("gain").rearrange("p (l k) -> p l k", k=KT)
        conv_w = p_("conv_w").rearrange("p (c j) -> p c j", j=CONV_W)
        router = p_("router").rearrange("p (k e) -> p k e", e=NE)
        w_small = p_("w_small").rearrange("p (k e) -> p k e", e=2 * H)
        rms = raw[:, 0, CONV_W - 1:]

        def carve(base, at, *dims):
            n = int(np.prod(dims))
            v = base[:, at:at + n]
            if len(dims) == 2:
                v = v.rearrange("p (a b) -> p a b", b=dims[1])
            if len(dims) == 3:
                v = v.rearrange("p (a b c) -> p a b c", b=dims[1], c=dims[2])
            return v

        qkv = carve(scr, 0, QKV, T)
        zT = carve(scr, QKV * T, H, T)
        nrm = carve(scr, (QKV + H) * T, 2 * H, T)
        oT = carve(scr, (QKV + H) * T, H, T)
        osq = carve(scr, (QKV + 2 * H) * T, H, T)
        core = ring[:, 4:8, :].rearrange("p s n -> p (s n)")
        ktok = carve(core, 0, NI, P)
        vtok = carve(core, 2048, NI, P)
        coefT = carve(core, 4096, NI, P)
        attT = carve(core, 6144, NI, P)
        X = carve(core, 8192, NI, P)
        Z = carve(core, 10240, NI, P)
        Y = carve(core, 12288, NI, P)
        lmask = carve(core, 14336, LEVELS, P)
        decT = carve(core, 15232, 2, GRP * P)
        rhs_w = X[:, 0:8, :]
        u_tok = X[:, 8:16, :]
        S_new = Y[:, 0:8, :]
        S_fin = Y[:, 8:16, :]
        wide = decT[0:64]
        kv_rows = carve(core, 14336, 2, P)[0:64]
        states = ring[:, 0:2, :].rearrange("p s n -> p (s n)").rearrange("p (i v) -> p i v", v=DK)
        sm_at = [0]

        def sm(*dims):
            v = carve(small, sm_at[0], *dims)
            sm_at[0] += int(np.prod(dims))
            return v

        ba = sm(3, 2 * H)
        beta = sm(3, H)
        gdec = sm(3, H)
        t_abs = sm(3, H)
        t_exp = sm(3, H)
        e_alog = sm(H)
        cum = sm(CH, H)
        neg_ecum = sm(CH, H)
        to_end = sm(CH, H)
        e_end = sm(CH, H)
        ge_s = sm(H)
        diag8 = sm(2, 64)
        row_b = sm(2, 64)
        sk = sm(64)
        sq_ = sm(64)
        qk_ = sm(64)
        u_s = sm(64)
        sil = carve(scr, 47 * T - T, 2, T)
        aT = carve(scr, 0, FT, T)
        gate_b = carve(scr, FT * T, NE, T)
        aq = carve(scr, 0, 16, T)
        rope = scr[:, 16 * T:16 * T + ROPE_N]
        rot_p = rope[:, 0:ROT]
        cosT, sinT = rope[0:ROT, ROT:ROT + T], rope[0:ROT, ROT + T:ROT + 2 * T]
        at = 16 * T + ROPE_N
        rot_t = carve(scr, at, T); at += T
        v_tok = carve(scr, at, CH * KVH, P); at += CH * KVH * P
        logit = carve(scr, at, NS, P); at += NS * P
        prob = carve(scr, at, NS, P); at += NS * P
        o_att = carve(scr, at, H, T); at += H * T
        pr_s = carve(scr, at, 2, 384); at += 768
        pr_T = carve(scr, at, 2, 384); at += 768
        a_small = scr[:, at:48 * T]
        st_max, st_sum = a_small[:, 0:8], a_small[:, 8:16]
        pmax, psums, prec = a_small[:, 16:20], a_small[:, 20:24], a_small[:, 24:28]
        hflat = hT[:, :, :].rearrange("p k t -> p (k t)")
        mx8 = hflat[0:8, 0:128]
        gs8 = hflat[0:8, 128:256]
        gate8 = carve(hflat, 256, 8, 8)[0:8]
        cmp8 = carve(hflat, 320, 8, 8, 8)[0:8]
        eq8 = carve(hflat, 832, 8, 8, 8)[0:8]
        rank8 = carve(hflat, 1344, 8, 8)[0:8]
        bm8 = carve(hflat, 1408, 8, 8)[0:8]
        m8 = hflat[0:8, 1472:1480]
        lnew = hflat[0:8, 1480:1488]
        pn8 = hflat[0:8, 1488:1496]
        bias8 = hflat[0:8, 1496:1624]
        prodn = carve(hflat, 1624, H, NS)
        pnd = carve(hflat, 1688, H, NS)
        pnb = carve(hflat, 1752, H, NS)
        den = carve(hflat, 1816, NS, H)
        bias_wide = scr[0:8, at - 1536:at - 512].rearrange("p (b n) -> p b n", b=8)
        r_at = FT * T + NE * T
        gate_d = carve(scr, r_at, NE, T)
        weighted = carve(scr, r_at + NE * T, 2, T)
        rl = sm(3, NE)
        rcmp = carve(scr, 0, 3 * NE, NE)
        req = carve(scr, 192, 3 * NE, NE)
        rrank = carve(scr, 384, 3, NE)
        rmax = carve(scr, 408, 3)
        rgate = carve(scr, 416, 3, NE)
        gT = scr[0:8, 448:448 + T]

        ring_full = [sem(f"ring_full{s}") for s in range(SLOTS)]
        x_loaded, prm_loaded, lmask_loaded, rope_loaded = sem("x_loaded"), sem("prm_loaded"), sem("lmask_loaded"), sem("rope_loaded")
        table_loaded = sem("table_loaded")
        stored = sem("stored")
        states_stored = sem("states_stored")
        consts_set = sem("consts_set")
        squares, sum_sq, root, normed = sem("squares"), sem("sum_sq"), sem("root"), sem("normed")
        dve_link, act_link, pool_link = sem("dve_link"), sem("act_link"), sem("pool_link")
        proj, raw_ready, conv_done, z_ready = sem("proj"), sem("raw_ready"), sem("conv_done"), sem("z_ready")
        raw_saved, conv_s_done, silu_done, small_ready = sem("raw_saved"), sem("conv_s_done"), sem("silu_done"), sem("small_ready")
        qk_sq, qk_sum, qk_root, qk_normed = sem("qk_sq"), sem("qk_sum"), sem("qk_root"), sem("qk_normed")
        gates_a, gates_e, gates_done = sem("gates_a"), sem("gates_e"), sem("gates_done")
        cum_ps, cum_sb, cum_exp = sem("cum_ps"), sem("cum_sb"), sem("cum_exp")
        rowdec, arg_done, dec_exp, ecum_row, kk_ready, coef_done = (
            sem("rowdec"), sem("arg_done"), sem("dec_exp"), sem("ecum_row"), sem("kk_ready"), sem("coef_done"))
        turned, turned_sb = sem("turned"), sem("turned_sb")
        y_ps, y_sb, x_ps, z_ps, x_sb, z_sb = sem("y_ps"), sem("y_sb"), sem("x_ps"), sem("z_ps"), sem("x_sb"), sem("z_sb")
        kdec_done, q_dec_done = sem("kdec_done"), sem("q_dec_done")
        ks_ps, w_sb, u_ps, u_sb, s_ps, s_sb, o_ps, o_sb = (
            sem("ks_ps"), sem("w_sb"), sem("u_ps"), sem("u_sb"), sem("s_ps"), sem("s_sb"), sem("o_ps"), sem("o_sb"))
        core_done = sem("core_done")
        sdiag, srow_ps, sread_ps, sdecayed, su_done, st_ps, st_sb, sou, sout_ps, snew = (
            sem("sdiag"), sem("srow_ps"), sem("sread_ps"), sem("sdecayed"), sem("su_done"), sem("st_ps"), sem("st_sb"),
            sem("sou"), sem("sout_ps"), sem("snew"))
        osq_done, osum, oroot, o_normed = sem("osq_done"), sem("osum"), sem("oroot"), sem("o_normed")
        outp, out_added = sem("outp"), sem("out_added")
        f_gate, f_up, f_silu, f_act, f_down, f_added = (sem(f"f_{n}") for n in ("gate", "up", "silu", "act", "down", "added"))
        m_gate, m_up, m_silu, m_act, m_down, m_added = (sem(f"m_{n}") for n in ("gate", "up", "silu", "act", "down", "added"))
        x_sum = sem("x_sum")
        aproj, aproj_sb, rot_ps, roped, v_ps, v_sb = sem("aproj"), sem("aproj_sb"), sem("rot_ps"), sem("roped"), sem("v_ps"), sem("v_sb")
        sc_ps, sc_max, sc_exp, p_sb, pT_ps, pT_sb, po_ps, po_sb = (
            sem("sc_ps"), sem("sc_max"), sem("sc_exp"), sem("p_sb"), sem("pT_ps"), sem("pT_sb"), sem("po_ps"), sem("po_sb"))
        k_read, l_sb, l_turned, st_red, st_turned, prod_done, lnew_ps, bias_done = (
            sem("k_read"), sem("l_sb"), sem("l_turned"), sem("st_red"), sem("st_turned"), sem("prod_done"), sem("lnew_ps"), sem("bias_done"))
        pn_arg, pn_exp, pnd_done, bias_ps, parg, pexp, den_ps, v_read, od_done = (
            sem("pn_arg"), sem("pn_exp"), sem("pnd_done"), sem("bias_ps"), sem("parg"), sem("pexp"), sem("den_ps"), sem("v_read"), sem("od_done"))
        aout, aout_added = sem("aout"), sem("aout_added")
        r_ps, r_arg, r_exp, r_gate, r_turned, r_diag, gb_ps, gb_sb = (
            sem("r_ps"), sem("r_arg"), sem("r_exp"), sem("r_gate"), sem("r_turned"), sem("r_diag"), sem("gb_ps"), sem("gb_sb"))

        mm = nc.tensor.matmul

        def tile4(n):
            return ring[:, n % SLOTS, :].rearrange("p (c k m) -> p c k m", c=4, k=KT)

        block = ctx.enter_context(nc.Block())

        @block.sync
        def _(sp):
            def slot_free(n):
                m = n - SLOTS
                if m < 0:
                    return
                if m < C_STATE:
                    sp.wait_ge(proj, 4 * (m + 1))
                elif m < C_OUT:
                    sp.wait_ge(states_stored, 16)
                elif m < C_GU:
                    sp.wait_ge(outp, 4 * (m - C_OUT + 1))
                elif m < C_DOWN:
                    sp.wait_ge(f_up, 2 * (m - C_GU + 1))
                elif m < C_AIN:
                    sp.wait_ge(f_down, m - C_DOWN + 1)
                elif m < C_K:
                    sp.wait_ge(aproj, 4 * (m - C_AIN + 1))
                elif m < C_V:
                    sp.wait_ge(k_read, m - C_K + 1)
                elif m < C_AOUT:
                    sp.wait_ge(v_read, m - C_V + 1)
                else:
                    sp.wait_ge(aout, 4 * (m - C_AOUT + 1))

            def load(n, src, size=SLOT):
                slot_free(n)
                if 4 <= n - C_STATE < 8:
                    sp.wait_ge(core_done, 1)
                sp.dma_start(ring[:, n % SLOTS, 0:size], src).then_inc(ring_full[n % SLOTS], 16)

            for n in range(8):
                load(C_IN + n, gdn_in_w[n])
            for n in range(2):
                load(C_STATE + n, state_in[n])
            for n in range(2):
                load(C_OUT + n, gdn_out_w[n])
            sp.wait_ge(proj, 4 * 8)
            sp.dma_start(core[:, 14336:15232], lmask_in).then_inc(lmask_loaded, 16)
            for n in range(FT // 2):
                load(C_GU + n, ffn_gu[n])
            for n in range(KT):
                load(C_DOWN + n, ffn_down[n], FT * P)
            for n in range(4):
                load(C_AIN + n, att_in_w[n])
            sp.wait_ge(table_loaded, 16)
            for first, pages in ((C_K, k_pages), (C_V, v_pages)):
                for c in range(2 * NS):
                    n = first + c
                    slot_free(n)
                    with sp.Fori(0, PPC) as page:
                        at_page = sp.value_load(table[0:1, bass.ds(page + c * PPC, 1)], min_val=0,
                                                max_val=k_pages.shape[0] - 1)
                        dst = ring[:, n % SLOTS, bass.ds(page * (SLOT // PPC), SLOT // PPC)]
                        sp.dma_start(dst, pages[bass.ds(at_page, 1)].rearrange("a p n -> p (a n)"))\
                          .then_inc(ring_full[n % SLOTS], 16)
            for n in range(2):
                load(C_AOUT + n, att_out_w[n])

            def load_expert(e, first):
                for i in range(MOE_CHUNKS):
                    m = i - SLOTS
                    if m >= 0:
                        if m < FT // 2:
                            sp.wait_ge(m_up, e * FT + 2 * (m + 1))
                        else:
                            sp.wait_ge(m_down, e * KT + m - FT // 2 + 1)
                    elif first:
                        slot_free(C_MOE + i)
                    else:
                        prev = max(j for j in range(MOE_CHUNKS) if j % SLOTS == i % SLOTS)
                        if prev < FT // 2:
                            sp.wait_ge(m_up, e * FT + (2 * (prev + 1) - FT))
                        else:
                            sp.wait_ge(m_down, e * KT + (prev - FT // 2 + 1 - KT))
                    if i < FT // 2:
                        src, size = moe_gu, SLOT
                        row = e * (FT // 2) + i
                    else:
                        src, size = moe_down, FT * P
                        row = e * KT + i - FT // 2
                    if first:
                        sp.dma_start(ring[:, i % SLOTS, 0:size], src[row]).then_inc(ring_full[i % SLOTS], 16)
                    else:
                        sp.dma_start(ring[:, i % SLOTS, 0:size], src[bass.ds(row, 1)].rearrange("a p n -> p (a n)"))\
                          .then_inc(ring_full[i % SLOTS], 16)

            load_expert(0, True)
            with sp.Fori(1, NE) as e:
                load_expert(e, False)
            sp.wait_ge(stored, 16 * STORES)

        @block.tensor
        def _(pe):
            def arrived(n):
                pe.wait_ge(ring_full[n % SLOTS], full_value(n))

            def norm_sums(i):
                pe.wait_ge(squares, i + 1)
                for k in range(KT):
                    last = mm(bank[7][:, 0:T], ones, hT[:, k, :], start=(k == 0), stop=(k == KT - 1))
                last.then_inc(sum_sq, 1)

            pe.wait_ge(prm_loaded, 48)
            norm_sums(0)
            for c in range(QKV + H):
                if c % 4 == 0:
                    arrived(C_IN + c // 4)
                if c >= 4:
                    if c - 4 < QKV:
                        pe.wait_ge(raw_ready, c - 3)
                    else:
                        pe.wait_ge(z_ready, c - 4 - QKV + 1)
                for k in range(KT):
                    if c == 0:
                        pe.wait_ge(normed, k + 1)
                    last = mm(bank[c % 4][:, 0:T], tile4(C_IN + c // 4)[:, c % 4, k, :], hT[:, k, :],
                              start=(k == 0), stop=(k == KT - 1))
                last.then_inc(proj, 1)
            for i, (t0, n) in enumerate(TOK_TILES):
                for k in range(KT):
                    last = mm(bank[4][0:n, 16 * i:16 * i + 16], hT[:, k, t0:t0 + n], w_small[:, k, :],
                              start=(k == 0), stop=(k == KT - 1))
            last.then_inc(small_ready, 1)
            pe.wait_ge(qk_sq, 1)
            for c in range(2 * H):
                if c < 4:
                    pe.wait_ge(z_ready, H)
                else:
                    pe.wait_ge(qk_root, c - 3)
                mm(bank[c % 4][:, 0:T], ones, nrm[:, c, :], start=True, stop=True).then_inc(qk_sum, 1)
            pe.wait_ge(gates_done, 1)
            for c in range(CH):
                mm(bank[5][:, 8 * c:8 * c + 8], upper, gdec[:, c, :], start=True, stop=True)
            mm(bank[5][:, 16:32], ones, gdec[:, 0:2, :].rearrange("p c h -> p (c h)"),
               start=True, stop=True).then_inc(cum_ps, 1)
            pe.wait_ge(qk_normed, 4)

            def turn(g, src):
                n = 2 * g + src
                if n >= 2:
                    pe.wait_ge(turned_sb, n - 1)
                for j in range(GRP):
                    i = GRP * g + j
                    c, h = i // H, i % H
                    last = nc.tensor.transpose(bank[6 + n % 2][:, P * j:P * (j + 1)],
                                               qkv[:, H * (1 + src) + h, P * c:P * (c + 1)], ident)
                last.then_inc(turned, 1)

            for g in range(NG):
                if g == 0:
                    pe.wait_ge(qk_root, 2 * H)
                elif g < 3:
                    pe.wait_ge(arg_done, g)
                else:
                    pe.wait_ge(ecum_row, 1)
                for j in range(GRP):
                    c, h = (GRP * g + j) // H, (GRP * g + j) % H
                    last = mm(bank[0][:, P * j:P * (j + 1)], gdec[:, c, h:h + 1].to_broadcast([P, P]), upper,
                              start=True, stop=True)
                last.then_inc(rowdec, 1)
                if g >= 1:
                    pe.wait_ge(coef_done, g)
                for b, q in ((1, 1), (2, 0)):
                    for j in range(GRP):
                        c, h = (GRP * g + j) // H, (GRP * g + j) % H
                        last = mm(bank[b][:, P * j:P * (j + 1)], qkv[:, H + h, P * c:P * (c + 1)],
                                  qkv[:, q * H + h, P * c:P * (c + 1)], start=True, stop=True)
                last.then_inc(kk_ready, 1)
                turn(g, 0)
                turn(g, 1)
            arrived(C_STATE)
            arrived(C_STATE + 1)
            for h in range(H):
                for b in range(NS):
                    i = h * NS + b
                    last = mm(bank[3][:, 2 * i:2 * i + 2], states[:, i, :], qkv[:, h:h + H + 1:H, NPR + b],
                              start=True, stop=True)
            last.then_inc(sread_ps, 1)
            pe.wait_ge(sdiag, 1)
            for r in range(2):
                mm(bank[5][:, 64 * r:64 * r + 64], ones[0:NS, :], diag8[0:NS, r, :], start=True, stop=True)
            mm(bank[5][:, 128:192], ones, qk_, start=True, stop=True).then_inc(srow_ps, 1)

            for l in range(LEVELS):
                for g in range(NG):
                    if l == 0:
                        pe.wait_ge(coef_done, NG)
                        pe.wait_ge(ecum_row, 2)
                        if g == 3:
                            pe.wait_ge(su_done, 1)
                    else:
                        pe.wait_ge(x_sb, NG * (l - 1) + g + 1)
                    for j in range(GRP):
                        i = GRP * g + j
                        out = bank[g][:, P * j:P * (j + 1)]
                        if l == 0:
                            last = nc.tensor.transpose(out, coefT[:, i, :], ident)
                        else:
                            last = mm(out, coefT[:, i, :], X[:, i, :], start=True, stop=True)
                    last.then_inc(y_ps, 1)
                for g in range(NG):
                    pe.wait_ge(y_sb, NG * l + g + 1)
                    bx, bz = bank[4 + g % 2], bank[6 + g % 2]
                    if l == 0 and g < 2:
                        pe.wait_ge(turned_sb, 2 * NG)
                        pe.wait_ge(su_done, 1)
                    if NG * l + g >= 2:
                        pe.wait_ge(z_sb, NG * l + g - 1)
                    if 0 < l < LEVELS - 1:
                        for j in range(GRP):
                            i = GRP * g + j
                            last = mm(bx[:, P * j:P * (j + 1)], Z[:, i, :], Y[:, i, :], start=True, stop=True)
                        last.then_inc(x_ps, 1)
                    for j in range(GRP):
                        i = GRP * g + j
                        if l == 0:
                            last = nc.tensor.transpose(bz[:, P * j:P * (j + 1)], Y[:, i, :], ident)
                        else:
                            last = mm(bz[:, P * j:P * (j + 1)], Y[:, i, :], Z[:, i, :], start=True, stop=True)
                    last.then_inc(z_ps, 1)
            pe.wait_ge(z_sb, NG * LEVELS)
            for c in range(CH):
                if c == 1:
                    pe.wait_ge(s_sb, 2)
                    for g in range(2):
                        for j in range(GRP):
                            h = GRP * g + j
                            last = mm(bank[g][:, P * j:P * (j + 1)], qkv[:, H + h, P:2 * P], S_new[:, h, :],
                                      start=True, stop=True)
                        last.then_inc(ks_ps, 1)
                for g in range(2):
                    if c == 1:
                        pe.wait_ge(w_sb, g + 1)
                    for j in range(GRP):
                        h = GRP * g + j
                        rhs = vtok[:, h, :] if c == 0 else rhs_w[:, h, :]
                        last = mm(bank[2 + g][:, P * j:P * (j + 1)], Z[:, H * c + h, :], rhs, start=True, stop=True)
                    last.then_inc(u_ps, 1)
                for g in range(2):
                    pe.wait_ge(u_sb, 2 * c + g + 1)
                    if c == 1:
                        pe.wait_ge(s_sb, 2)
                    if c == 0 and g == 0:
                        pe.wait_ge(kdec_done, 1)
                    for j in range(GRP):
                        h = GRP * g + j
                        last = mm(bank[4 + g][:, P * j:P * (j + 1)], ktok[:, H * c + h, :], u_tok[:, h, :],
                                  start=True, stop=True)
                    last.then_inc(s_ps, 1)
                    if c == 1:
                        pe.wait_ge(q_dec_done, 1)
                        pe.wait_ge(o_sb, g + 1)
                    for j in range(GRP):
                        h = GRP * g + j
                        out = bank[6 + g][:, P * j:P * (j + 1)]
                        last = mm(out, u_tok[:, h, :], attT[:, H * c + h, :], start=True, stop=(c == 0))
                        if c == 1:
                            last = mm(out, S_new[:, h, :], qkv[:, h, P:2 * P], start=False, stop=True)
                    last.then_inc(o_ps, 1)
            pe.wait_ge(sou, 1)
            pe.wait_ge(w_sb, 2)
            nc.tensor.transpose(bank[0][0:64, 0:P], u_s, ident)
            nc.tensor.transpose(bank[0][0:64, P:2 * P],
                                sk, ident).then_inc(st_ps, 1)
            for i in range(16):
                pe.wait_ge(st_sb, 2 + i)
                if i < 2:
                    pe.wait_ge(u_sb, 4)
                else:
                    pe.wait_ge(snew, i - 1)
                mm(bank[2 + i % 2], kv_rows[:, 1, :], wide[:, i % 2, :], start=True, stop=True).then_inc(sout_ps, 1)
            for h in range(H):
                pe.wait_ge(osq_done, h + 1)
                if h < 2:
                    pe.wait_ge(snew, 16)
                else:
                    pe.wait_ge(oroot, h - 1)
                mm(bank[2 + h % 2][:, 0:T], ones, osq[:, h, :], start=True, stop=True).then_inc(osum, 1)

            def out_projection(first, src, src_ready, done, added):
                for d in range(KT):
                    if d % 4 == 0:
                        arrived(first + d // 4)
                    if d >= 4:
                        pe.wait_ge(added, d - 3)
                    for h in range(H):
                        if d == 0:
                            src_ready(h)
                        last = mm(bank[4 + d % 4][:, 0:T], tile4(first + d // 4)[:, d % 4, h, :], src[:, h, :],
                                  start=(h == 0), stop=(h == H - 1))
                    last.then_inc(done, 1)

            def o_ready(h):
                pe.wait_ge(o_normed, h + 1)
                if h == 0:
                    pe.wait_ge(o_sb, 4)
                    pe.wait_ge(s_sb, 4)

            out_projection(C_OUT, oT, o_ready, outp, out_added)

            def feed_forward(e, slot_of, wait_full, gate_s, up_s, act_s, down_s, added_s):
                for f in range(FT):
                    if f % 2 == 0:
                        wait_full(f // 2)
                    w = ring[:, slot_of(f // 2), :].rearrange("p (f u k m) -> p f u k m", f=2, u=2, k=KT)
                    pe.wait_ge(act_s, e * FT + f - 1) if not isinstance(e, int) or e * FT + f >= 2 else None
                    for u, s in ((0, gate_s), (1, up_s)):
                        for k in range(KT):
                            last = mm(bank[2 * (f % 2) + u][:, 0:T], w[:, f % 2, u, k, :], hT[:, k, :],
                                      start=(k == 0), stop=(k == KT - 1))
                        last.then_inc(s, 1)
                for d in range(KT):
                    wait_full(FT // 2 + d)
                    w = ring[:, slot_of(FT // 2 + d), 0:FT * P].rearrange("p (f m) -> p f m", m=P)
                    if not isinstance(e, int) or e * KT + d >= 3:
                        pe.wait_ge(added_s, e * KT + d - 2)
                    for f in range(FT):
                        if d == 0:
                            pe.wait_ge(act_s, e * FT + f + 1)
                        last = mm(bank[4 + d % 3][:, 0:T], w[:, f, :], aT[:, f, :], start=(f == 0), stop=(f == FT - 1))
                    last.then_inc(down_s, 1)

            norm_sums(1)
            pe.wait_ge(normed, 2 * KT)
            feed_forward(0, lambda i: (C_GU + i) % SLOTS, lambda i: arrived(C_GU + i),
                         f_gate, f_up, f_act, f_down, f_added)

            norm_sums(2)

            def rotate(c):
                pe.wait_ge(rope_loaded, 16)
                pe.wait_ge(aproj_sb, c + 1)
                if c >= 2:
                    pe.wait_ge(roped, c - 1)
                mm(bank[4 + c % 2][0:ROT, 0:T], rot_p, aq[:, c, :], start=True, stop=True).then_inc(rot_ps, 1)

            for c in range(16):
                if c % 4 == 0:
                    arrived(C_AIN + c // 4)
                if c >= 4:
                    pe.wait_ge(aproj_sb, c - 3)
                for k in range(KT):
                    if c == 0:
                        pe.wait_ge(normed, 2 * KT + k + 1)
                    last = mm(bank[c % 4][:, 0:T], tile4(C_AIN + c // 4)[:, c % 4, k, :], hT[:, k, :],
                              start=(k == 0), stop=(k == KT - 1))
                last.then_inc(aproj, 1)
                if 1 <= c <= 12:
                    rotate(c - 1)
            pe.wait_ge(aproj_sb, 16)
            for t in range(CH):
                for h in range(KVH):
                    last = nc.tensor.transpose(bank[6 + t][:, P * h:P * (h + 1)], aq[:, 12 + h, P * t:P * (t + 1)], ident)
                last.then_inc(v_ps, 1)
            pe.wait_ge(roped, 12)

            def scores(h):
                if h >= 2:
                    pe.wait_ge(sc_max, h - 1)
                kv = 8 + h // 2
                mm(bank[h % 2][:, 0:P], aq[:, h, 0:P], aq[:, kv, 0:P], start=True, stop=True)
                mm(bank[h % 2][:, P:3 * P], aq[:, h, P:2 * P], aq[:, kv, 0:2 * P],
                   start=True, stop=True).then_inc(sc_ps, 1)

            def turn_probs(h):
                pe.wait_ge(p_sb, h + 1)
                if h >= 2:
                    pe.wait_ge(pT_sb, h - 1)
                for j in range(3):
                    last = nc.tensor.transpose(bank[2 + h % 2][:, P * j:P * (j + 1)], pr_s[:, h % 2, P * j:P * (j + 1)], ident)
                last.then_inc(pT_ps, 1)

            def values(h):
                pe.wait_ge(pT_sb, h + 1)
                pe.wait_ge(v_sb, 2)
                if h >= 2:
                    pe.wait_ge(po_sb, h - 1)
                b, kv = bank[4 + h % 2], h // 2
                mm(b[:, 0:P], v_tok[:, kv, :], pr_T[:, h % 2, 0:P], start=True, stop=True)
                mm(b[:, P:2 * P], v_tok[:, kv, :], pr_T[:, h % 2, P:2 * P], start=True, stop=False)
                mm(b[:, P:2 * P], v_tok[:, KVH + kv, :], pr_T[:, h % 2, 2 * P:3 * P],
                   start=False, stop=True).then_inc(po_ps, 1)

            for i in range(H + 2):
                if i < H:
                    scores(i)
                if 1 <= i <= H:
                    turn_probs(i - 1)
                if i >= 2:
                    values(i - 2)
            for c in range(2 * NS):
                n, b = C_K + c, c // 2
                arrived(n)
                keys = ring[:, n % SLOTS, :].rearrange("p (g h t) -> p g h t", g=PPC, h=KVH)
                for g in range(PPC):
                    for h in range(KVH):
                        at_col = (b % 4) * P + ((c % 2) * PPC + g) * H + 2 * h
                        last = mm(bank[6 + b // 4][:, at_col:at_col + 2], keys[:, g, h, :],
                                  aq[:, 2 * h:2 * h + 2, NPR + b], start=True, stop=True)
                last.then_inc(k_read, 1)
            for i in range(2):
                pe.wait_ge(l_sb, i + 1)
                pe.wait_ge(sc_max, 8)
                for j in range(4):
                    last = nc.tensor.transpose(bank[i][:, P * j:P * (j + 1)], logit[:, 4 * i + j, :], ident)
                last.then_inc(l_turned, 1)
            pe.wait_ge(prod_done, 1)
            for h in range(H):
                last = mm(bank[3][0:NS, h:h + 1], prodn[:, h, :], ones[:, 0:1], start=True, stop=True)
            last.then_inc(lnew_ps, 1)
            pe.wait_ge(st_red, 1)
            nc.tensor.transpose(bank[2][0:NS, 0:P], st_max, ident)
            nc.tensor.transpose(bank[2][0:NS, P:2 * P], st_sum, ident).then_inc(st_turned, 1)
            pe.wait_ge(bias_done, 1)
            pe.wait_ge(po_sb, H)
            for i in range(2):
                last = mm(bank[4 + i], ones[0:NS, :], bias_wide[:, 4 * i:4 * i + 4, :].rearrange("p b n -> p (b n)"),
                          start=True, stop=True)
            last.then_inc(bias_ps, 1)
            pe.wait_ge(pnd_done, 1)
            mm(bank[2][:, 256:320], ones[0:NS, :], pnd[0:NS].rearrange("p h b -> p (h b)"), start=True, stop=True)\
                .then_inc(bias_ps, 1)
            for i in range(2):
                pe.wait_ge(pexp, i + 1)
                mm(bank[i], ones, prob[:, 4 * i:4 * i + 4, :].rearrange("p b n -> p (b n)"),
                   start=True, stop=True).then_inc(den_ps, 1)
            for c in range(2 * NS):
                n, b = C_V + c, c // 2
                arrived(n)
                vals = ring[:, n % SLOTS, :].rearrange("p (g h d) -> p g h d", g=PPC, h=KVH)
                for g in range(PPC):
                    for h in range(KVH):
                        page = (c % 2) * PPC + g
                        last = mm(bank[6][:, b * H + 2 * h:b * H + 2 * h + 2], vals[:, g, h, :],
                                  prob[:, b, page * H + 2 * h:page * H + 2 * h + 2],
                                  start=(c == 0 and g == 0 and h == 0), stop=(c == 2 * NS - 1 and g == PPC - 1 and h == KVH - 1),
                                  skip_group_check=True)
                last.then_inc(v_read, 1)

            def att_ready(h):
                if h == 0:
                    pe.wait_ge(po_sb, H)
                    pe.wait_ge(od_done, 1)

            out_projection(C_AOUT, o_att, att_ready, aout, aout_added)
            norm_sums(3)
            pe.wait_ge(normed, 4 * KT)
            for i, (t0, n) in enumerate(TOK_TILES):
                for k in range(KT):
                    last = mm(bank[0][0:n, NE * i:NE * i + NE], hT[:, k, t0:t0 + n], router[:, k, :],
                              start=(k == 0), stop=(k == KT - 1))
            last.then_inc(r_ps, 1)
            pe.wait_ge(r_gate, 1)
            for i, (t0, n) in enumerate(TOK_TILES):
                last = nc.tensor.transpose(bank[1][0:NE, t0:t0 + n], rgate[0:n, i, :], ident[0:n, 0:n])
            last.then_inc(r_turned, 1)
            pe.wait_ge(r_diag, 1)
            for e in range(NE):
                if e >= 2:
                    pe.wait_ge(gb_sb, e - 1)
                mm(bank[2 + e % 2][:, 0:T], ones[0:NE, :], gate_d[0:NE, e, :], start=True, stop=True).then_inc(gb_ps, 1)
            pe.wait_ge(gb_sb, NE)

            def expert(e):
                def full(i):
                    s = i % SLOTS
                    pe.wait_ge(ring_full[s], e * moe_fills(s) + (full_value(C_MOE + s) + 16 * (i // SLOTS)))
                feed_forward(e, lambda i: i % SLOTS, full, m_gate, m_up, m_act, m_down, m_added)

            expert(0)
            with pe.Fori(1, NE) as e:
                expert(e)
            norm_sums(4)

        @block.scalar
        def _(act):
            steps = [0]

            def link(ins):
                steps[0] += 1
                ins.then_inc(act_link, 1)
                act.wait_ge(act_link, steps[0])

            A = nc.scalar.activation
            act.dma_start(xT[:, :, :], x_in).then_inc(x_loaded, 16)
            act.dma_start(cst[:, :], cst_in).then_inc(prm_loaded, 16)
            act.dma_start(prm[:, :], prm_in).then_inc(prm_loaded, 16)
            act.dma_start(conv_prev[:, :, :, :], conv_in).then_inc(prm_loaded, 16)
            act.dma_start(table[:, :], table_in).then_inc(table_loaded, 16)
            act.wait_ge(prm_loaded, 48)

            def norm_root(i):
                act.wait_ge(sum_sq, i + 1)
                A(rms, bank[7][:, 0:T], ACT.Sqrt, bias=eps, scale=1.0 / D).then_inc(root, 1)

            act.wait_ge(consts_set, 1)
            norm_root(0)
            act.wait_ge(normed, KT)
            for c in range(QKV + 1):
                if c < QKV:
                    act.wait_ge(proj, c + 1)
                    if c >= 2:
                        act.wait_ge(conv_done, c - 1)
                        act.wait_ge(raw_saved, c - 1)
                    A(raw[:, c % 2, CONV_W - 1:], bank[c % 4][:, 0:T], ACT.Copy).then_inc(raw_ready, 1)
                if c >= 1:
                    act.wait_ge(conv_done, c)
                    A(qkv[:, c - 1, 0:NPR], qkv[:, c - 1, 0:NPR], ACT.Silu).then_inc(silu_done, 1)
            act.wait_ge(conv_s_done, 1)
            A(qkv[:, :, NPR:T], qkv[:, :, NPR:T], ACT.Silu).then_inc(silu_done, 1)
            for h in range(H):
                act.wait_ge(proj, QKV + h + 1)
                A(zT[:, h, :], bank[h % 4][:, 0:T], ACT.Silu).then_inc(z_ready, 1)
            for c in range(2 * H):
                act.wait_ge(qk_sum, c + 1)
                if c < H:
                    A(nrm[:, c, :], bank[c % 4][:, 0:T], ACT.Sqrt, bias=eps_q, scale=float(DK)).then_inc(qk_root, 1)
                else:
                    A(nrm[:, c, :], bank[c % 4][:, 0:T], ACT.Sqrt, bias=eps, scale=1.0).then_inc(qk_root, 1)
            act.wait_ge(gates_a, 1)
            A(beta, ba[:, :, 0:H], ACT.Exp, scale=-1.0)
            A(e_alog, p_("a_log"), ACT.Exp)
            link(A(t_exp, t_abs, ACT.Exp, scale=-1.0))
            A(t_exp, t_exp, ACT.Ln, bias=ones[:, 0:1]).then_inc(gates_e, 1)
            act.wait_ge(cum_sb, 1)
            A(neg_ecum, cum, ACT.Exp)
            A(e_end, e_end, ACT.Exp)
            A(ge_s[0:NS], gdec[0:NS, 2, :], ACT.Exp)
            A(to_end, to_end, ACT.Exp).then_inc(cum_exp, 1)

            def untuck(g):
                for src, dst in ((0, ktok), (1, vtok)):
                    n = 2 * g + src
                    act.wait_ge(turned, n + 1)
                    A(dst[:, GRP * g:GRP * (g + 1), :].rearrange("p i n -> p (i n)"), bank[6 + n % 2][:, :],
                      ACT.Copy).then_inc(turned_sb, 1)

            for g in range(NG):
                act.wait_ge(arg_done, g + 1)
                if g >= CH:
                    A(Y[:, GRP * (g - 2):GRP * (g - 1), :].rearrange("p i n -> p (i n)"), bank[0][:, :],
                      ACT.Exp).then_inc(ecum_row, 1)
                A(decT[:, g % 2, :], decT[:, g % 2, :], ACT.Exp).then_inc(dec_exp, 1)
                untuck(g)
            for c in range(CH):
                for g in range(2):
                    act.wait_ge(o_ps, 2 * c + g + 1)
                    if c == 0 and g == 0:
                        act.wait_ge(qk_normed, 4)
                    A(oT[:, GRP * g:GRP * (g + 1), P * c:P * (c + 1)],
                      bank[6 + g][:, :].rearrange("p (h t) -> p h t", t=P), ACT.Copy).then_inc(o_sb, 1)
            for h in range(H):
                act.wait_ge(osum, h + 1)
                A(osq[:, h, :], bank[2 + h % 2][:, 0:T], ACT.Sqrt, bias=eps, scale=1.0 / DK).then_inc(oroot, 1)
            norm_root(1)

            def silus(e, gate_s, act_s, silu_s):
                for f in range(FT):
                    act.wait_ge(gate_s, e * FT + f + 1)
                    if not isinstance(e, int) or e * FT + f >= 2:
                        act.wait_ge(act_s, e * FT + f - 1)
                    A(sil[:, f % 2, :], bank[2 * (f % 2)][:, 0:T], ACT.Silu).then_inc(silu_s, 1)

            silus(0, f_gate, f_act, f_silu)
            norm_root(2)
            for c in range(16):
                act.wait_ge(aproj, c + 1)
                if c == 0:
                    act.dma_start(rope, rope_in).then_inc(rope_loaded, 16)
                A(aq[:, c, :], bank[c % 4][:, 0:T], ACT.Copy).then_inc(aproj_sb, 1)
            for t in range(CH):
                act.wait_ge(v_ps, t + 1)
                A(v_tok[:, KVH * t:KVH * (t + 1), :].rearrange("p i n -> p (i n)"), bank[6 + t][:, :],
                  ACT.Copy).then_inc(v_sb, 1)

            def p_exp(h):
                act.wait_ge(sc_max, h + 1)
                i, m = h % 2, 2 * (h % 2)
                A(pr_s[:, i, 0:P], pr_s[:, i, 0:P], ACT.Exp, bias=pmax[:, m:m + 1], accum_out=psums[:, m:m + 1])
                A(pr_s[:, i, P:3 * P], pr_s[:, i, P:3 * P], ACT.Exp, bias=pmax[:, m + 1:m + 2],
                  accum_out=psums[:, m + 1:m + 2]).then_inc(sc_exp, 1)

            def p_turned(h):
                act.wait_ge(pT_ps, h + 1)
                if h >= 2:
                    act.wait_ge(po_ps, h - 1)
                A(pr_T[:, h % 2, :], bank[2 + h % 2][:, 0:3 * P], ACT.Copy).then_inc(pT_sb, 1)

            def p_out(h):
                act.wait_ge(po_ps, h + 1)
                A(o_att[:, h, 0:NPR], bank[4 + h % 2][:, 0:NPR], ACT.Copy).then_inc(po_sb, 1)

            for i in range(H + 2):
                if i < H:
                    p_exp(i)
                if 1 <= i <= H:
                    p_turned(i - 1)
                if i >= 2:
                    p_out(i - 2)
            for i in range(2):
                act.wait_ge(k_read, NS * (i + 1))
                A(logit[:, 4 * i:4 * i + 4, :].rearrange("p b n -> p (b n)"), bank[6 + i][:, :], ACT.Copy).then_inc(l_sb, 1)
            act.wait_ge(pn_arg, 1)
            A(pn8, pn8, ACT.Exp).then_inc(pn_exp, 1)
            for i in range(2):
                act.wait_ge(parg, i + 1)
                A(prob[:, 4 * i:4 * i + 4, :], prob[:, 4 * i:4 * i + 4, :], ACT.Exp).then_inc(pexp, 1)
            norm_root(3)
            act.wait_ge(r_arg, 1)
            A(rgate, rgate, ACT.Exp).then_inc(r_exp, 1)
            for e in range(NE):
                act.wait_ge(gb_ps, e + 1)
                A(gate_b[:, e, :], bank[2 + e % 2][:, 0:T], ACT.Copy).then_inc(gb_sb, 1)
            silus(0, m_gate, m_act, m_silu)
            with act.Fori(1, NE) as e:
                silus(e, m_gate, m_act, m_silu)
            norm_root(4)

        @block.gpsimd
        def _(pool):
            steps = [0]

            def link(ins):
                steps[0] += 1
                ins.then_inc(pool_link, 1)
                pool.wait_ge(pool_link, steps[0])

            G = nc.gpsimd
            link(G.memset(raw[:, :, :], 0.0))
            link(G.memset(small[:, :], 0.0))
            G.memset(small[:, 766:767], 0.0).then_inc(consts_set, 1)
            for c in range(QKV):
                pool.wait_ge(raw_ready, c + 1)
                G.tensor_copy(conv_last[:, c, :], raw[:, c % 2, NPR:NPR + CONV_W - 1])
                G.tensor_copy(conv_new[:, c, :], raw[:, c % 2, NPR + CONV_W - 1:]).then_inc(raw_saved, 1)
            pool.wait_ge(raw_saved, QKV)
            pool.wait_ge(prm_loaded, 48)
            dst = qkv[:, :, NPR:T]
            tmp = nrm[:, 0, 0:QKV * NS].rearrange("p (c b) -> p c b", b=NS)
            wide_w = lambda j: conv_w[:, :, j:j + 1].to_broadcast([P, QKV, NS])
            link(G.tensor_tensor(dst, conv_prev[:, :, 0, :], wide_w(0), ALU.mult))
            for j in range(1, CONV_W):
                src = conv_prev[:, :, j, :] if j < CONV_W - 1 else conv_new[:, :, :]
                link(G.tensor_tensor(tmp, src, wide_w(j), ALU.mult))
                if j < CONV_W - 1:
                    link(G.tensor_tensor(dst, dst, tmp, ALU.add))
                else:
                    G.tensor_tensor(dst, dst, tmp, ALU.add).then_inc(conv_s_done, 1)
            pool.dma_start(convp_out, conv_last[:, :, :]).then_inc(stored, 16)
            pool.dma_start(convs_out[:, :, 0:CONV_W - 2, :], conv_prev[:, :, 1:, :]).then_inc(stored, 16)
            pool.dma_start(convs_out[:, :, CONV_W - 2, :], conv_new[:, :, :]).then_inc(stored, 16)
            pool.wait_ge(sread_ps, 1)
            pool.wait_ge(su_done, 1)
            for i in range(8):
                s = states[:, 8 * i:8 * i + 8, :]
                G.tensor_tensor(s, s, row_b[:, 1, 8 * i:8 * i + 8].unsqueeze(2).to_broadcast([P, 8, DK]),
                                ALU.mult).then_inc(sdecayed, 1)
            pool.wait_ge(st_sb, 1)
            for i in range(16):
                if i >= 2:
                    pool.wait_ge(sout_ps, i - 1)
                G.tensor_tensor(wide[:, i % 2, :].rearrange("p (a v) -> p a v", a=4),
                                kv_rows[:, 0, :].unsqueeze(1).to_broadcast([64, 4, DK]),
                                ident[0:64, 4 * i:4 * i + 4].unsqueeze(2).to_broadcast([64, 4, DK]),
                                ALU.mult).then_inc(st_sb, 1)
            pool.wait_ge(snew, 16)
            pool.dma_start(deltas_out, states[:, :, :]).then_inc(states_stored, 16)
            pool.wait_ge(s_sb, 4)
            pool.wait_ge(o_sb, 4)
            pool.dma_start(deltap_out, S_fin).then_inc(stored, 16)
            pool.wait_ge(stored, 64)
            pool.wait_ge(states_stored, 16)
            G.memset(small[:, 766:767], 0.0).then_inc(core_done, 1)
            pool.wait_ge(roped, 12)
            pool.wait_ge(aproj_sb, 16)
            pool.dma_start(kv_out, aq[:, 8:16, :]).then_inc(stored, 16)
            pool.wait_ge(normed, 5 * KT)
            pool.dma_start(y_out, hT[:, :, :]).then_inc(stored, 16)

        @block.vector
        def _(dve):
            steps = [0]

            def link(ins):
                steps[0] += 1
                ins.then_inc(dve_link, 1)
                dve.wait_ge(dve_link, steps[0])

            V = nc.vector

            def norm(i):
                V.tensor_tensor(hT[:, :, :], xT[:, :, :], xT[:, :, :], ALU.mult).then_inc(squares, 1)
                dve.wait_ge(root, i + 1)
                link(V.reciprocal(rms, rms))
                for k in range(KT):
                    V.scalar_tensor_tensor(out=hT[:, k, :], in0=xT[:, k, :], scalar=gain[:, i, k:k + 1], in1=rms,
                                           op0=ALU.mult, op1=ALU.mult).then_inc(normed, 1)

            dve.wait_ge(x_loaded, 16)
            dve.wait_ge(prm_loaded, 48)
            dve.wait_ge(consts_set, 1)
            norm(0)
            for c in range(QKV):
                dve.wait_ge(raw_ready, c + 1)
                r, dst = raw[:, c % 2, :], qkv[:, c, 0:NPR]
                link(V.tensor_scalar(dst, r[:, 0:NPR], conv_w[:, c, 0:1], None, ALU.mult))
                for j in range(1, CONV_W):
                    ins = V.scalar_tensor_tensor(out=dst, in0=r[:, j:j + NPR], scalar=conv_w[:, c, j:j + 1], in1=dst,
                                                 op0=ALU.mult, op1=ALU.add)
                    if j < CONV_W - 1:
                        link(ins)
                    else:
                        ins.then_inc(conv_done, 1)
            dve.wait_ge(silu_done, QKV + 1)
            V.tensor_tensor(nrm, qkv[:, 0:2 * H, :], qkv[:, 0:2 * H, :], ALU.mult).then_inc(qk_sq, 1)
            dve.wait_ge(small_ready, 1)
            V.tensor_copy(ba[:, 0:2, :], bank[4][:, 0:32].rearrange("p (i n) -> p i n", i=2))
            link(V.tensor_copy(ba[0:NS, 2, :], bank[4][0:NS, 32:48]))
            xg = ba[:, :, H:2 * H]
            link(V.tensor_tensor(xg, xg, p_("dt_bias").unsqueeze(1).to_broadcast([P, 3, H]), ALU.add))
            V.scalar_tensor_tensor(out=t_abs, in0=xg, scalar=-1.0, in1=xg, op0=ALU.mult, op1=ALU.max).then_inc(gates_a, 1)
            dve.wait_ge(gates_e, 1)
            link(V.tensor_scalar(beta, beta, 1.0, None, ALU.add))
            V.reciprocal(beta, beta)
            link(V.scalar_tensor_tensor(out=gdec, in0=xg, scalar=0.0, in1=t_exp, op0=ALU.max, op1=ALU.add))
            link(V.scalar_tensor_tensor(out=gdec, in0=gdec, scalar=-1.0, in1=e_alog.unsqueeze(1).to_broadcast([P, 3, H]),
                                        op0=ALU.mult, op1=ALU.mult))
            V.tensor_copy(small[:, 767:768], small[:, 766:767]).then_inc(gates_done, 1)
            for i in range(4):
                dve.wait_ge(qk_root, 4 * (i + 1))
                r = nrm[:, 4 * i:4 * i + 4, :]
                link(V.reciprocal(r, r))
                q = qkv[:, 4 * i:4 * i + 4, :]
                V.tensor_tensor(q, q, r, ALU.mult).then_inc(qk_normed, 1)
            dve.wait_ge(cum_ps, 1)
            V.tensor_copy(cum, bank[5][:, 0:16].rearrange("p (c h) -> p c h", c=2))
            link(V.tensor_copy(e_end, bank[5][:, 16:32].rearrange("p (c h) -> p c h", c=2)))
            V.tensor_tensor(to_end, e_end, cum, ALU.subtract).then_inc(cum_sb, 1)
            dve.wait_ge(qk_normed, 4)
            V.tensor_tensor(qk_.rearrange("p (h b) -> p h b", b=NS), qkv[:, 0:H, NPR:T], qkv[:, H:2 * H, NPR:T], ALU.mult)
            dve.wait_ge(cum_exp, 1)
            link(V.tensor_scalar(neg_ecum, neg_ecum, -1.0, None, ALU.mult))
            id8 = ident[0:NS, 0:NS].unsqueeze(1).to_broadcast([NS, H, NS])
            for r, src in ((0, beta[0:NS, 2, :]), (1, ge_s[0:NS, :])):
                ins = V.tensor_tensor(diag8[0:NS, r, :].rearrange("p (h b) -> p h b", b=NS),
                                      src.unsqueeze(2).to_broadcast([NS, H, NS]), id8, ALU.mult)
            ins.then_inc(sdiag, 1)
            for g in range(NG):
                dve.wait_ge(rowdec, g + 1)
                if g == 0:
                    dve.wait_ge(lmask_loaded, 16)
                for j in range(GRP):
                    c, h = (GRP * g + j) // H, (GRP * g + j) % H
                    ins = V.tensor_scalar(decT[:, g % 2, P * j:P * (j + 1)], bank[0][:, P * j:P * (j + 1)],
                                          cum[:, c, h:h + 1], 0.0, ALU.subtract, ALU.min)
                ins.then_inc(arg_done, 1)
                dve.wait_ge(dec_exp, g + 1)
                dve.wait_ge(kk_ready, g + 1)
                dm = decT[:, g % 2, :].rearrange("p (i n) -> p i n", i=GRP)
                link(V.tensor_tensor(dm, dm, upper.unsqueeze(1).to_broadcast([P, GRP, P]), ALU.mult))
                V.tensor_tensor(attT[:, GRP * g:GRP * (g + 1), :].rearrange("p i n -> p (i n)"), bank[2][:, :],
                                decT[:, g % 2, :], ALU.mult)
                for j in range(GRP):
                    i = GRP * g + j
                    ins = V.scalar_tensor_tensor(out=coefT[:, i, :], in0=bank[1][:, P * j:P * (j + 1)],
                                                 scalar=beta[:, i // H, i % H:i % H + 1],
                                                 in1=decT[:, g % 2, P * j:P * (j + 1)], op0=ALU.mult, op1=ALU.mult)
                ins.then_inc(coef_done, 1)
            dve.wait_ge(ecum_row, 2)
            V.tensor_tensor(qkv[:, 0:H, P:2 * P], qkv[:, 0:H, P:2 * P], Y[:, 0:H, :], ALU.mult).then_inc(q_dec_done, 1)
            dve.wait_ge(srow_ps, 1)
            dve.wait_ge(sread_ps, 1)
            V.tensor_copy(row_b.rearrange("p r n -> p (r n)"), bank[5][:, 0:128])
            link(V.tensor_copy(qk_, bank[5][:, 128:192]))
            read = bank[3][:, 0:128].rearrange("p (i r) -> p r i", r=2)
            link(V.tensor_tensor(sk, read[:, 1, :], row_b[:, 1, :], ALU.mult))
            V.tensor_tensor(sq_, read[:, 0, :], row_b[:, 1, :], ALU.mult).then_inc(su_done, 1)
            hb = lambda v: v.rearrange("p (h b) -> p h b", b=NS)
            link(V.tensor_tensor(hb(u_s), qkv[:, 2 * H:3 * H, NPR:T], hb(sk), ALU.subtract))
            link(V.tensor_tensor(u_s, u_s, row_b[:, 0, :], ALU.mult))
            V.tensor_copy(hb(sk), qkv[:, H:2 * H, NPR:T])
            link(V.tensor_tensor(qk_, qk_, u_s, ALU.mult))
            V.tensor_tensor(oT[:, :, NPR:T], hb(sq_), hb(qk_), ALU.add).then_inc(sou, 1)
            for l in range(LEVELS):
                if l == 3:
                    dve.wait_ge(turned_sb, 2 * NG)
                    for i in range(NI):
                        ins = V.tensor_scalar(ktok[:, i, :], ktok[:, i, :], to_end[:, i // H, i % H:i % H + 1], None, ALU.mult)
                    ins.then_inc(kdec_done, 1)
                for g in range(NG):
                    gi = slice(GRP * g, GRP * (g + 1))
                    dve.wait_ge(y_ps, NG * l + g + 1)
                    if l == 0 and g == 0:
                        dve.wait_ge(q_dec_done, 1)
                    V.tensor_tensor(Y[:, gi, :], bank[g][:, :].rearrange("p (i n) -> p i n", i=GRP),
                                    lmask[:, l:l + 1, :].to_broadcast([P, GRP, P]), ALU.mult).then_inc(y_sb, 1)
                for g in range(NG):
                    gi = slice(GRP * g, GRP * (g + 1))
                    fl = lambda v: v[:, gi, :].rearrange("p i n -> p (i n)")
                    if l == 0:
                        idw = ident.unsqueeze(1).to_broadcast([P, GRP, P])
                        dve.wait_ge(y_sb, g + 1)
                        V.tensor_tensor(X[:, gi, :], idw, Y[:, gi, :], ALU.subtract).then_inc(x_sb, 1)
                        dve.wait_ge(z_ps, g + 1)
                        V.tensor_tensor(Z[:, gi, :], idw, bank[6 + g % 2][:, :].rearrange("p (i n) -> p i n", i=GRP),
                                        ALU.subtract).then_inc(z_sb, 1)
                    else:
                        if l < LEVELS - 1:
                            dve.wait_ge(x_ps, NG * (l - 1) + g + 1)
                            V.tensor_tensor(fl(X), fl(X), bank[4 + g % 2][:, :], ALU.subtract).then_inc(x_sb, 1)
                        dve.wait_ge(z_ps, NG * l + g + 1)
                        V.tensor_tensor(fl(Z), fl(Z), bank[6 + g % 2][:, :], ALU.subtract).then_inc(z_sb, 1)
            for c in range(CH):
                if c == 1:
                    for g in range(2):
                        dve.wait_ge(ks_ps, g + 1)
                        for j in range(GRP):
                            h = GRP * g + j
                            ins = V.scalar_tensor_tensor(out=rhs_w[:, h, :], in0=bank[g][:, P * j:P * (j + 1)],
                                                         scalar=neg_ecum[:, 1, h:h + 1], in1=vtok[:, H + h, :],
                                                         op0=ALU.mult, op1=ALU.add)
                        ins.then_inc(w_sb, 1)
                for g in range(2):
                    dve.wait_ge(u_ps, 2 * c + g + 1)
                    if c == 1:
                        dve.wait_ge(o_ps, g + 1)
                    for j in range(GRP):
                        h = GRP * g + j
                        ins = V.tensor_scalar(u_tok[:, h, :], bank[2 + g][:, P * j:P * (j + 1)],
                                              beta[:, c, h:h + 1], None, ALU.mult)
                    ins.then_inc(u_sb, 1)
                for g in range(2):
                    dve.wait_ge(s_ps, 2 * c + g + 1)
                    if c == 0:
                        V.tensor_copy(S_new[:, GRP * g:GRP * (g + 1), :].rearrange("p i n -> p (i n)"),
                                      bank[4 + g][:, :]).then_inc(s_sb, 1)
                    else:
                        dve.wait_ge(s_sb, 2)
                        for j in range(GRP):
                            h = GRP * g + j
                            ins = V.scalar_tensor_tensor(out=S_fin[:, h, :], in0=S_new[:, h, :],
                                                         scalar=e_end[:, 1, h:h + 1], in1=bank[4 + g][:, P * j:P * (j + 1)],
                                                         op0=ALU.mult, op1=ALU.add)
                        ins.then_inc(s_sb, 1)
            dve.wait_ge(st_ps, 1)
            V.tensor_copy(kv_rows.rearrange("p r n -> p (r n)"), bank[0][0:64, 0:2 * P]).then_inc(st_sb, 1)
            for h in range(H):
                if h == 0:
                    dve.wait_ge(o_sb, 4)
                    dve.wait_ge(sou, 1)
                V.tensor_tensor(osq[:, h, :], oT[:, h, :], oT[:, h, :], ALU.mult).then_inc(osq_done, 1)
            for i in range(16):
                dve.wait_ge(sout_ps, i + 1)
                dve.wait_ge(sdecayed, i // 2 + 1)
                s = states[:, 4 * i:4 * i + 4, :].rearrange("p i n -> p (i n)")
                V.tensor_tensor(s, s, bank[2 + i % 2][:, :], ALU.add).then_inc(snew, 1)
            for h in range(H):
                dve.wait_ge(oroot, h + 1)
                link(V.reciprocal(osq[:, h, :], osq[:, h, :]))
                link(V.scalar_tensor_tensor(out=oT[:, h, :], in0=oT[:, h, :], scalar=p_("o_gain"), in1=osq[:, h, :],
                                            op0=ALU.mult, op1=ALU.mult))
                V.tensor_tensor(oT[:, h, :], oT[:, h, :], zT[:, h, :], ALU.mult).then_inc(o_normed, 1)

            def add_out(done, added):
                for d in range(KT):
                    dve.wait_ge(done, d + 1)
                    V.tensor_tensor(xT[:, d, :], xT[:, d, :], bank[4 + d % 4][:, 0:T], ALU.add).then_inc(added, 1)
                dve.wait_ge(added, KT)

            add_out(outp, out_added)
            norm(1)

            def gated(e, up_s, silu_s, act_s):
                for f in range(FT):
                    dve.wait_ge(silu_s, e * FT + f + 1)
                    dve.wait_ge(up_s, e * FT + f + 1)
                    V.tensor_tensor(aT[:, f, :], sil[:, f % 2, :], bank[2 * (f % 2) + 1][:, 0:T], ALU.mult)\
                        .then_inc(act_s, 1)

            gated(0, f_up, f_silu, f_act)
            for d in range(KT):
                dve.wait_ge(f_down, d + 1)
                V.tensor_tensor(xT[:, d, :], xT[:, d, :], bank[4 + d % 3][:, 0:T], ALU.add).then_inc(f_added, 1)
            dve.wait_ge(f_added, KT)
            norm(2)
            dve.wait_ge(rope_loaded, 16)
            for c in range(12):
                a = aq[0:ROT, c, :]
                dve.wait_ge(rot_ps, c + 1)
                if c >= 1:
                    dve.wait_ge(roped, c)
                V.tensor_tensor(rot_t[0:ROT, :], bank[4 + c % 2][0:ROT, 0:T], sinT, ALU.mult)
                link(V.tensor_tensor(a, a, cosT, ALU.mult))
                V.tensor_tensor(a, a, rot_t[0:ROT, :], ALU.add).then_inc(roped, 1)
            dve.wait_ge(roped, 12)

            def p_max(h):
                dve.wait_ge(sc_ps, h + 1)
                if h >= 2:
                    dve.wait_ge(pT_ps, h - 1)
                i, m = h % 2, 2 * (h % 2)
                b = bank[h % 2]
                V.scalar_tensor_tensor(out=pr_s[:, i, 0:P], in0=b[:, 0:P], scalar=SCALE, in1=causal, op0=ALU.mult, op1=ALU.add)
                V.tensor_scalar(pr_s[:, i, P:2 * P], b[:, P:2 * P], SCALE, None, ALU.mult)
                link(V.scalar_tensor_tensor(out=pr_s[:, i, 2 * P:3 * P], in0=b[:, 2 * P:3 * P], scalar=SCALE, in1=causal,
                                            op0=ALU.mult, op1=ALU.add))
                V.tensor_reduce(pmax[:, m:m + 1], pr_s[:, i, 0:P], AX, ALU.max)
                link(V.tensor_reduce(pmax[:, m + 1:m + 2], pr_s[:, i, P:3 * P], AX, ALU.max))
                V.tensor_scalar(pmax[:, m:m + 2], pmax[:, m:m + 2], -1.0, None, ALU.mult).then_inc(sc_max, 1)

            def p_scale(h):
                i, m = h % 2, 2 * (h % 2)
                dve.wait_ge(sc_exp, h + 1)
                link(V.reciprocal(prec[:, m:m + 2], psums[:, m:m + 2]))
                V.tensor_scalar(pr_s[:, i, 0:P], pr_s[:, i, 0:P], prec[:, m:m + 1], None, ALU.mult)
                V.tensor_scalar(pr_s[:, i, P:3 * P], pr_s[:, i, P:3 * P], prec[:, m + 1:m + 2], None, ALU.mult)\
                    .then_inc(p_sb, 1)

            for i in range(H + 1):
                if i < H:
                    p_max(i)
                if i >= 1:
                    p_scale(i - 1)
            kv_new = aq[:, 8:12, NPR:T].unsqueeze(2).to_broadcast([P, KVH, 2, NS])
            V.tensor_tensor(prodn.rearrange("p (k r) b -> p k r b", r=2),
                            aq[:, 0:H, NPR:T].rearrange("p (k r) b -> p k r b", r=2), kv_new, ALU.mult).then_inc(prod_done, 1)
            for i in range(2):
                dve.wait_ge(l_turned, i + 1)
                t = bank[i][:, :].rearrange("p (b n) -> p b n", b=4)
                V.tensor_reduce(st_max[:, 4 * i:4 * i + 4], t, AX, ALU.max)
                ins = V.tensor_reduce(st_sum[:, 4 * i:4 * i + 4], t, AX, ALU.add)
            ins.then_inc(st_red, 1)
            dve.wait_ge(lnew_ps, 1)
            V.tensor_copy(lnew, bank[3][0:NS, 0:H])
            dve.wait_ge(st_turned, 1)
            V.tensor_copy(mx8, bank[2][0:NS, 0:P])
            link(V.tensor_copy(gs8, bank[2][0:NS, P:2 * P]))
            pair = lambda v: v.rearrange("p (k two h) -> p two h k", two=2, h=H)
            link(V.tensor_tensor(gate8, pair(gs8)[:, 0], pair(gs8)[:, 1], ALU.add))
            other, own = gate8.unsqueeze(2).to_broadcast([8, 8, 8, 8]), gate8.unsqueeze(3).to_broadcast([8, 8, 8, 8])
            V.tensor_tensor(cmp8, other, own, ALU.is_gt)
            link(V.tensor_tensor(eq8, other, own, ALU.is_equal))
            link(V.tensor_tensor(eq8, eq8, before[0:8].unsqueeze(1).to_broadcast([8, 8, 8, 8]), ALU.mult))
            link(V.tensor_tensor(cmp8, cmp8, eq8, ALU.add))
            link(V.tensor_reduce(rank8, cmp8, AX, ALU.add))
            link(V.tensor_scalar(rank8, rank8, float(TOPK) - 0.5, -BIG, ALU.is_gt, ALU.mult))
            link(V.tensor_tensor(bm8, pair(mx8)[:, 0], pair(mx8)[:, 1], ALU.max))
            link(V.tensor_tensor(bm8, bm8, rank8, ALU.add))
            link(V.tensor_reduce(m8, bm8, AX, ALU.max))
            link(V.tensor_tensor(m8, m8, lnew, ALU.max))
            link(V.tensor_scalar(m8, m8, -SCALE, None, ALU.mult))
            link(V.tensor_tensor(bm8, rank8, m8.unsqueeze(2).to_broadcast([8, 8, 8]), ALU.add))
            for two in range(2):
                ins = V.tensor_copy(bias8.rearrange("p (k two h) -> p two h k", two=2, h=H)[:, two], bm8)
            link(ins)
            dve.wait_ge(po_ps, H)
            V.tensor_tensor(bias_wide, bias8.unsqueeze(1).to_broadcast([8, 8, P]),
                            ident[0:8, 0:8].unsqueeze(2).to_broadcast([8, 8, P]), ALU.mult).then_inc(bias_done, 1)
            V.scalar_tensor_tensor(out=pn8, in0=lnew, scalar=SCALE, in1=m8, op0=ALU.mult, op1=ALU.add).then_inc(pn_arg, 1)
            dve.wait_ge(pn_exp, 1)
            V.tensor_tensor(pnd[0:8], pn8.unsqueeze(2).to_broadcast([8, 8, 8]),
                            ident[0:8, 0:8].unsqueeze(1).to_broadcast([8, 8, 8]), ALU.mult).then_inc(pnd_done, 1)
            dve.wait_ge(bias_ps, 2)
            dve.wait_ge(l_sb, 2)
            for i in range(2):
                V.scalar_tensor_tensor(out=prob[:, 4 * i:4 * i + 4, :].rearrange("p b n -> p (b n)"),
                                       in0=logit[:, 4 * i:4 * i + 4, :].rearrange("p b n -> p (b n)"), scalar=SCALE,
                                       in1=bank[4 + i][:, :], op0=ALU.mult, op1=ALU.add).then_inc(parg, 1)
            link(V.tensor_copy(pnb.rearrange("p h b -> p (h b)"), bank[2][:, 256:320]))
            for i in range(2):
                dve.wait_ge(den_ps, i + 1)
                ins = V.tensor_reduce(den[:, 4 * i:4 * i + 4, :],
                                      bank[i][:, :].rearrange("p (b g h) -> p b h g", b=4, h=H), AX, ALU.add)
            link(ins)
            link(V.tensor_tensor(den, den, pnb.rearrange("p h b -> p b h"), ALU.add))
            V.reciprocal(den, den)
            v_new = aq[:, 12:16, NPR:T].unsqueeze(2).to_broadcast([P, KVH, 2, NS])
            link(V.tensor_tensor(pnb.rearrange("p (k r) b -> p k r b", r=2), pnb.rearrange("p (k r) b -> p k r b", r=2),
                                 v_new, ALU.mult))
            dve.wait_ge(v_read, 2 * NS)
            link(V.tensor_tensor(pnb, pnb, bank[6][:, 0:64].rearrange("p (b h) -> p h b", h=H), ALU.add))
            V.tensor_tensor(o_att[:, :, NPR:T], pnb, den.rearrange("p b h -> p h b"), ALU.mult).then_inc(od_done, 1)
            add_out(aout, aout_added)
            norm(3)
            dve.wait_ge(r_ps, 1)
            V.tensor_copy(rl[:, 0:2, :], bank[0][:, 0:16].rearrange("p (i e) -> p i e", i=2))
            link(V.tensor_copy(rl[0:NS, 2, :], bank[0][0:NS, 16:24]))
            r4 = lambda v: v.rearrange("p (t i) j -> p t i j", t=3)
            other, own = rl.unsqueeze(2).to_broadcast([P, 3, NE, NE]), rl.unsqueeze(3).to_broadcast([P, 3, NE, NE])
            V.tensor_tensor(r4(rcmp), other, own, ALU.is_gt)
            link(V.tensor_tensor(r4(req), other, own, ALU.is_equal))
            link(V.tensor_tensor(r4(req), r4(req), before.unsqueeze(1).to_broadcast([P, 3, NE, NE]), ALU.mult))
            link(V.tensor_tensor(rcmp, rcmp, req, ALU.add))
            link(V.tensor_reduce(rrank.rearrange("p t e -> p (t e)"), rcmp, AX, ALU.add))
            V.tensor_scalar(rrank, rrank, 1.5, None, ALU.is_lt)
            link(V.tensor_reduce(rmax, rl, AX, ALU.max))
            V.tensor_tensor(rgate, rl, rmax.unsqueeze(2).to_broadcast([P, 3, NE]), ALU.subtract).then_inc(r_arg, 1)
            dve.wait_ge(r_exp, 1)
            link(V.tensor_tensor(rgate, rgate, rrank, ALU.mult))
            link(V.tensor_reduce(rmax, rgate, AX, ALU.add))
            link(V.reciprocal(rmax, rmax))
            V.tensor_tensor(rgate, rgate, rmax.unsqueeze(2).to_broadcast([P, 3, NE]), ALU.mult).then_inc(r_gate, 1)
            dve.wait_ge(r_turned, 1)
            link(V.tensor_copy(gT, bank[1][0:NE, 0:T]))
            V.tensor_tensor(gate_d[0:NE], gT.unsqueeze(1).to_broadcast([NE, NE, T]),
                            ident[0:NE, 0:NE].unsqueeze(2).to_broadcast([NE, NE, T]), ALU.mult).then_inc(r_diag, 1)
            dve.wait_ge(gb_sb, NE)
            dve.wait_ge(stored, 16 * 5)

            def expert(e):
                gated(e, m_up, m_silu, m_act)
                for d in range(KT):
                    dve.wait_ge(m_down, e * KT + d + 1)
                    g = gate_b[:, e, :] if isinstance(e, int) else gate_b[:, bass.ds(e, 1), :].rearrange("p a t -> p (a t)")
                    V.tensor_tensor(weighted[:, d % 2, :], bank[4 + d % 3][:, 0:T], g, ALU.mult).then_inc(m_added, 1)
                    dve.wait_ge(m_added, e * KT + d + 1)
                    last = V.tensor_tensor(xT[:, d, :], xT[:, d, :], weighted[:, d % 2, :], ALU.add)
                last.then_inc(x_sum, 1)
                dve.wait_ge(x_sum, e + 1)

            expert(0)
            with dve.Fori(1, NE) as e:
                expert(e)
            norm(4)


def _constants():
    r = np.arange(P)
    c = {
        "ident": np.eye(P), "ones": np.ones((P, P)), "upper": r[:, None] <= r[None, :],
        "causal": np.where(r[None, :] <= r[:, None], 0.0, -BIG),
        "before": np.tile((np.arange(8)[None, :] < np.arange(8)[:, None]).reshape(1, 64), (P, 1)),
        "eps": np.tile(np.array([[EPS, EPS * DK]]), (P, 1)),
    }
    cst = np.concatenate([np.asarray(c[n], np.float32) for n in CST], axis=1)
    masks = []
    for level in range(LEVELS):
        s = 1 << level
        same = (r[:, None] // (2 * s)) == (r[None, :] // (2 * s))
        masks.append(same & ((r[:, None] // s) % 2 == 1) & ((r[None, :] // s) % 2 == 0))
    lmask = np.stack(masks, axis=1).reshape(P, LEVELS * P).astype(np.float32)
    half = ROT // 2
    rot = np.zeros((P, ROT), np.float32)
    rot[np.arange(half) + half, np.arange(half)] = -1.0
    rot[np.arange(half), np.arange(half) + half] = 1.0
    inv = np.power(np.float32(500000.0), -np.arange(half, dtype=np.float32) * np.float32(2.0 / ROT))
    pos = np.concatenate([np.arange(NPR), np.full(NS, POS0)]).astype(np.float32)
    ang = np.tile((pos[None, :] * inv[:, None]).astype(np.float32), (2, 1))
    rope = np.zeros((P, ROPE_N), np.float32)
    rope[:, :ROT] = rot
    rope[:ROT, ROT:ROT + T] = np.cos(ang)
    rope[:ROT, ROT + T:] = np.sin(ang)
    return cst, lmask, rope


def kernel(**inputs):
    import numpy as _np
    import concourse.bacc as _bacc
    from concourse import mybir as _mybir
    from concourse.bass_utils import run_bass_kernel_spmd as _run

    a = {k: _np.asarray(v) for k, v in inputs.items()}
    cont = _np.ascontiguousarray

    def columns(w, per_chunk):
        k, n = w.shape
        t = w.reshape(k // P, P, n // (P * per_chunk), per_chunk, P).transpose(2, 1, 3, 0, 4)
        return cont(t.reshape(t.shape[0], P, -1))

    def gate_up(g, u):
        e = g.shape[0]
        parts = [w.reshape(e, KT, P, FT // 2, 2, P).transpose(0, 3, 2, 4, 1, 5) for w in (g, u)]
        return cont(_np.stack(parts, axis=4)).reshape(e * (FT // 2), P, SLOT)

    def down(w):
        e = w.shape[0]
        return cont(w.reshape(e, FT, P, KT, P).transpose(0, 3, 2, 1, 4)).reshape(e * KT, P, FT * P)

    x = _np.concatenate([a["x_prompt"][0], a["x_sample"][:, 0]], axis=0)
    cst, lmask, rope = _constants()
    gains = _np.stack([a["norm_mix"][0], a["norm_ffn"][0], a["norm_mix"][1], a["norm_ffn"][1], a["norm_final"]])
    w_in = a["gdn_w_in"][0]
    n_wide = (QKV + H) * P
    prm = {
        "gain": gains.reshape(5, KT, P).transpose(2, 0, 1), "o_gain": a["gdn_o_norm"][0][:, None],
        "conv_w": a["gdn_conv_w"][0].reshape(CONV_W, QKV, P).transpose(2, 1, 0),
        "a_log": _np.tile(a["gdn_a_log"][0][None], (P, 1)), "dt_bias": _np.tile(a["gdn_dt_bias"][0][None], (P, 1)),
        "router": a["moe_router"][0].reshape(KT, P, NE).transpose(1, 0, 2),
        "w_small": w_in[:, n_wide:].reshape(KT, P, 2 * H).transpose(1, 0, 2),
    }
    given = {
        "x": x.reshape(T, KT, P).transpose(2, 1, 0),
        "cst": cst, "lmask": lmask, "rope": rope,
        "prm": _np.concatenate([prm[n].reshape(P, -1) for n in PRM], axis=1),
        "conv": a["state_conv"][0].reshape(NS, CONV_W - 1, QKV, P).transpose(3, 2, 1, 0),
        "table": a["page_table"].reshape(1, -1),
        "gdn_in": columns(w_in[:, :n_wide], 4),
        "state": a["state_delta"][0].transpose(2, 1, 0, 3).reshape(DK, 2, SLOT).transpose(1, 0, 2),
        "gdn_out": columns(a["gdn_w_out"][0], 4),
        "ffn_gu": gate_up(a["ffn_w_gate"], a["ffn_w_up"]), "ffn_down": down(a["ffn_w_down"]),
        "att_in": columns(a["att_w_in"][0], 4),
        "k_pages": a["cache_k"][0].transpose(0, 3, 2, 1).reshape(-1, P, KVH * PAGE),
        "v_pages": a["cache_v"][0].reshape(-1, PAGE, KVH * DK),
        "att_out": columns(a["att_w_out"][0], 4),
        "moe_gu": gate_up(a["moe_w_gate"][0], a["moe_w_up"][0]), "moe_down": down(a["moe_w_down"][0]),
    }
    outs = {"y": (P, KT, T), "convp": (P, QKV, CONV_W - 1), "convs": (P, QKV, CONV_W - 1, NS),
            "deltap": (P, H, DK), "deltas": (P, H * NS, DK), "kv": (P, 2 * KVH, T)}

    nc = _bacc.Bacc("TRN2", target_bir_lowering=False, num_devices=1)
    arrays, args = {}, []
    for name, v in given.items():
        arrays[f"in_{name}"] = cont(v)
        args.append(nc.dram_tensor(f"in_{name}", v.shape, _mybir.dt.from_np(v.dtype), kind="ExternalInput").ap())
    for name, shape in outs.items():
        args.append(nc.dram_tensor(f"out_{name}", shape, F32, kind="ExternalOutput").ap())
    program(nc, *args)
    r = _run(nc, [arrays], core_ids=[0]).results[0]
    y = r["out_y"].transpose(2, 1, 0).reshape(T, D)
    kv = r["out_kv"].transpose(2, 1, 0)
    convs = r["out_convs"].transpose(3, 2, 1, 0).reshape(1, NS, CONV_W - 1, QKV * P)
    deltas = r["out_deltas"].reshape(DK, H, NS, DK).transpose(2, 1, 0, 3)[None]
    return (y[None, :NPR], y[NPR:, None],
            r["out_convp"].transpose(2, 1, 0).reshape(1, 1, CONV_W - 1, QKV * P),
            r["out_deltap"].transpose(1, 0, 2)[None, None],
            kv[None, None, :NPR, :KVH], kv[None, None, :NPR, KVH:],
            convs, deltas, kv[None, NPR:, None, :KVH], kv[None, NPR:, None, KVH:])
```

```python
from contextlib import ExitStack

import numpy as np

import concourse.bass as bass
from concourse import mybir

F32 = mybir.dt.float32
I32 = mybir.dt.int32
ALU = mybir.AluOpType
ACT = mybir.ActivationFunctionType
AX = mybir.AxisListType.X

P = 128
D = 1024
KT = D // P
NPR = 256
NS = 8
T = NPR + NS
TOK_TILES = ((0, P), (P, P), (NPR, NS))
H = 8
KVH = 4
DK = 128
CONV_W = 4
QKV = 3 * H
CH = 2
NI = CH * H
GRP = 4
NG = NI // GRP
LEVELS = 7
FT = 3584 // P
NE = 8
N_PAGES = 16
PAGE = 128
PPC = 8
BLOCKS = N_PAGES * PAGE // 256
TOPK = 3
ROT = 32
POS0 = N_PAGES * PAGE
SCALE = DK ** -0.5
EPS = 1e-6
BIG = 1e30

SLOTS = 8
SLOT = 4096
C_IN = 0
C_STATE = C_IN + 8
C_OUT = C_STATE + 2
C_GU = C_OUT + 2
C_DOWN = C_GU + FT // 2
C_AIN = C_DOWN + KT
C_K = C_AIN + 4
C_V = C_K + 2 * NS
C_AOUT = C_V + 2 * NS
C_MOE = C_AOUT + 2
MOE_CHUNKS = FT // 2 + KT
CAP = 128
STORES = 6
assert C_MOE % SLOTS == 0


def fills_per_chunk(n):
    return 16 * (PPC if C_K <= n < C_AOUT else 1)


def full_value(n):
    return sum(fills_per_chunk(m) for m in range(n % SLOTS, n + 1, SLOTS))


def moe_fills(slot):
    return 16 * len(range(slot, MOE_CHUNKS, SLOTS))


CST = {}
_at = 0
for _name, _n in (("ident", P), ("ones", P), ("upper", P), ("causal", P), ("before", 64), ("eps", 2), ("slot_no", CAP)):
    CST[_name] = (_at, _n)
    _at += _n
CST_N = _at
PRM = {}
_at = 0
for _name, _n in (("gain", 5 * KT), ("o_gain", 1), ("conv_w", QKV * CONV_W), ("a_log", H), ("dt_bias", H),
                  ("router", KT * NE), ("w_small", KT * 2 * H)):
    PRM[_name] = (_at, _n)
    _at += _n
PRM_N = _at
ROPE_N = ROT + 2 * T


def program(nc, x_in, cst_in, lmask_in, rope_in, prm_in, conv_in, table_in, gdn_in_w, state_in, gdn_out_w,
            ffn_gu, ffn_down, att_in_w, k_pages, v_pages, att_out_w, moe_gu, moe_down,
            y_out, convp_out, convs_out, deltap_out, deltas_out, kv_out):
    with ExitStack() as ctx:
        def sb(name, shape, dt=F32):
            return ctx.enter_context(nc.sbuf_tensor(name, shape, dt))

        def sem(name):
            return ctx.enter_context(nc.semaphore(name))

        ring = sb("ring", [P, SLOTS, SLOT])
        xT = sb("xT", [P, KT, T])
        hT = sb("hT", [P, KT, T])
        scr = sb("scr", [P, 48 * T])
        cst = sb("cst", [P, CST_N])
        prm = sb("prm", [P, PRM_N])
        conv_prev = sb("conv_prev", [P, QKV, CONV_W - 1, NS])
        raw = sb("raw", [P, 2, CONV_W - 1 + T])
        conv_last = sb("conv_last", [P, QKV, CONV_W - 1])
        conv_new = sb("conv_new", [P, QKV, NS])
        small = sb("small", [P, 768])
        table = sb("table", [1, NS * N_PAGES], I32)
        dense_flag = sb("dense_flag", [1, 1], I32)
        bank = [ctx.enter_context(nc.psum_tensor(f"bank{i}", [P, 512], F32))[:, :] for i in range(8)]

        def c_(name):
            a, n = CST[name]
            return cst[:, a:a + n]

        def p_(name):
            a, n = PRM[name]
            return prm[:, a:a + n]

        ident, ones, upper, causal = c_("ident"), c_("ones"), c_("upper"), c_("causal")
        before = c_("before").rearrange("p (i j) -> p i j", i=8)
        eps, eps_q = cst[:, CST["eps"][0]:CST["eps"][0] + 1], cst[:, CST["eps"][0] + 1:CST["eps"][0] + 2]
        gain = p_("gain").rearrange("p (l k) -> p l k", k=KT)
        conv_w = p_("conv_w").rearrange("p (c j) -> p c j", j=CONV_W)
        router = p_("router").rearrange("p (k e) -> p k e", e=NE)
        w_small = p_("w_small").rearrange("p (k e) -> p k e", e=2 * H)
        rms = raw[:, 0, CONV_W - 1:]

        def carve(base, at, *dims):
            n = int(np.prod(dims))
            v = base[:, at:at + n]
            if len(dims) == 2:
                v = v.rearrange("p (a b) -> p a b", b=dims[1])
            if len(dims) == 3:
                v = v.rearrange("p (a b c) -> p a b c", b=dims[1], c=dims[2])
            return v

        qkv = carve(scr, 0, QKV, T)
        zT = carve(scr, QKV * T, H, T)
        nrm = carve(scr, (QKV + H) * T, 2 * H, T)
        oT = carve(scr, (QKV + H) * T, H, T)
        osq = carve(scr, (QKV + 2 * H) * T, H, T)
        core = ring[:, 4:8, :].rearrange("p s n -> p (s n)")
        ktok = carve(core, 0, NI, P)
        vtok = carve(core, 2048, NI, P)
        coefT = carve(core, 4096, NI, P)
        attT = carve(core, 6144, NI, P)
        X = carve(core, 8192, NI, P)
        Z = carve(core, 10240, NI, P)
        Y = carve(core, 12288, NI, P)
        lmask = carve(core, 14336, LEVELS, P)
        decT = carve(core, 15232, 2, GRP * P)
        rhs_w = X[:, 0:8, :]
        u_tok = X[:, 8:16, :]
        S_new = Y[:, 0:8, :]
        S_fin = Y[:, 8:16, :]
        wide = decT[0:64]
        kv_rows = carve(core, 14336, 2, P)[0:64]
        states = ring[:, 0:2, :].rearrange("p s n -> p (s n)").rearrange("p (i v) -> p i v", v=DK)
        sm_at = [0]

        def sm(*dims):
            v = carve(small, sm_at[0], *dims)
            sm_at[0] += int(np.prod(dims))
            return v

        ba = sm(3, 2 * H)
        beta = sm(3, H)
        gdec = sm(3, H)
        t_abs = sm(3, H)
        t_exp = sm(3, H)
        e_alog = sm(H)
        cum = sm(CH, H)
        neg_ecum = sm(CH, H)
        to_end = sm(CH, H)
        e_end = sm(CH, H)
        ge_s = sm(H)
        diag8 = sm(2, 64)
        row_b = sm(2, 64)
        sk = sm(64)
        sq_ = sm(64)
        qk_ = sm(64)
        u_s = sm(64)
        sil = carve(scr, 47 * T - T, 2, T)
        aT = carve(scr, 0, FT, T)
        gate_b = carve(scr, FT * T, NE, T)
        aq = carve(scr, 0, 16, T)
        rope = scr[:, 16 * T:16 * T + ROPE_N]
        rot_p = rope[:, 0:ROT]
        cosT, sinT = rope[0:ROT, ROT:ROT + T], rope[0:ROT, ROT + T:ROT + 2 * T]
        at = 16 * T + ROPE_N
        rot_t = carve(scr, at, T); at += T
        v_tok = carve(scr, at, CH * KVH, P); at += CH * KVH * P
        prob = scr[0:64, at:at + N_PAGES * PAGE]; at += N_PAGES * PAGE
        o_att = carve(scr, at, H, T); at += H * T
        pr_s = carve(scr, at, 2, 384); at += 768
        pr_T = carve(scr, at, 2, 384); at += 768
        a_small = scr[:, at:48 * T]
        pmax, psums, prec = a_small[:, 16:20], a_small[:, 20:24], a_small[:, 24:28]
        hflat = hT[:, :, :].rearrange("p k t -> p (k t)")
        q_wide = hflat[:, 0:NS * KVH * 64].rearrange("p (i r) -> p i r", r=64)
        q_own = hflat.rearrange("p (b k r) -> p b k r", b=NS, k=KVH)[:, :, :, 0:2]
        prodn = hflat[:, NS * KVH * 64:NS * KVH * 64 + 64]
        prob_T = hflat[:, 0:N_PAGES * 64].rearrange("p (g r) -> p g r", r=64)
        st = [32]

        def stat(rows, *dims):
            v = carve(a_small, st[0], *dims)[0:rows]
            st[0] += int(np.prod(dims))
            return v

        st_max, st_sum, pen, biases, sums = (stat(64, BLOCKS) for _ in range(5))
        cmp_b, eq_b = stat(64, BLOCKS, BLOCKS), stat(64, BLOCKS, BLOCKS)
        m_neg, l_new, p_new, r_den = (stat(64, 1) for _ in range(4))
        rd_diag, p_diag = stat(64, 64), stat(64, 64)
        o_new = stat(P, NS, H)
        kv_of_head = stat(8, KVH)
        assert st[0] <= 48 * T - at
        o8 = carve(scr, at - 1536, NS, DK)[0:8]
        o_wide = carve(scr, at - 512, KVH, DK)[0:8]
        r_at = FT * T + NE * T
        gate_d = carve(scr, r_at, NE, T)
        weighted = carve(scr, r_at + NE * T, 2, T)
        rl = sm(3, NE)
        sm_at[0] = 0
        rpos = sm(3, NE + 1)
        rgate = sm(3, NE + 1)
        rrank = sm(3, NE)
        counts = sm(NE)
        over = sm(1)
        s_act = carve(scr, 0, FT, CAP)
        at = FT * CAP
        htok = carve(scr, at, 3, D); at += 3 * D
        xe = carve(scr, at, KT, CAP); at += KT * CAP
        pick = carve(scr, at, 3, CAP); at += 3 * CAP
        pick_g = carve(scr, at, 3, CAP); at += 3 * CAP
        spread = scr[0:CAP, at:at + T]; at += T
        yeT = carve(scr, at, KT, CAP); at += KT * CAP
        ye = scr[0:CAP, at:at + D]; at += D
        s_sil = carve(scr, at, 2, CAP); at += 2 * CAP
        assert at <= 48 * T
        rcmp = carve(scr, 0, 3 * NE, NE)
        req = carve(scr, 192, 3 * NE, NE)
        rmax = carve(scr, 408, 3)
        gT = scr[0:8, 448:448 + T]

        ring_full = [sem(f"ring_full{s}") for s in range(SLOTS)]
        x_loaded, prm_loaded, lmask_loaded, rope_loaded = sem("x_loaded"), sem("prm_loaded"), sem("lmask_loaded"), sem("rope_loaded")
        table_loaded = sem("table_loaded")
        stored = sem("stored")
        states_stored = sem("states_stored")
        consts_set = sem("consts_set")
        squares, sum_sq, root, normed = sem("squares"), sem("sum_sq"), sem("root"), sem("normed")
        dve_link, act_link, pool_link = sem("dve_link"), sem("act_link"), sem("pool_link")
        proj, raw_ready, conv_done, z_ready = sem("proj"), sem("raw_ready"), sem("conv_done"), sem("z_ready")
        raw_saved, conv_s_done, silu_done, small_ready = sem("raw_saved"), sem("conv_s_done"), sem("silu_done"), sem("small_ready")
        qk_sq, qk_sum, qk_root, qk_normed = sem("qk_sq"), sem("qk_sum"), sem("qk_root"), sem("qk_normed")
        gates_a, gates_e, gates_done = sem("gates_a"), sem("gates_e"), sem("gates_done")
        cum_ps, cum_sb, cum_exp = sem("cum_ps"), sem("cum_sb"), sem("cum_exp")
        rowdec, arg_done, dec_exp, ecum_row, kk_ready, coef_done = (
            sem("rowdec"), sem("arg_done"), sem("dec_exp"), sem("ecum_row"), sem("kk_ready"), sem("coef_done"))
        turned, turned_sb = sem("turned"), sem("turned_sb")
        y_ps, y_sb, x_ps, z_ps, x_sb, z_sb = sem("y_ps"), sem("y_sb"), sem("x_ps"), sem("z_ps"), sem("x_sb"), sem("z_sb")
        kdec_done, q_dec_done = sem("kdec_done"), sem("q_dec_done")
        ks_ps, w_sb, u_ps, u_sb, s_ps, s_sb, o_ps, o_sb = (
            sem("ks_ps"), sem("w_sb"), sem("u_ps"), sem("u_sb"), sem("s_ps"), sem("s_sb"), sem("o_ps"), sem("o_sb"))
        core_done = sem("core_done")
        sdiag, srow_ps, sread_ps, sdecayed, su_done, st_ps, st_sb, sou, sout_ps, snew = (
            sem("sdiag"), sem("srow_ps"), sem("sread_ps"), sem("sdecayed"), sem("su_done"), sem("st_ps"), sem("st_sb"),
            sem("sou"), sem("sout_ps"), sem("snew"))
        osq_done, osum, oroot, o_normed = sem("osq_done"), sem("osum"), sem("oroot"), sem("o_normed")
        outp, out_added = sem("outp"), sem("out_added")
        f_gate, f_up, f_silu, f_act, f_down, f_added = (sem(f"f_{n}") for n in ("gate", "up", "silu", "act", "down", "added"))
        m_gate, m_up, m_silu, m_act, m_down, m_added = (sem(f"m_{n}") for n in ("gate", "up", "silu", "act", "down", "added"))
        x_sum = sem("x_sum")
        pos_ps, over_set, h_turned, h_tok = sem("pos_ps"), sem("over_set"), sem("h_turned"), sem("h_tok")
        picked, gathered, xe_sb, yT_sb, y_turned, ye_sb, spread_ps, spread_sb, comb, comb_added = (
            sem("picked"), sem("gathered"), sem("xe_sb"), sem("yT_sb"), sem("y_turned"), sem("ye_sb"), sem("spread_ps"),
            sem("spread_sb"), sem("comb"), sem("comb_added"))
        aproj, aproj_sb, rot_ps, roped, v_ps, v_sb = sem("aproj"), sem("aproj_sb"), sem("rot_ps"), sem("roped"), sem("v_ps"), sem("v_sb")
        sc_ps, sc_max, sc_exp, p_sb, pT_ps, pT_sb, po_ps, po_sb = (
            sem("sc_ps"), sem("sc_max"), sem("sc_exp"), sem("p_sb"), sem("pT_ps"), sem("pT_sb"), sem("po_ps"), sem("po_sb"))
        q_wide_set, k_read, prod_done, lnew_ps, bias_done, pexp, diag_done, probT_ps, probT_sb, v_read, o8_done, o8_turned, od_done = (
            sem(n) for n in ("q_wide_set", "k_read", "prod_done", "lnew_ps", "bias_done", "pexp", "diag_done", "probT_ps",
                             "probT_sb", "v_read", "o8_done", "o8_turned", "od_done"))
        aout, aout_added = sem("aout"), sem("aout_added")
        r_ps, r_arg, r_exp, r_gate, r_turned, r_diag, gb_ps, gb_sb = (
            sem("r_ps"), sem("r_arg"), sem("r_exp"), sem("r_gate"), sem("r_turned"), sem("r_diag"), sem("gb_ps"), sem("gb_sb"))

        mm = nc.tensor.matmul

        def tile4(n):
            return ring[:, n % SLOTS, :].rearrange("p (c k m) -> p c k m", c=4, k=KT)

        def slot_free(eng, n):
            m = n - SLOTS
            if m < 0:
                return
            if m < C_STATE:
                eng.wait_ge(proj, 4 * (m + 1))
            elif m < C_OUT:
                eng.wait_ge(states_stored, 16)
            elif m < C_GU:
                eng.wait_ge(outp, 4 * (m - C_OUT + 1))
            elif m < C_DOWN:
                eng.wait_ge(f_up, 2 * (m - C_GU + 1))
            elif m < C_AIN:
                eng.wait_ge(f_down, m - C_DOWN + 1)
            elif m < C_K:
                eng.wait_ge(aproj, 4 * (m - C_AIN + 1))
            elif m < C_V:
                eng.wait_ge(k_read, m - C_K + 1)
            elif m < C_AOUT:
                eng.wait_ge(v_read, m - C_V + 1)
            else:
                eng.wait_ge(aout, 4 * (m - C_AOUT + 1))

        def load_pages(eng, n, pages):
            first, cache = (C_K, k_pages) if n < C_V else (C_V, v_pages)
            slot_free(eng, n)
            for page in pages:
                entry = (n - first) * PPC + page
                at_page = eng.value_load(table[0:1, entry:entry + 1], min_val=0, max_val=cache.shape[0] - 1)
                dst = ring[:, n % SLOTS, page * (SLOT // PPC):(page + 1) * (SLOT // PPC)]
                eng.dma_start(dst, cache[bass.ds(at_page, 1)].rearrange("a p n -> p (a n)"))\
                   .then_inc(ring_full[n % SLOTS], 16)

        C_BOTH = C_K + SLOTS

        block = ctx.enter_context(nc.Block())

        @block.sync
        def _(sp):
            def load(n, src, size=SLOT):
                slot_free(sp, n)
                if 4 <= n - C_STATE < 8:
                    sp.wait_ge(core_done, 1)
                sp.dma_start(ring[:, n % SLOTS, 0:size], src).then_inc(ring_full[n % SLOTS], 16)

            for n in range(8):
                load(C_IN + n, gdn_in_w[n])
            for n in range(2):
                load(C_STATE + n, state_in[n])
            for n in range(2):
                load(C_OUT + n, gdn_out_w[n])
            sp.wait_ge(proj, 4 * 8)
            sp.dma_start(core[:, 14336:15232], lmask_in).then_inc(lmask_loaded, 16)
            for n in range(FT // 2):
                load(C_GU + n, ffn_gu[n])
            for n in range(KT):
                load(C_DOWN + n, ffn_down[n], FT * P)
            for n in range(4):
                load(C_AIN + n, att_in_w[n])
            sp.wait_ge(table_loaded, 16)
            for n in range(C_K, C_AOUT):
                load_pages(sp, n, range(0, PPC) if n < C_BOTH else range(0, PPC // 2))
            for n in range(2):
                load(C_AOUT + n, att_out_w[n])

            def load_expert(e, first):
                for i in range(MOE_CHUNKS):
                    m = i - SLOTS
                    if m >= 0:
                        if m < FT // 2:
                            sp.wait_ge(m_up, e * FT + 2 * (m + 1))
                        else:
                            sp.wait_ge(m_down, e * KT + m - FT // 2 + 1)
                    elif first:
                        slot_free(sp, C_MOE + i)
                    else:
                        prev = max(j for j in range(MOE_CHUNKS) if j % SLOTS == i % SLOTS)
                        if prev < FT // 2:
                            sp.wait_ge(m_up, e * FT + (2 * (prev + 1) - FT))
                        else:
                            sp.wait_ge(m_down, e * KT + (prev - FT // 2 + 1 - KT))
                    if i < FT // 2:
                        src, size = moe_gu, SLOT
                        row = e * (FT // 2) + i
                    else:
                        src, size = moe_down, FT * P
                        row = e * KT + i - FT // 2
                    if first:
                        sp.dma_start(ring[:, i % SLOTS, 0:size], src[row]).then_inc(ring_full[i % SLOTS], 16)
                    else:
                        sp.dma_start(ring[:, i % SLOTS, 0:size], src[bass.ds(row, 1)].rearrange("a p n -> p (a n)"))\
                          .then_inc(ring_full[i % SLOTS], 16)

            load_expert(0, True)
            with sp.Fori(1, NE) as e:
                load_expert(e, False)
            sp.wait_ge(stored, 16 * STORES)

        @block.tensor
        def _(pe):
            def arrived(n):
                pe.wait_ge(ring_full[n % SLOTS], full_value(n))

            def norm_sums(i):
                pe.wait_ge(squares, i + 1)
                for k in range(KT):
                    last = mm(bank[7][:, 0:T], ones, hT[:, k, :], start=(k == 0), stop=(k == KT - 1))
                last.then_inc(sum_sq, 1)

            pe.wait_ge(prm_loaded, 48)
            norm_sums(0)
            for c in range(QKV + H):
                if c % 4 == 0:
                    arrived(C_IN + c // 4)
                if c >= 4:
                    if c - 4 < QKV:
                        pe.wait_ge(raw_ready, c - 3)
                    else:
                        pe.wait_ge(z_ready, c - 4 - QKV + 1)
                for k in range(KT):
                    if c == 0:
                        pe.wait_ge(normed, k + 1)
                    last = mm(bank[c % 4][:, 0:T], tile4(C_IN + c // 4)[:, c % 4, k, :], hT[:, k, :],
                              start=(k == 0), stop=(k == KT - 1))
                last.then_inc(proj, 1)
            for i, (t0, n) in enumerate(TOK_TILES):
                for k in range(KT):
                    last = mm(bank[4][0:n, 16 * i:16 * i + 16], hT[:, k, t0:t0 + n], w_small[:, k, :],
                              start=(k == 0), stop=(k == KT - 1))
            last.then_inc(small_ready, 1)
            pe.wait_ge(qk_sq, 1)
            for c in range(2 * H):
                if c < 4:
                    pe.wait_ge(z_ready, H)
                else:
                    pe.wait_ge(qk_root, c - 3)
                mm(bank[c % 4][:, 0:T], ones, nrm[:, c, :], start=True, stop=True).then_inc(qk_sum, 1)
            pe.wait_ge(gates_done, 1)
            for c in range(CH):
                mm(bank[5][:, 8 * c:8 * c + 8], upper, gdec[:, c, :], start=True, stop=True)
            mm(bank[5][:, 16:32], ones, gdec[:, 0:2, :].rearrange("p c h -> p (c h)"),
               start=True, stop=True).then_inc(cum_ps, 1)
            pe.wait_ge(qk_normed, 4)

            def turn(g, src):
                n = 2 * g + src
                if n >= 2:
                    pe.wait_ge(turned_sb, n - 1)
                for j in range(GRP):
                    i = GRP * g + j
                    c, h = i // H, i % H
                    last = nc.tensor.transpose(bank[6 + n % 2][:, P * j:P * (j + 1)],
                                               qkv[:, H * (1 + src) + h, P * c:P * (c + 1)], ident)
                last.then_inc(turned, 1)

            for g in range(NG):
                if g == 0:
                    pe.wait_ge(qk_root, 2 * H)
                elif g < 3:
                    pe.wait_ge(arg_done, g)
                else:
                    pe.wait_ge(ecum_row, 1)
                for j in range(GRP):
                    c, h = (GRP * g + j) // H, (GRP * g + j) % H
                    last = mm(bank[0][:, P * j:P * (j + 1)], gdec[:, c, h:h + 1].to_broadcast([P, P]), upper,
                              start=True, stop=True)
                last.then_inc(rowdec, 1)
                if g >= 1:
                    pe.wait_ge(coef_done, g)
                for b, q in ((1, 1), (2, 0)):
                    for j in range(GRP):
                        c, h = (GRP * g + j) // H, (GRP * g + j) % H
                        last = mm(bank[b][:, P * j:P * (j + 1)], qkv[:, H + h, P * c:P * (c + 1)],
                                  qkv[:, q * H + h, P * c:P * (c + 1)], start=True, stop=True)
                last.then_inc(kk_ready, 1)
                turn(g, 0)
                turn(g, 1)
            arrived(C_STATE)
            arrived(C_STATE + 1)
            for h in range(H):
                for b in range(NS):
                    i = h * NS + b
                    last = mm(bank[3][:, 2 * i:2 * i + 2], states[:, i, :], qkv[:, h:h + H + 1:H, NPR + b],
                              start=True, stop=True)
            last.then_inc(sread_ps, 1)
            pe.wait_ge(sdiag, 1)
            for r in range(2):
                mm(bank[5][:, 64 * r:64 * r + 64], ones[0:NS, :], diag8[0:NS, r, :], start=True, stop=True)
            mm(bank[5][:, 128:192], ones, qk_, start=True, stop=True).then_inc(srow_ps, 1)

            for l in range(LEVELS):
                for g in range(NG):
                    if l == 0:
                        pe.wait_ge(coef_done, NG)
                        pe.wait_ge(ecum_row, 2)
                        if g == 3:
                            pe.wait_ge(su_done, 1)
                    else:
                        pe.wait_ge(x_sb, NG * (l - 1) + g + 1)
                    for j in range(GRP):
                        i = GRP * g + j
                        out = bank[g][:, P * j:P * (j + 1)]
                        if l == 0:
                            last = nc.tensor.transpose(out, coefT[:, i, :], ident)
                        else:
                            last = mm(out, coefT[:, i, :], X[:, i, :], start=True, stop=True)
                    last.then_inc(y_ps, 1)
                for g in range(NG):
                    pe.wait_ge(y_sb, NG * l + g + 1)
                    bx, bz = bank[4 + g % 2], bank[6 + g % 2]
                    if l == 0 and g < 2:
                        pe.wait_ge(turned_sb, 2 * NG)
                        pe.wait_ge(su_done, 1)
                    if NG * l + g >= 2:
                        pe.wait_ge(z_sb, NG * l + g - 1)
                    if 0 < l < LEVELS - 1:
                        for j in range(GRP):
                            i = GRP * g + j
                            last = mm(bx[:, P * j:P * (j + 1)], Z[:, i, :], Y[:, i, :], start=True, stop=True)
                        last.then_inc(x_ps, 1)
                    for j in range(GRP):
                        i = GRP * g + j
                        if l == 0:
                            last = nc.tensor.transpose(bz[:, P * j:P * (j + 1)], Y[:, i, :], ident)
                        else:
                            last = mm(bz[:, P * j:P * (j + 1)], Y[:, i, :], Z[:, i, :], start=True, stop=True)
                    last.then_inc(z_ps, 1)
            pe.wait_ge(z_sb, NG * LEVELS)
            for c in range(CH):
                if c == 1:
                    pe.wait_ge(s_sb, 2)
                    for g in range(2):
                        for j in range(GRP):
                            h = GRP * g + j
                            last = mm(bank[g][:, P * j:P * (j + 1)], qkv[:, H + h, P:2 * P], S_new[:, h, :],
                                      start=True, stop=True)
                        last.then_inc(ks_ps, 1)
                for g in range(2):
                    if c == 1:
                        pe.wait_ge(w_sb, g + 1)
                    for j in range(GRP):
                        h = GRP * g + j
                        rhs = vtok[:, h, :] if c == 0 else rhs_w[:, h, :]
                        last = mm(bank[2 + g][:, P * j:P * (j + 1)], Z[:, H * c + h, :], rhs, start=True, stop=True)
                    last.then_inc(u_ps, 1)
                for g in range(2):
                    pe.wait_ge(u_sb, 2 * c + g + 1)
                    if c == 1:
                        pe.wait_ge(s_sb, 2)
                    if c == 0 and g == 0:
                        pe.wait_ge(kdec_done, 1)
                    for j in range(GRP):
                        h = GRP * g + j
                        last = mm(bank[4 + g][:, P * j:P * (j + 1)], ktok[:, H * c + h, :], u_tok[:, h, :],
                                  start=True, stop=True)
                    last.then_inc(s_ps, 1)
                    if c == 1:
                        pe.wait_ge(q_dec_done, 1)
                        pe.wait_ge(o_sb, g + 1)
                    for j in range(GRP):
                        h = GRP * g + j
                        out = bank[6 + g][:, P * j:P * (j + 1)]
                        last = mm(out, u_tok[:, h, :], attT[:, H * c + h, :], start=True, stop=(c == 0))
                        if c == 1:
                            last = mm(out, S_new[:, h, :], qkv[:, h, P:2 * P], start=False, stop=True)
                    last.then_inc(o_ps, 1)
            pe.wait_ge(sou, 1)
            pe.wait_ge(w_sb, 2)
            nc.tensor.transpose(bank[0][0:64, 0:P], u_s, ident)
            nc.tensor.transpose(bank[0][0:64, P:2 * P],
                                sk, ident).then_inc(st_ps, 1)
            for i in range(16):
                pe.wait_ge(st_sb, 2 + i)
                if i < 2:
                    pe.wait_ge(u_sb, 4)
                else:
                    pe.wait_ge(snew, i - 1)
                mm(bank[2 + i % 2], kv_rows[:, 1, :], wide[:, i % 2, :], start=True, stop=True).then_inc(sout_ps, 1)
            for h in range(H):
                pe.wait_ge(osq_done, h + 1)
                if h < 2:
                    pe.wait_ge(snew, 16)
                else:
                    pe.wait_ge(oroot, h - 1)
                mm(bank[2 + h % 2][:, 0:T], ones, osq[:, h, :], start=True, stop=True).then_inc(osum, 1)

            def out_projection(first, src, src_ready, done, added):
                for d in range(KT):
                    if d % 4 == 0:
                        arrived(first + d // 4)
                    if d >= 4:
                        pe.wait_ge(added, d - 3)
                    for h in range(H):
                        if d == 0:
                            src_ready(h)
                        last = mm(bank[4 + d % 4][:, 0:T], tile4(first + d // 4)[:, d % 4, h, :], src[:, h, :],
                                  start=(h == 0), stop=(h == H - 1))
                    last.then_inc(done, 1)

            def o_ready(h):
                pe.wait_ge(o_normed, h + 1)
                if h == 0:
                    pe.wait_ge(o_sb, 4)
                    pe.wait_ge(s_sb, 4)

            out_projection(C_OUT, oT, o_ready, outp, out_added)

            def feed_forward(e, slot_of, wait_full, gate_s, up_s, act_s, down_s, added_s):
                for f in range(FT):
                    if f % 2 == 0:
                        wait_full(f // 2)
                    w = ring[:, slot_of(f // 2), :].rearrange("p (f u k m) -> p f u k m", f=2, u=2, k=KT)
                    pe.wait_ge(act_s, e * FT + f - 1) if not isinstance(e, int) or e * FT + f >= 2 else None
                    for u, s in ((0, gate_s), (1, up_s)):
                        for k in range(KT):
                            last = mm(bank[2 * (f % 2) + u][:, 0:T], w[:, f % 2, u, k, :], hT[:, k, :],
                                      start=(k == 0), stop=(k == KT - 1))
                        last.then_inc(s, 1)
                for d in range(KT):
                    wait_full(FT // 2 + d)
                    w = ring[:, slot_of(FT // 2 + d), 0:FT * P].rearrange("p (f m) -> p f m", m=P)
                    if not isinstance(e, int) or e * KT + d >= 3:
                        pe.wait_ge(added_s, e * KT + d - 2)
                    for f in range(FT):
                        if d == 0:
                            pe.wait_ge(act_s, e * FT + f + 1)
                        last = mm(bank[4 + d % 3][:, 0:T], w[:, f, :], aT[:, f, :], start=(f == 0), stop=(f == FT - 1))
                    last.then_inc(down_s, 1)

            norm_sums(1)
            pe.wait_ge(normed, 2 * KT)
            feed_forward(0, lambda i: (C_GU + i) % SLOTS, lambda i: arrived(C_GU + i),
                         f_gate, f_up, f_act, f_down, f_added)

            norm_sums(2)

            def rotate(c):
                pe.wait_ge(rope_loaded, 16)
                pe.wait_ge(aproj_sb, c + 1)
                if c >= 2:
                    pe.wait_ge(roped, c - 1)
                mm(bank[4 + c % 2][0:ROT, 0:T], rot_p, aq[:, c, :], start=True, stop=True).then_inc(rot_ps, 1)

            for c in range(16):
                if c % 4 == 0:
                    arrived(C_AIN + c // 4)
                if c >= 4:
                    pe.wait_ge(aproj_sb, c - 3)
                for k in range(KT):
                    if c == 0:
                        pe.wait_ge(normed, 2 * KT + k + 1)
                    last = mm(bank[c % 4][:, 0:T], tile4(C_AIN + c // 4)[:, c % 4, k, :], hT[:, k, :],
                              start=(k == 0), stop=(k == KT - 1))
                last.then_inc(aproj, 1)
                if 1 <= c <= 12:
                    rotate(c - 1)
            pe.wait_ge(aproj_sb, 16)
            for t in range(CH):
                for h in range(KVH):
                    last = nc.tensor.transpose(bank[6 + t][:, P * h:P * (h + 1)], aq[:, 12 + h, P * t:P * (t + 1)], ident)
                last.then_inc(v_ps, 1)
            pe.wait_ge(roped, 12)

            def scores(h):
                if h >= 2:
                    pe.wait_ge(sc_max, h - 1)
                kv = 8 + h // 2
                mm(bank[h % 2][:, 0:P], aq[:, h, 0:P], aq[:, kv, 0:P], start=True, stop=True)
                mm(bank[h % 2][:, P:3 * P], aq[:, h, P:2 * P], aq[:, kv, 0:2 * P],
                   start=True, stop=True).then_inc(sc_ps, 1)

            def turn_probs(h):
                pe.wait_ge(p_sb, h + 1)
                if h >= 2:
                    pe.wait_ge(pT_sb, h - 1)
                for j in range(3):
                    last = nc.tensor.transpose(bank[2 + h % 2][:, P * j:P * (j + 1)], pr_s[:, h % 2, P * j:P * (j + 1)], ident)
                last.then_inc(pT_ps, 1)

            def values(h):
                pe.wait_ge(pT_sb, h + 1)
                pe.wait_ge(v_sb, 2)
                if h >= 2:
                    pe.wait_ge(po_sb, h - 1)
                b, kv = bank[4 + h % 2], h // 2
                mm(b[:, 0:P], v_tok[:, kv, :], pr_T[:, h % 2, 0:P], start=True, stop=True)
                mm(b[:, P:2 * P], v_tok[:, kv, :], pr_T[:, h % 2, P:2 * P], start=True, stop=False)
                mm(b[:, P:2 * P], v_tok[:, KVH + kv, :], pr_T[:, h % 2, 2 * P:3 * P],
                   start=False, stop=True).then_inc(po_ps, 1)

            for i in range(H + 2):
                if i < H:
                    scores(i)
                if 1 <= i <= H:
                    turn_probs(i - 1)
                if i >= 2:
                    values(i - 2)
            pe.wait_ge(prod_done, 1)
            mm(bank[6][0:64, 0:1], prodn, ones[:, 0:1], start=True, stop=True).then_inc(lnew_ps, 1)
            pe.wait_ge(q_wide_set, 1)
            pe.wait_ge(sc_max, H)
            pe.wait_ge(pT_sb, H)
            for c in range(2 * NS):
                n, b = C_K + c, c // 2
                arrived(n)
                keys = ring[:, n % SLOTS, :].rearrange("p (q g h t) -> p q g h t", q=2, g=4, h=KVH)
                for h in range(KVH):
                    for q in range(2):
                        last = mm(bank[2 * (c % 2) + q][0:64, :].rearrange("p (g t) -> p g t", t=PAGE),
                                  q_wide[:, KVH * b + h, :], keys[:, q, :, h, :],
                                  start=(b == 0 and h == 0), stop=(b == NS - 1 and h == KVH - 1), skip_group_check=True)
                last.then_inc(k_read, 1)
            pe.wait_ge(diag_done, 1)
            pe.wait_ge(po_sb, H)
            for g in range(N_PAGES):
                last = mm(bank[4 + g // 8][:, 64 * (g % 8):64 * (g % 8 + 1)], prob[:, PAGE * g:PAGE * (g + 1)], rd_diag,
                          start=True, stop=True)
                if g % 8 == 7:
                    last.then_inc(probT_ps, 1)
            mm(bank[7][:, 0:64], ones[0:64, :], p_diag, start=True, stop=True).then_inc(probT_ps, 1)

            def turn_o(b):
                pe.wait_ge(o8_done, b + 1)
                nc.tensor.transpose(bank[6][:, H * b:H * (b + 1)], o8[:, b, :], ident[0:8, 0:8]).then_inc(o8_turned, 1)

            for c in range(2 * NS):
                n, b = C_V + c, c // 2
                arrived(n)
                if c % 8 == 0:
                    pe.wait_ge(probT_sb, 2)
                if c % 2 == 0 and b >= 4:
                    pe.wait_ge(o8_done, b - 3)
                for g in range(PPC):
                    page = (c % 2) * PPC + g
                    last = mm(bank[b % 4][0:8, :], prob_T[:, page, H * b:H * (b + 1)],
                              ring[:, n % SLOTS, 512 * g:512 * (g + 1)], start=(page == 0), stop=(page == N_PAGES - 1))
                last.then_inc(v_read, 1)
                if c % 2 == 0 and b >= 1:
                    turn_o(b - 1)
            turn_o(NS - 1)

            def att_ready(h):
                if h == 0:
                    pe.wait_ge(po_sb, H)
                    pe.wait_ge(od_done, 1)

            out_projection(C_AOUT, o_att, att_ready, aout, aout_added)
            norm_sums(3)
            pe.wait_ge(normed, 4 * KT)
            for i, (t0, n) in enumerate(TOK_TILES):
                for k in range(KT):
                    last = mm(bank[0][0:n, NE * i:NE * i + NE], hT[:, k, t0:t0 + n], router[:, k, :],
                              start=(k == 0), stop=(k == KT - 1))
            last.then_inc(r_ps, 1)
            pe.wait_ge(r_gate, 1)
            for i, (t0, n) in enumerate(TOK_TILES):
                out = bank[0][0:n, 32 + NE * i:32 + NE * (i + 1)]
                for j in range(i):
                    mm(out, ones[:, 0:n], rrank[:, j, :], start=(j == 0), stop=False)
                mm(out, upper[0:n, 0:n], rrank[0:n, i, :], start=(i == 0), stop=True)
            for i, (t0, n) in enumerate(TOK_TILES):
                last = mm(bank[0][0:1, 64:64 + NE], ones[0:n, 0:1], rrank[0:n, i, :], start=(i == 0), stop=(i == 2))
            last.then_inc(pos_ps, 1)
            for i, (t0, n) in enumerate(TOK_TILES):
                for half in range(2):
                    m = 2 * i + half
                    if m >= 2:
                        pe.wait_ge(h_tok, m - 1)
                    for j in range(4):
                        last = nc.tensor.transpose(bank[2 + half][0:n, P * j:P * (j + 1)],
                                                   hT[:, 4 * half + j, t0:t0 + n], ident)
                    last.then_inc(h_turned, 1)
            pe.wait_ge(h_tok, 6)

            def expert_full(e):
                def full(i):
                    sl = i % SLOTS
                    pe.wait_ge(ring_full[sl], e * moe_fills(sl) + (full_value(C_MOE + sl) + 16 * (i // SLOTS)))
                return full

            def gather(e):
                pe.wait_ge(picked, e + 1)
                for half in range(2):
                    for j in range(4):
                        k = 4 * half + j
                        for i, (t0, n) in enumerate(TOK_TILES):
                            last = mm(bank[6 + half][:, CAP * j:CAP * (j + 1)], htok[0:n, i, P * k:P * (k + 1)],
                                      pick[0:n, i, :], start=(i == 0), stop=(i == 2))
                    last.then_inc(gathered, 1)

            def turn_y(e):
                pe.wait_ge(yT_sb, e * KT + KT)
                pe.wait_ge(xe_sb, 2 * e + 4)
                for half in range(2):
                    for j in range(4):
                        last = nc.tensor.transpose(bank[6 + half][0:CAP, P * j:P * (j + 1)], yeT[:, 4 * half + j, :], ident)
                    last.then_inc(y_turned, 1)

            def combine(e, d):
                if d == 0:
                    pe.wait_ge(ye_sb, 2 * e + 2)
                if d >= 2:
                    pe.wait_ge(comb_added, e * KT + d - 1)
                mm(bank[6 + d % 2][:, 0:T], ye[:, P * d:P * (d + 1)], spread, start=True, stop=True).then_inc(comb, 1)

            def sparse_expert(e, first):
                full = expert_full(e)
                for f in range(FT):
                    if not first:
                        if f == 4:
                            turn_y(e - 1)
                        if 8 <= f < 8 + KT:
                            combine(e - 1, f - 8)
                    if f == 18:
                        if not first:
                            pe.wait_ge(comb_added, e * KT)
                        for i, (t0, n) in enumerate(TOK_TILES):
                            last = nc.tensor.transpose(bank[6][0:CAP, t0:t0 + n], pick_g[0:n, i, :], ident[0:n, 0:n])
                        last.then_inc(spread_ps, 1)
                    if f % 2 == 0:
                        full(f // 2)
                    if f == 0:
                        pe.wait_ge(xe_sb, 2 * e + 2)
                    w = ring[:, (f // 2) % SLOTS, :].rearrange("p (f u k m) -> p f u k m", f=2, u=2, k=KT)
                    if not first or f >= 2:
                        pe.wait_ge(m_act, e * FT + f - 1)
                    for u, sm_ in ((0, m_gate), (1, m_up)):
                        for k in range(KT):
                            last = mm(bank[2 * (f % 2) + u][:, 0:CAP], w[:, f % 2, u, k, :], xe[:, k, :],
                                      start=(k == 0), stop=(k == KT - 1))
                        last.then_inc(sm_, 1)
                for d in range(KT):
                    if d == 2:
                        pe.wait_ge(spread_sb, e + 1)
                        gather(e + 1)
                    full(FT // 2 + d)
                    w = ring[:, (FT // 2 + d) % SLOTS, 0:FT * P].rearrange("p (f m) -> p f m", m=P)
                    if not first or d >= 2:
                        pe.wait_ge(yT_sb, e * KT + d - 1)
                    for f in range(FT):
                        if d == 0:
                            pe.wait_ge(m_act, e * FT + f + 1)
                        last = mm(bank[4 + d % 2][:, 0:CAP], w[:, f, :], s_act[:, f, :], start=(f == 0), stop=(f == FT - 1))
                    last.then_inc(m_down, 1)

            def dense_expert(e):
                feed_forward(e, lambda i: i % SLOTS, expert_full(e), m_gate, m_up, m_act, m_down, m_added)

            pe.wait_ge(over_set, 1)
            dense = pe.value_load(dense_flag[0:1, 0:1], min_val=0, max_val=1)
            with pe.If(dense == 0):
                gather(0)
                sparse_expert(0, True)
                with pe.Fori(1, NE) as e:
                    sparse_expert(e, False)
                turn_y(NE - 1)
                for d in range(KT):
                    combine(NE - 1, d)
            with pe.Else():
                for i, (t0, n) in enumerate(TOK_TILES):
                    last = nc.tensor.transpose(bank[1][0:NE, t0:t0 + n], rgate[0:n, i, 0:NE], ident[0:n, 0:n])
                last.then_inc(r_turned, 1)
                pe.wait_ge(r_diag, 2)
                for e in range(NE):
                    if e >= 2:
                        pe.wait_ge(gb_sb, e - 1)
                    mm(bank[2 + e % 2][:, 0:T], ones[0:NE, :], gate_d[0:NE, e, :], start=True, stop=True).then_inc(gb_ps, 1)
                pe.wait_ge(gb_sb, NE)
                dense_expert(0)
                with pe.Fori(1, NE) as e:
                    dense_expert(e)
            norm_sums(4)

        @block.scalar
        def _(act):
            steps = [0]

            def link(ins):
                steps[0] += 1
                ins.then_inc(act_link, 1)
                act.wait_ge(act_link, steps[0])

            A = nc.scalar.activation
            act.dma_start(xT[:, :, :], x_in).then_inc(x_loaded, 16)
            act.dma_start(cst[:, :], cst_in).then_inc(prm_loaded, 16)
            act.dma_start(prm[:, :], prm_in).then_inc(prm_loaded, 16)
            act.dma_start(conv_prev[:, :, :, :], conv_in).then_inc(prm_loaded, 16)
            act.dma_start(table[:, :], table_in).then_inc(table_loaded, 16)
            act.wait_ge(prm_loaded, 48)

            def norm_root(i):
                act.wait_ge(sum_sq, i + 1)
                A(rms, bank[7][:, 0:T], ACT.Sqrt, bias=eps, scale=1.0 / D).then_inc(root, 1)

            act.wait_ge(consts_set, 1)
            norm_root(0)
            act.wait_ge(normed, KT)
            for c in range(QKV + 1):
                if c < QKV:
                    act.wait_ge(proj, c + 1)
                    if c >= 2:
                        act.wait_ge(conv_done, c - 1)
                        act.wait_ge(raw_saved, c - 1)
                    A(raw[:, c % 2, CONV_W - 1:], bank[c % 4][:, 0:T], ACT.Copy).then_inc(raw_ready, 1)
                if c >= 1:
                    act.wait_ge(conv_done, c)
                    A(qkv[:, c - 1, 0:NPR], qkv[:, c - 1, 0:NPR], ACT.Silu).then_inc(silu_done, 1)
            act.wait_ge(conv_s_done, 1)
            A(qkv[:, :, NPR:T], qkv[:, :, NPR:T], ACT.Silu).then_inc(silu_done, 1)
            for h in range(H):
                act.wait_ge(proj, QKV + h + 1)
                A(zT[:, h, :], bank[h % 4][:, 0:T], ACT.Silu).then_inc(z_ready, 1)
            for c in range(2 * H):
                act.wait_ge(qk_sum, c + 1)
                if c < H:
                    A(nrm[:, c, :], bank[c % 4][:, 0:T], ACT.Sqrt, bias=eps_q, scale=float(DK)).then_inc(qk_root, 1)
                else:
                    A(nrm[:, c, :], bank[c % 4][:, 0:T], ACT.Sqrt, bias=eps, scale=1.0).then_inc(qk_root, 1)
            act.wait_ge(gates_a, 1)
            A(beta, ba[:, :, 0:H], ACT.Exp, scale=-1.0)
            A(e_alog, p_("a_log"), ACT.Exp)
            link(A(t_exp, t_abs, ACT.Exp, scale=-1.0))
            A(t_exp, t_exp, ACT.Ln, bias=ones[:, 0:1]).then_inc(gates_e, 1)
            act.wait_ge(cum_sb, 1)
            A(neg_ecum, cum, ACT.Exp)
            A(e_end, e_end, ACT.Exp)
            A(ge_s[0:NS], gdec[0:NS, 2, :], ACT.Exp)
            A(to_end, to_end, ACT.Exp).then_inc(cum_exp, 1)

            def untuck(g):
                for src, dst in ((0, ktok), (1, vtok)):
                    n = 2 * g + src
                    act.wait_ge(turned, n + 1)
                    A(dst[:, GRP * g:GRP * (g + 1), :].rearrange("p i n -> p (i n)"), bank[6 + n % 2][:, :],
                      ACT.Copy).then_inc(turned_sb, 1)

            for g in range(NG):
                act.wait_ge(arg_done, g + 1)
                if g >= CH:
                    A(Y[:, GRP * (g - 2):GRP * (g - 1), :].rearrange("p i n -> p (i n)"), bank[0][:, :],
                      ACT.Exp).then_inc(ecum_row, 1)
                A(decT[:, g % 2, :], decT[:, g % 2, :], ACT.Exp).then_inc(dec_exp, 1)
                untuck(g)
            for c in range(CH):
                for g in range(2):
                    act.wait_ge(o_ps, 2 * c + g + 1)
                    if c == 0 and g == 0:
                        act.wait_ge(qk_normed, 4)
                    A(oT[:, GRP * g:GRP * (g + 1), P * c:P * (c + 1)],
                      bank[6 + g][:, :].rearrange("p (h t) -> p h t", t=P), ACT.Copy).then_inc(o_sb, 1)
            for h in range(H):
                act.wait_ge(osum, h + 1)
                A(osq[:, h, :], bank[2 + h % 2][:, 0:T], ACT.Sqrt, bias=eps, scale=1.0 / DK).then_inc(oroot, 1)
            norm_root(1)

            def silus(e, gate_s, act_s, silu_s):
                for f in range(FT):
                    act.wait_ge(gate_s, e * FT + f + 1)
                    if not isinstance(e, int) or e * FT + f >= 2:
                        act.wait_ge(act_s, e * FT + f - 1)
                    A(sil[:, f % 2, :], bank[2 * (f % 2)][:, 0:T], ACT.Silu).then_inc(silu_s, 1)

            silus(0, f_gate, f_act, f_silu)
            norm_root(2)
            for c in range(16):
                act.wait_ge(aproj, c + 1)
                if c == 0:
                    act.dma_start(rope, rope_in).then_inc(rope_loaded, 16)
                A(aq[:, c, :], bank[c % 4][:, 0:T], ACT.Copy).then_inc(aproj_sb, 1)
            for t in range(CH):
                act.wait_ge(v_ps, t + 1)
                A(v_tok[:, KVH * t:KVH * (t + 1), :].rearrange("p i n -> p (i n)"), bank[6 + t][:, :],
                  ACT.Copy).then_inc(v_sb, 1)

            def p_exp(h):
                act.wait_ge(sc_max, h + 1)
                i, m = h % 2, 2 * (h % 2)
                A(pr_s[:, i, 0:P], pr_s[:, i, 0:P], ACT.Exp, bias=pmax[:, m:m + 1], accum_out=psums[:, m:m + 1])
                A(pr_s[:, i, P:3 * P], pr_s[:, i, P:3 * P], ACT.Exp, bias=pmax[:, m + 1:m + 2],
                  accum_out=psums[:, m + 1:m + 2]).then_inc(sc_exp, 1)

            def p_turned(h):
                act.wait_ge(pT_ps, h + 1)
                if h >= 2:
                    act.wait_ge(po_ps, h - 1)
                A(pr_T[:, h % 2, :], bank[2 + h % 2][:, 0:3 * P], ACT.Copy).then_inc(pT_sb, 1)

            def p_out(h):
                act.wait_ge(po_ps, h + 1)
                A(o_att[:, h, 0:NPR], bank[4 + h % 2][:, 0:NPR], ACT.Copy).then_inc(po_sb, 1)

            for i in range(H + 2):
                if i < H:
                    p_exp(i)
                if 1 <= i <= H:
                    p_turned(i - 1)
                if i >= 2:
                    p_out(i - 2)
            for n in range(C_BOTH, C_V + SLOTS):
                load_pages(act, n, range(PPC // 2, PPC))
            act.wait_ge(bias_done, 1)
            for n in range(BLOCKS):
                A(prob[:, 256 * n:256 * (n + 1)], bank[n // 2][0:64, 256 * (n % 2):256 * (n % 2 + 1)], ACT.Exp,
                  bias=biases[:, n:n + 1], scale=SCALE, accum_out=sums[:, n:n + 1])
            A(p_new, l_new, ACT.Exp, bias=m_neg, scale=SCALE).then_inc(pexp, 1)
            for i in range(2):
                act.wait_ge(probT_ps, i + 1)
                A(prob_T[:, 8 * i:8 * (i + 1), :].rearrange("p g r -> p (g r)"), bank[4 + i][:, :], ACT.Copy)\
                    .then_inc(probT_sb, 1)
            for n in range(C_V + SLOTS, C_AOUT):
                load_pages(act, n, range(PPC // 2, PPC))
            norm_root(3)
            act.wait_ge(r_arg, 1)
            A(rgate[:, :, 0:NE], rgate[:, :, 0:NE], ACT.Exp).then_inc(r_exp, 1)
            act.wait_ge(stored, 16 * 5)
            for i, (t0, n) in enumerate(TOK_TILES):
                for half in range(2):
                    m = 2 * i + half
                    act.wait_ge(h_turned, m + 1)
                    A(htok[0:n, i, 512 * half:512 * (half + 1)], bank[2 + half][0:n, :], ACT.Copy).then_inc(h_tok, 1)

            def take_gathered(e):
                for half in range(2):
                    act.wait_ge(gathered, 2 * e + half + 1)
                    A(xe[:, 4 * half:4 * half + 4, :].rearrange("p k n -> p (k n)"), bank[6 + half][:, 0:4 * CAP],
                      ACT.Copy).then_inc(xe_sb, 1)

            def take_turned(e):
                for half in range(2):
                    act.wait_ge(y_turned, 2 * e + half + 1)
                    if not isinstance(e, int) or e > 0:
                        act.wait_ge(comb, e * KT)
                    A(ye[:, 512 * half:512 * (half + 1)], bank[6 + half][0:CAP, :], ACT.Copy).then_inc(ye_sb, 1)

            def sparse_expert(e, first):
                for f in range(FT):
                    if f == 4 and not first:
                        if isinstance(e, int):
                            take_turned(e - 1)
                        else:
                            for half in range(2):
                                act.wait_ge(y_turned, 2 * e + half - 1)
                                A(ye[:, 512 * half:512 * (half + 1)], bank[6 + half][0:CAP, :], ACT.Copy).then_inc(ye_sb, 1)
                    if f == 18:
                        act.wait_ge(spread_ps, e + 1)
                        if not first:
                            act.wait_ge(comb, e * KT)
                        A(spread, bank[6][0:CAP, 0:T], ACT.Copy).then_inc(spread_sb, 1)
                    act.wait_ge(m_gate, e * FT + f + 1)
                    if not first or f >= 2:
                        act.wait_ge(m_act, e * FT + f - 1)
                    A(s_sil[:, f % 2, :], bank[2 * (f % 2)][:, 0:CAP], ACT.Silu).then_inc(m_silu, 1)
                for d in range(KT):
                    if d == 2:
                        take_gathered(e + 1)
                    act.wait_ge(m_down, e * KT + d + 1)
                    if not first and d == 0:
                        act.wait_ge(y_turned, 2 * e)
                    A(yeT[:, d, :], bank[4 + d % 2][:, 0:CAP], ACT.Copy).then_inc(yT_sb, 1)

            act.wait_ge(over_set, 1)
            dense = act.value_load(dense_flag[0:1, 0:1], min_val=0, max_val=1)
            with act.If(dense == 0):
                take_gathered(0)
                sparse_expert(0, True)
                with act.Fori(1, NE) as e:
                    sparse_expert(e, False)
                take_turned(NE - 1)
            with act.Else():
                for e in range(NE):
                    act.wait_ge(gb_ps, e + 1)
                    A(gate_b[:, e, :], bank[2 + e % 2][:, 0:T], ACT.Copy).then_inc(gb_sb, 1)
                silus(0, m_gate, m_act, m_silu)
                with act.Fori(1, NE) as e:
                    silus(e, m_gate, m_act, m_silu)
            norm_root(4)

        @block.gpsimd
        def _(pool):
            steps = [0]

            def link(ins):
                steps[0] += 1
                ins.then_inc(pool_link, 1)
                pool.wait_ge(pool_link, steps[0])

            G = nc.gpsimd
            link(G.memset(raw[:, :, :], 0.0))
            link(G.memset(small[:, :], 0.0))
            G.memset(small[:, 766:767], 0.0).then_inc(consts_set, 1)
            for c in range(QKV):
                pool.wait_ge(raw_ready, c + 1)
                G.tensor_copy(conv_last[:, c, :], raw[:, c % 2, NPR:NPR + CONV_W - 1])
                G.tensor_copy(conv_new[:, c, :], raw[:, c % 2, NPR + CONV_W - 1:]).then_inc(raw_saved, 1)
            pool.wait_ge(raw_saved, QKV)
            pool.wait_ge(prm_loaded, 48)
            dst = qkv[:, :, NPR:T]
            tmp = nrm[:, 0, 0:QKV * NS].rearrange("p (c b) -> p c b", b=NS)
            wide_w = lambda j: conv_w[:, :, j:j + 1].to_broadcast([P, QKV, NS])
            link(G.tensor_tensor(dst, conv_prev[:, :, 0, :], wide_w(0), ALU.mult))
            for j in range(1, CONV_W):
                src = conv_prev[:, :, j, :] if j < CONV_W - 1 else conv_new[:, :, :]
                link(G.tensor_tensor(tmp, src, wide_w(j), ALU.mult))
                if j < CONV_W - 1:
                    link(G.tensor_tensor(dst, dst, tmp, ALU.add))
                else:
                    G.tensor_tensor(dst, dst, tmp, ALU.add).then_inc(conv_s_done, 1)
            pool.dma_start(convp_out, conv_last[:, :, :]).then_inc(stored, 16)
            pool.dma_start(convs_out[:, :, 0:CONV_W - 2, :], conv_prev[:, :, 1:, :]).then_inc(stored, 16)
            pool.dma_start(convs_out[:, :, CONV_W - 2, :], conv_new[:, :, :]).then_inc(stored, 16)
            pool.wait_ge(sread_ps, 1)
            pool.wait_ge(su_done, 1)
            for i in range(8):
                s = states[:, 8 * i:8 * i + 8, :]
                G.tensor_tensor(s, s, row_b[:, 1, 8 * i:8 * i + 8].unsqueeze(2).to_broadcast([P, 8, DK]),
                                ALU.mult).then_inc(sdecayed, 1)
            pool.wait_ge(st_sb, 1)
            for i in range(16):
                if i >= 2:
                    pool.wait_ge(sout_ps, i - 1)
                G.tensor_tensor(wide[:, i % 2, :].rearrange("p (a v) -> p a v", a=4),
                                kv_rows[:, 0, :].unsqueeze(1).to_broadcast([64, 4, DK]),
                                ident[0:64, 4 * i:4 * i + 4].unsqueeze(2).to_broadcast([64, 4, DK]),
                                ALU.mult).then_inc(st_sb, 1)
            pool.wait_ge(snew, 16)
            pool.dma_start(deltas_out, states[:, :, :]).then_inc(states_stored, 16)
            pool.wait_ge(s_sb, 4)
            pool.wait_ge(o_sb, 4)
            pool.dma_start(deltap_out, S_fin).then_inc(stored, 16)
            pool.wait_ge(stored, 64)
            pool.wait_ge(states_stored, 16)
            G.memset(small[:, 766:767], 0.0).then_inc(core_done, 1)
            pool.wait_ge(roped, 12)
            pool.wait_ge(aproj_sb, 16)
            pool.dma_start(kv_out, aq[:, 8:16, :]).then_inc(stored, 16)
            pool.wait_ge(normed, 5 * KT)
            pool.dma_start(y_out, hT[:, :, :]).then_inc(stored, 16)

        @block.vector
        def _(dve):
            steps = [0]

            def link(ins):
                steps[0] += 1
                ins.then_inc(dve_link, 1)
                dve.wait_ge(dve_link, steps[0])

            V = nc.vector

            def norm(i):
                V.tensor_tensor(hT[:, :, :], xT[:, :, :], xT[:, :, :], ALU.mult).then_inc(squares, 1)
                dve.wait_ge(root, i + 1)
                link(V.reciprocal(rms, rms))
                for k in range(KT):
                    V.scalar_tensor_tensor(out=hT[:, k, :], in0=xT[:, k, :], scalar=gain[:, i, k:k + 1], in1=rms,
                                           op0=ALU.mult, op1=ALU.mult).then_inc(normed, 1)

            dve.wait_ge(x_loaded, 16)
            dve.wait_ge(prm_loaded, 48)
            dve.wait_ge(consts_set, 1)
            norm(0)
            for c in range(QKV):
                dve.wait_ge(raw_ready, c + 1)
                r, dst = raw[:, c % 2, :], qkv[:, c, 0:NPR]
                link(V.tensor_scalar(dst, r[:, 0:NPR], conv_w[:, c, 0:1], None, ALU.mult))
                for j in range(1, CONV_W):
                    ins = V.scalar_tensor_tensor(out=dst, in0=r[:, j:j + NPR], scalar=conv_w[:, c, j:j + 1], in1=dst,
                                                 op0=ALU.mult, op1=ALU.add)
                    if j < CONV_W - 1:
                        link(ins)
                    else:
                        ins.then_inc(conv_done, 1)
            dve.wait_ge(silu_done, QKV + 1)
            V.tensor_tensor(nrm, qkv[:, 0:2 * H, :], qkv[:, 0:2 * H, :], ALU.mult).then_inc(qk_sq, 1)
            dve.wait_ge(small_ready, 1)
            V.tensor_copy(ba[:, 0:2, :], bank[4][:, 0:32].rearrange("p (i n) -> p i n", i=2))
            link(V.tensor_copy(ba[0:NS, 2, :], bank[4][0:NS, 32:48]))
            xg = ba[:, :, H:2 * H]
            link(V.tensor_tensor(xg, xg, p_("dt_bias").unsqueeze(1).to_broadcast([P, 3, H]), ALU.add))
            V.scalar_tensor_tensor(out=t_abs, in0=xg, scalar=-1.0, in1=xg, op0=ALU.mult, op1=ALU.max).then_inc(gates_a, 1)
            dve.wait_ge(gates_e, 1)
            link(V.tensor_scalar(beta, beta, 1.0, None, ALU.add))
            V.reciprocal(beta, beta)
            link(V.scalar_tensor_tensor(out=gdec, in0=xg, scalar=0.0, in1=t_exp, op0=ALU.max, op1=ALU.add))
            link(V.scalar_tensor_tensor(out=gdec, in0=gdec, scalar=-1.0, in1=e_alog.unsqueeze(1).to_broadcast([P, 3, H]),
                                        op0=ALU.mult, op1=ALU.mult))
            V.tensor_copy(small[:, 767:768], small[:, 766:767]).then_inc(gates_done, 1)
            for i in range(4):
                dve.wait_ge(qk_root, 4 * (i + 1))
                r = nrm[:, 4 * i:4 * i + 4, :]
                link(V.reciprocal(r, r))
                q = qkv[:, 4 * i:4 * i + 4, :]
                V.tensor_tensor(q, q, r, ALU.mult).then_inc(qk_normed, 1)
            dve.wait_ge(cum_ps, 1)
            V.tensor_copy(cum, bank[5][:, 0:16].rearrange("p (c h) -> p c h", c=2))
            link(V.tensor_copy(e_end, bank[5][:, 16:32].rearrange("p (c h) -> p c h", c=2)))
            V.tensor_tensor(to_end, e_end, cum, ALU.subtract).then_inc(cum_sb, 1)
            dve.wait_ge(qk_normed, 4)
            V.tensor_tensor(qk_.rearrange("p (h b) -> p h b", b=NS), qkv[:, 0:H, NPR:T], qkv[:, H:2 * H, NPR:T], ALU.mult)
            dve.wait_ge(cum_exp, 1)
            link(V.tensor_scalar(neg_ecum, neg_ecum, -1.0, None, ALU.mult))
            id8 = ident[0:NS, 0:NS].unsqueeze(1).to_broadcast([NS, H, NS])
            for r, src in ((0, beta[0:NS, 2, :]), (1, ge_s[0:NS, :])):
                ins = V.tensor_tensor(diag8[0:NS, r, :].rearrange("p (h b) -> p h b", b=NS),
                                      src.unsqueeze(2).to_broadcast([NS, H, NS]), id8, ALU.mult)
            ins.then_inc(sdiag, 1)
            for g in range(NG):
                dve.wait_ge(rowdec, g + 1)
                if g == 0:
                    dve.wait_ge(lmask_loaded, 16)
                for j in range(GRP):
                    c, h = (GRP * g + j) // H, (GRP * g + j) % H
                    ins = V.tensor_scalar(decT[:, g % 2, P * j:P * (j + 1)], bank[0][:, P * j:P * (j + 1)],
                                          cum[:, c, h:h + 1], 0.0, ALU.subtract, ALU.min)
                ins.then_inc(arg_done, 1)
                dve.wait_ge(dec_exp, g + 1)
                dve.wait_ge(kk_ready, g + 1)
                dm = decT[:, g % 2, :].rearrange("p (i n) -> p i n", i=GRP)
                link(V.tensor_tensor(dm, dm, upper.unsqueeze(1).to_broadcast([P, GRP, P]), ALU.mult))
                V.tensor_tensor(attT[:, GRP * g:GRP * (g + 1), :].rearrange("p i n -> p (i n)"), bank[2][:, :],
                                decT[:, g % 2, :], ALU.mult)
                for j in range(GRP):
                    i = GRP * g + j
                    ins = V.scalar_tensor_tensor(out=coefT[:, i, :], in0=bank[1][:, P * j:P * (j + 1)],
                                                 scalar=beta[:, i // H, i % H:i % H + 1],
                                                 in1=decT[:, g % 2, P * j:P * (j + 1)], op0=ALU.mult, op1=ALU.mult)
                ins.then_inc(coef_done, 1)
            dve.wait_ge(ecum_row, 2)
            V.tensor_tensor(qkv[:, 0:H, P:2 * P], qkv[:, 0:H, P:2 * P], Y[:, 0:H, :], ALU.mult).then_inc(q_dec_done, 1)
            dve.wait_ge(srow_ps, 1)
            dve.wait_ge(sread_ps, 1)
            V.tensor_copy(row_b.rearrange("p r n -> p (r n)"), bank[5][:, 0:128])
            link(V.tensor_copy(qk_, bank[5][:, 128:192]))
            read = bank[3][:, 0:128].rearrange("p (i r) -> p r i", r=2)
            link(V.tensor_tensor(sk, read[:, 1, :], row_b[:, 1, :], ALU.mult))
            V.tensor_tensor(sq_, read[:, 0, :], row_b[:, 1, :], ALU.mult).then_inc(su_done, 1)
            hb = lambda v: v.rearrange("p (h b) -> p h b", b=NS)
            link(V.tensor_tensor(hb(u_s), qkv[:, 2 * H:3 * H, NPR:T], hb(sk), ALU.subtract))
            link(V.tensor_tensor(u_s, u_s, row_b[:, 0, :], ALU.mult))
            V.tensor_copy(hb(sk), qkv[:, H:2 * H, NPR:T])
            link(V.tensor_tensor(qk_, qk_, u_s, ALU.mult))
            V.tensor_tensor(oT[:, :, NPR:T], hb(sq_), hb(qk_), ALU.add).then_inc(sou, 1)
            for l in range(LEVELS):
                if l == 3:
                    dve.wait_ge(turned_sb, 2 * NG)
                    for i in range(NI):
                        ins = V.tensor_scalar(ktok[:, i, :], ktok[:, i, :], to_end[:, i // H, i % H:i % H + 1], None, ALU.mult)
                    ins.then_inc(kdec_done, 1)
                for g in range(NG):
                    gi = slice(GRP * g, GRP * (g + 1))
                    dve.wait_ge(y_ps, NG * l + g + 1)
                    if l == 0 and g == 0:
                        dve.wait_ge(q_dec_done, 1)
                    V.tensor_tensor(Y[:, gi, :], bank[g][:, :].rearrange("p (i n) -> p i n", i=GRP),
                                    lmask[:, l:l + 1, :].to_broadcast([P, GRP, P]), ALU.mult).then_inc(y_sb, 1)
                for g in range(NG):
                    gi = slice(GRP * g, GRP * (g + 1))
                    fl = lambda v: v[:, gi, :].rearrange("p i n -> p (i n)")
                    if l == 0:
                        idw = ident.unsqueeze(1).to_broadcast([P, GRP, P])
                        dve.wait_ge(y_sb, g + 1)
                        V.tensor_tensor(X[:, gi, :], idw, Y[:, gi, :], ALU.subtract).then_inc(x_sb, 1)
                        dve.wait_ge(z_ps, g + 1)
                        V.tensor_tensor(Z[:, gi, :], idw, bank[6 + g % 2][:, :].rearrange("p (i n) -> p i n", i=GRP),
                                        ALU.subtract).then_inc(z_sb, 1)
                    else:
                        if l < LEVELS - 1:
                            dve.wait_ge(x_ps, NG * (l - 1) + g + 1)
                            V.tensor_tensor(fl(X), fl(X), bank[4 + g % 2][:, :], ALU.subtract).then_inc(x_sb, 1)
                        dve.wait_ge(z_ps, NG * l + g + 1)
                        V.tensor_tensor(fl(Z), fl(Z), bank[6 + g % 2][:, :], ALU.subtract).then_inc(z_sb, 1)
            for c in range(CH):
                if c == 1:
                    for g in range(2):
                        dve.wait_ge(ks_ps, g + 1)
                        for j in range(GRP):
                            h = GRP * g + j
                            ins = V.scalar_tensor_tensor(out=rhs_w[:, h, :], in0=bank[g][:, P * j:P * (j + 1)],
                                                         scalar=neg_ecum[:, 1, h:h + 1], in1=vtok[:, H + h, :],
                                                         op0=ALU.mult, op1=ALU.add)
                        ins.then_inc(w_sb, 1)
                for g in range(2):
                    dve.wait_ge(u_ps, 2 * c + g + 1)
                    if c == 1:
                        dve.wait_ge(o_ps, g + 1)
                    for j in range(GRP):
                        h = GRP * g + j
                        ins = V.tensor_scalar(u_tok[:, h, :], bank[2 + g][:, P * j:P * (j + 1)],
                                              beta[:, c, h:h + 1], None, ALU.mult)
                    ins.then_inc(u_sb, 1)
                for g in range(2):
                    dve.wait_ge(s_ps, 2 * c + g + 1)
                    if c == 0:
                        V.tensor_copy(S_new[:, GRP * g:GRP * (g + 1), :].rearrange("p i n -> p (i n)"),
                                      bank[4 + g][:, :]).then_inc(s_sb, 1)
                    else:
                        dve.wait_ge(s_sb, 2)
                        for j in range(GRP):
                            h = GRP * g + j
                            ins = V.scalar_tensor_tensor(out=S_fin[:, h, :], in0=S_new[:, h, :],
                                                         scalar=e_end[:, 1, h:h + 1], in1=bank[4 + g][:, P * j:P * (j + 1)],
                                                         op0=ALU.mult, op1=ALU.add)
                        ins.then_inc(s_sb, 1)
            dve.wait_ge(st_ps, 1)
            V.tensor_copy(kv_rows.rearrange("p r n -> p (r n)"), bank[0][0:64, 0:2 * P]).then_inc(st_sb, 1)
            for h in range(H):
                if h == 0:
                    dve.wait_ge(o_sb, 4)
                    dve.wait_ge(sou, 1)
                V.tensor_tensor(osq[:, h, :], oT[:, h, :], oT[:, h, :], ALU.mult).then_inc(osq_done, 1)
            for i in range(16):
                dve.wait_ge(sout_ps, i + 1)
                dve.wait_ge(sdecayed, i // 2 + 1)
                s = states[:, 4 * i:4 * i + 4, :].rearrange("p i n -> p (i n)")
                V.tensor_tensor(s, s, bank[2 + i % 2][:, :], ALU.add).then_inc(snew, 1)
            for h in range(H):
                dve.wait_ge(oroot, h + 1)
                link(V.reciprocal(osq[:, h, :], osq[:, h, :]))
                link(V.scalar_tensor_tensor(out=oT[:, h, :], in0=oT[:, h, :], scalar=p_("o_gain"), in1=osq[:, h, :],
                                            op0=ALU.mult, op1=ALU.mult))
                V.tensor_tensor(oT[:, h, :], oT[:, h, :], zT[:, h, :], ALU.mult).then_inc(o_normed, 1)

            def add_out(done, added):
                for d in range(KT):
                    dve.wait_ge(done, d + 1)
                    V.tensor_tensor(xT[:, d, :], xT[:, d, :], bank[4 + d % 4][:, 0:T], ALU.add).then_inc(added, 1)
                dve.wait_ge(added, KT)

            add_out(outp, out_added)
            norm(1)

            def gated(e, up_s, silu_s, act_s):
                for f in range(FT):
                    dve.wait_ge(silu_s, e * FT + f + 1)
                    dve.wait_ge(up_s, e * FT + f + 1)
                    V.tensor_tensor(aT[:, f, :], sil[:, f % 2, :], bank[2 * (f % 2) + 1][:, 0:T], ALU.mult)\
                        .then_inc(act_s, 1)

            gated(0, f_up, f_silu, f_act)
            for d in range(KT):
                dve.wait_ge(f_down, d + 1)
                V.tensor_tensor(xT[:, d, :], xT[:, d, :], bank[4 + d % 3][:, 0:T], ALU.add).then_inc(f_added, 1)
            dve.wait_ge(f_added, KT)
            norm(2)
            dve.wait_ge(rope_loaded, 16)
            for c in range(12):
                a = aq[0:ROT, c, :]
                dve.wait_ge(rot_ps, c + 1)
                if c >= 1:
                    dve.wait_ge(roped, c)
                V.tensor_tensor(rot_t[0:ROT, :], bank[4 + c % 2][0:ROT, 0:T], sinT, ALU.mult)
                link(V.tensor_tensor(a, a, cosT, ALU.mult))
                V.tensor_tensor(a, a, rot_t[0:ROT, :], ALU.add).then_inc(roped, 1)
            dve.wait_ge(roped, 12)

            def p_max(h):
                dve.wait_ge(sc_ps, h + 1)
                if h >= 2:
                    dve.wait_ge(pT_ps, h - 1)
                i, m = h % 2, 2 * (h % 2)
                b = bank[h % 2]
                V.scalar_tensor_tensor(out=pr_s[:, i, 0:P], in0=b[:, 0:P], scalar=SCALE, in1=causal, op0=ALU.mult, op1=ALU.add)
                V.tensor_scalar(pr_s[:, i, P:2 * P], b[:, P:2 * P], SCALE, None, ALU.mult)
                link(V.scalar_tensor_tensor(out=pr_s[:, i, 2 * P:3 * P], in0=b[:, 2 * P:3 * P], scalar=SCALE, in1=causal,
                                            op0=ALU.mult, op1=ALU.add))
                V.tensor_reduce(pmax[:, m:m + 1], pr_s[:, i, 0:P], AX, ALU.max)
                link(V.tensor_reduce(pmax[:, m + 1:m + 2], pr_s[:, i, P:3 * P], AX, ALU.max))
                V.tensor_scalar(pmax[:, m:m + 2], pmax[:, m:m + 2], -1.0, None, ALU.mult).then_inc(sc_max, 1)

            def p_scale(h):
                i, m = h % 2, 2 * (h % 2)
                dve.wait_ge(sc_exp, h + 1)
                link(V.reciprocal(prec[:, m:m + 2], psums[:, m:m + 2]))
                V.tensor_scalar(pr_s[:, i, 0:P], pr_s[:, i, 0:P], prec[:, m:m + 1], None, ALU.mult)
                V.tensor_scalar(pr_s[:, i, P:3 * P], pr_s[:, i, P:3 * P], prec[:, m + 1:m + 2], None, ALU.mult)\
                    .then_inc(p_sb, 1)

            for i in range(H + 1):
                if i == 2:
                    dve.wait_ge(aproj, 16)
                    link(V.memset(hflat, 0.0))
                    V.tensor_copy(q_own.rearrange("p b k r -> p k r b"),
                                  aq[:, 0:H, NPR:T].rearrange("p (k r) b -> p k r b", r=2)).then_inc(q_wide_set, 1)
                    V.tensor_tensor(prodn.rearrange("p (b k r) -> p k r b", k=KVH, r=2),
                                    aq[:, 0:H, NPR:T].rearrange("p (k r) b -> p k r b", r=2),
                                    aq[:, 8:12, NPR:T].unsqueeze(2).to_broadcast([P, KVH, 2, NS]), ALU.mult)\
                        .then_inc(prod_done, 1)
                if i < H:
                    p_max(i)
                if i >= 1:
                    p_scale(i - 1)
            dve.wait_ge(lnew_ps, 1)
            V.tensor_copy(l_new, bank[6][0:64, 0:1])
            V.tensor_reduce(kv_of_head, ident[0:8, 0:8].rearrange("p (k r) -> p k r", r=2), AX, ALU.add)
            for q in range(4):
                dve.wait_ge(k_read, 2 * NS - 1 + q // 2)
                t = bank[q][0:64, :].rearrange("p (n t) -> p n t", n=2)
                V.tensor_reduce(st_max[:, 2 * q:2 * q + 2], t, AX, ALU.max)
                ins = V.tensor_reduce(st_sum[:, 2 * q:2 * q + 2], t, AX, ALU.add)
            link(ins)
            other, own = st_sum.unsqueeze(1).to_broadcast([64, 8, 8]), st_sum.unsqueeze(2).to_broadcast([64, 8, 8])
            V.tensor_tensor(cmp_b, other, own, ALU.is_gt)
            link(V.tensor_tensor(eq_b, other, own, ALU.is_equal))
            link(V.tensor_tensor(eq_b, eq_b, before[0:64], ALU.mult))
            link(V.tensor_tensor(cmp_b, cmp_b, eq_b, ALU.add))
            link(V.tensor_reduce(pen, cmp_b, AX, ALU.add))
            link(V.tensor_scalar(pen, pen, float(TOPK) - 0.5, -BIG, ALU.is_gt, ALU.mult))
            link(V.tensor_tensor(st_max, st_max, pen, ALU.add))
            link(V.tensor_reduce(m_neg, st_max, AX, ALU.max))
            link(V.tensor_scalar(m_neg, m_neg, l_new, -SCALE, ALU.max, ALU.mult))
            V.tensor_scalar(biases, pen, m_neg, None, ALU.add).then_inc(bias_done, 1)
            dve.wait_ge(pexp, 1)
            link(V.tensor_reduce(r_den, sums, AX, ALU.add))
            link(V.tensor_tensor(r_den, r_den, p_new, ALU.add))
            link(V.reciprocal(r_den, r_den))
            link(V.tensor_scalar(rd_diag, ident[0:64, 0:64], r_den, None, ALU.mult))
            V.tensor_scalar(p_diag, rd_diag, p_new, None, ALU.mult).then_inc(diag_done, 1)
            dve.wait_ge(probT_ps, 3)
            V.tensor_tensor(o_new.rearrange("p b (k r) -> p k r b", r=2),
                            bank[7][:, 0:64].rearrange("p (b k r) -> p k r b", b=NS, r=2),
                            aq[:, 12:16, NPR:T].unsqueeze(2).to_broadcast([P, KVH, 2, NS]), ALU.mult)
            dve.wait_ge(po_ps, H)
            for b in range(NS):
                dve.wait_ge(v_read, 2 * (b + 1))
                if b >= 1:
                    dve.wait_ge(o8_done, b)
                link(V.tensor_tensor(o_wide, bank[b % 4][0:8, :].rearrange("p (k d) -> p k d", k=KVH),
                                     kv_of_head.unsqueeze(2).to_broadcast([8, KVH, DK]), ALU.mult))
                V.tensor_reduce(o8[:, b, :], o_wide.rearrange("p k d -> p d k"), AX, ALU.add).then_inc(o8_done, 1)
            dve.wait_ge(o8_turned, NS)
            V.tensor_tensor(o_att[:, :, NPR:T], bank[6][:, 0:64].rearrange("p (b h) -> p h b", h=H),
                            o_new.rearrange("p b h -> p h b"), ALU.add).then_inc(od_done, 1)
            add_out(aout, aout_added)
            norm(3)
            dve.wait_ge(r_ps, 1)
            V.tensor_copy(rl[:, 0:2, :], bank[0][:, 0:16].rearrange("p (i e) -> p i e", i=2))
            link(V.tensor_copy(rl[0:NS, 2, :], bank[0][0:NS, 16:24]))
            r4 = lambda v: v.rearrange("p (t i) j -> p t i j", t=3)
            other, own = rl.unsqueeze(2).to_broadcast([P, 3, NE, NE]), rl.unsqueeze(3).to_broadcast([P, 3, NE, NE])
            V.tensor_tensor(r4(rcmp), other, own, ALU.is_gt)
            link(V.tensor_tensor(r4(req), other, own, ALU.is_equal))
            link(V.tensor_tensor(r4(req), r4(req), before.unsqueeze(1).to_broadcast([P, 3, NE, NE]), ALU.mult))
            link(V.tensor_tensor(rcmp, rcmp, req, ALU.add))
            link(V.tensor_reduce(rrank.rearrange("p t e -> p (t e)"), rcmp, AX, ALU.add))
            V.tensor_scalar(rrank, rrank, 1.5, None, ALU.is_lt)
            link(V.tensor_reduce(rmax, rl, AX, ALU.max))
            V.tensor_tensor(rgate[:, :, 0:NE], rl, rmax.unsqueeze(2).to_broadcast([P, 3, NE]), ALU.subtract).then_inc(r_arg, 1)
            dve.wait_ge(r_exp, 1)
            rg = rgate[:, :, 0:NE]
            link(V.tensor_tensor(rg, rg, rrank, ALU.mult))
            link(V.tensor_reduce(rmax, rg, AX, ALU.add))
            link(V.reciprocal(rmax, rmax))
            V.tensor_tensor(rg, rg, rmax.unsqueeze(2).to_broadcast([P, 3, NE]), ALU.mult).then_inc(r_gate, 1)
            dve.wait_ge(pos_ps, 1)
            link(V.memset(rpos, -1.0))
            V.tensor_tensor(rpos[:, 0:2, 0:NE], bank[0][:, 32:32 + 2 * NE].rearrange("p (i e) -> p i e", i=2), rrank[:, 0:2, :],
                            ALU.mult)
            V.tensor_tensor(rpos[0:NS, 2, 0:NE], bank[0][0:NS, 32 + 2 * NE:32 + 3 * NE], rrank[0:NS, 2, :], ALU.mult)
            link(V.tensor_copy(counts[0:1, :], bank[0][0:1, 64:64 + NE]))
            V.tensor_scalar(rpos[:, :, 0:NE], rpos[:, :, 0:NE], -1.0, None, ALU.add)
            link(V.tensor_reduce(over[0:1, :], counts[0:1, :], AX, ALU.max))
            V.tensor_scalar(dense_flag[:, :], over[0:1, :], CAP + 0.5, None, ALU.is_gt).then_inc(over_set, 1)
            dve.wait_ge(over_set, 1)
            dve.wait_ge(stored, 16 * 5)

            def pick_tokens(e):
                for i, (t0, n) in enumerate(TOK_TILES):
                    at_e = e if isinstance(e, slice) else bass.ds(e, 1)
                    V.tensor_scalar(pick_g[0:n, i, :], c_("slot_no")[0:n], rpos[0:n, i, at_e], rgate[0:n, i, at_e],
                                    ALU.is_equal, ALU.mult)
                    last = V.tensor_scalar(pick[0:n, i, :], c_("slot_no")[0:n], rpos[0:n, i, at_e], None, ALU.is_equal)
                last.then_inc(picked, 1)

            def add_combined(e, d):
                dve.wait_ge(comb, e * KT + d + 1)
                V.tensor_tensor(xT[:, d, :], xT[:, d, :], bank[6 + d % 2][:, 0:T], ALU.add).then_inc(comb_added, 1)

            def sparse_expert(e, first):
                for f in range(FT):
                    if not first and 8 <= f < 8 + KT:
                        dve.wait_ge(comb, e * KT + (f - 8 + 1 - KT))
                        if f == 8:
                            dve.wait_ge(comb_added, (e - 1) * KT)
                        V.tensor_tensor(xT[:, f - 8, :], xT[:, f - 8, :], bank[6 + f % 2][:, 0:T], ALU.add)\
                            .then_inc(comb_added, 1)
                    if f == 22:
                        dve.wait_ge(spread_ps, e + 1)
                        dve.wait_ge(gathered, 2 * e + 2)
                        pick_tokens(e + 1)
                    dve.wait_ge(m_silu, e * FT + f + 1)
                    dve.wait_ge(m_up, e * FT + f + 1)
                    V.tensor_tensor(s_act[:, f, :], s_sil[:, f % 2, :], bank[2 * (f % 2) + 1][:, 0:CAP], ALU.mult)\
                        .then_inc(m_act, 1)

            def dense_expert(e):
                gated(e, m_up, m_silu, m_act)
                for d in range(KT):
                    dve.wait_ge(m_down, e * KT + d + 1)
                    g = gate_b[:, e, :] if isinstance(e, int) else gate_b[:, bass.ds(e, 1), :].rearrange("p a t -> p (a t)")
                    V.tensor_tensor(weighted[:, d % 2, :], bank[4 + d % 3][:, 0:T], g, ALU.mult).then_inc(m_added, 1)
                    dve.wait_ge(m_added, e * KT + d + 1)
                    last = V.tensor_tensor(xT[:, d, :], xT[:, d, :], weighted[:, d % 2, :], ALU.add)
                last.then_inc(x_sum, 1)
                dve.wait_ge(x_sum, e + 1)

            dense = dve.value_load(dense_flag[0:1, 0:1], min_val=0, max_val=1)
            with dve.If(dense == 0):
                pick_tokens(0)
                sparse_expert(0, True)
                with dve.Fori(1, NE) as e:
                    sparse_expert(e, False)
                for d in range(KT):
                    add_combined(NE - 1, d)
                dve.wait_ge(comb_added, NE * KT)
            with dve.Else():
                dve.wait_ge(r_turned, 1)
                V.tensor_copy(gT, bank[1][0:NE, 0:T]).then_inc(r_diag, 1)
                dve.wait_ge(r_diag, 1)
                V.tensor_tensor(gate_d[0:NE], gT.unsqueeze(1).to_broadcast([NE, NE, T]),
                                ident[0:NE, 0:NE].unsqueeze(2).to_broadcast([NE, NE, T]), ALU.mult).then_inc(r_diag, 1)
                dve.wait_ge(gb_sb, NE)
                dense_expert(0)
                with dve.Fori(1, NE) as e:
                    dense_expert(e)
            norm(4)


def _constants():
    r = np.arange(P)
    c = {
        "ident": np.eye(P), "ones": np.ones((P, P)), "upper": r[:, None] <= r[None, :],
        "causal": np.where(r[None, :] <= r[:, None], 0.0, -BIG),
        "before": np.tile((np.arange(8)[None, :] < np.arange(8)[:, None]).reshape(1, 64), (P, 1)),
        "eps": np.tile(np.array([[EPS, EPS * DK]]), (P, 1)), "slot_no": np.tile(np.arange(CAP)[None], (P, 1)),
    }
    cst = np.concatenate([np.asarray(c[n], np.float32) for n in CST], axis=1)
    masks = []
    for level in range(LEVELS):
        s = 1 << level
        same = (r[:, None] // (2 * s)) == (r[None, :] // (2 * s))
        masks.append(same & ((r[:, None] // s) % 2 == 1) & ((r[None, :] // s) % 2 == 0))
    lmask = np.stack(masks, axis=1).reshape(P, LEVELS * P).astype(np.float32)
    half = ROT // 2
    rot = np.zeros((P, ROT), np.float32)
    rot[np.arange(half) + half, np.arange(half)] = -1.0
    rot[np.arange(half), np.arange(half) + half] = 1.0
    inv = np.power(np.float32(500000.0), -np.arange(half, dtype=np.float32) * np.float32(2.0 / ROT))
    pos = np.concatenate([np.arange(NPR), np.full(NS, POS0)]).astype(np.float32)
    ang = np.tile((pos[None, :] * inv[:, None]).astype(np.float32), (2, 1))
    rope = np.zeros((P, ROPE_N), np.float32)
    rope[:, :ROT] = rot
    rope[:ROT, ROT:ROT + T] = np.cos(ang)
    rope[:ROT, ROT + T:] = np.sin(ang)
    return cst, lmask, rope


def kernel(**inputs):
    import numpy as _np
    import concourse.bacc as _bacc
    from concourse import mybir as _mybir
    from concourse.bass_utils import run_bass_kernel_spmd as _run

    a = {k: _np.asarray(v) for k, v in inputs.items()}
    cont = _np.ascontiguousarray

    def columns(w, per_chunk):
        k, n = w.shape
        t = w.reshape(k // P, P, n // (P * per_chunk), per_chunk, P).transpose(2, 1, 3, 0, 4)
        return cont(t.reshape(t.shape[0], P, -1))

    def gate_up(g, u):
        e = g.shape[0]
        parts = [w.reshape(e, KT, P, FT // 2, 2, P).transpose(0, 3, 2, 4, 1, 5) for w in (g, u)]
        return cont(_np.stack(parts, axis=4)).reshape(e * (FT // 2), P, SLOT)

    def down(w):
        e = w.shape[0]
        return cont(w.reshape(e, FT, P, KT, P).transpose(0, 3, 2, 1, 4)).reshape(e * KT, P, FT * P)

    x = _np.concatenate([a["x_prompt"][0], a["x_sample"][:, 0]], axis=0)
    cst, lmask, rope = _constants()
    gains = _np.stack([a["norm_mix"][0], a["norm_ffn"][0], a["norm_mix"][1], a["norm_ffn"][1], a["norm_final"]])
    w_in = a["gdn_w_in"][0]
    n_wide = (QKV + H) * P
    prm = {
        "gain": gains.reshape(5, KT, P).transpose(2, 0, 1), "o_gain": a["gdn_o_norm"][0][:, None],
        "conv_w": a["gdn_conv_w"][0].reshape(CONV_W, QKV, P).transpose(2, 1, 0),
        "a_log": _np.tile(a["gdn_a_log"][0][None], (P, 1)), "dt_bias": _np.tile(a["gdn_dt_bias"][0][None], (P, 1)),
        "router": a["moe_router"][0].reshape(KT, P, NE).transpose(1, 0, 2),
        "w_small": w_in[:, n_wide:].reshape(KT, P, 2 * H).transpose(1, 0, 2),
    }
    given = {
        "x": x.reshape(T, KT, P).transpose(2, 1, 0),
        "cst": cst, "lmask": lmask, "rope": rope,
        "prm": _np.concatenate([prm[n].reshape(P, -1) for n in PRM], axis=1),
        "conv": a["state_conv"][0].reshape(NS, CONV_W - 1, QKV, P).transpose(3, 2, 1, 0),
        "table": a["page_table"].reshape(1, -1),
        "gdn_in": columns(w_in[:, :n_wide], 4),
        "state": a["state_delta"][0].transpose(2, 1, 0, 3).reshape(DK, 2, SLOT).transpose(1, 0, 2),
        "gdn_out": columns(a["gdn_w_out"][0], 4),
        "ffn_gu": gate_up(a["ffn_w_gate"], a["ffn_w_up"]), "ffn_down": down(a["ffn_w_down"]),
        "att_in": columns(a["att_w_in"][0], 4),
        "k_pages": a["cache_k"][0].transpose(0, 3, 2, 1).reshape(-1, P, KVH * PAGE),
        "v_pages": a["cache_v"][0].reshape(-1, PAGE, KVH * DK),
        "att_out": columns(a["att_w_out"][0], 4),
        "moe_gu": gate_up(a["moe_w_gate"][0], a["moe_w_up"][0]), "moe_down": down(a["moe_w_down"][0]),
    }
    outs = {"y": (P, KT, T), "convp": (P, QKV, CONV_W - 1), "convs": (P, QKV, CONV_W - 1, NS),
            "deltap": (P, H, DK), "deltas": (P, H * NS, DK), "kv": (P, 2 * KVH, T)}

    nc = _bacc.Bacc("TRN2", target_bir_lowering=False, num_devices=1)
    arrays, args = {}, []
    for name, v in given.items():
        arrays[f"in_{name}"] = cont(v)
        args.append(nc.dram_tensor(f"in_{name}", v.shape, _mybir.dt.from_np(v.dtype), kind="ExternalInput").ap())
    for name, shape in outs.items():
        args.append(nc.dram_tensor(f"out_{name}", shape, F32, kind="ExternalOutput").ap())
    program(nc, *args)
    r = _run(nc, [arrays], core_ids=[0]).results[0]
    y = r["out_y"].transpose(2, 1, 0).reshape(T, D)
    kv = r["out_kv"].transpose(2, 1, 0)
    convs = r["out_convs"].transpose(3, 2, 1, 0).reshape(1, NS, CONV_W - 1, QKV * P)
    deltas = r["out_deltas"].reshape(DK, H, NS, DK).transpose(2, 1, 0, 3)[None]
    return (y[None, :NPR], y[NPR:, None],
            r["out_convp"].transpose(2, 1, 0).reshape(1, 1, CONV_W - 1, QKV * P),
            r["out_deltap"].transpose(1, 0, 2)[None, None],
            kv[None, None, :NPR, :KVH], kv[None, None, :NPR, KVH:],
            convs, deltas, kv[None, NPR:, None, :KVH], kv[None, NPR:, None, KVH:])
```

```python
from contextlib import ExitStack

import numpy as np

import concourse.bass as bass
from concourse import mybir

F32 = mybir.dt.float32
F32R = mybir.dt.float32r
I32 = mybir.dt.int32
ALU = mybir.AluOpType
ACT = mybir.ActivationFunctionType
AX = mybir.AxisListType.X

P = 128
D = 1024
KT = D // P
NPR = 256
NS = 8
T = NPR + NS
TOK_TILES = ((0, P), (P, P), (NPR, NS))
H = 8
KVH = 4
DK = 128
CONV_W = 4
QKV = 3 * H
CH = 2
NI = CH * H
GRP = 4
NG = NI // GRP
LEVELS = 7
FT = 3584 // P
NE = 8
N_PAGES = 16
PAGE = 128
PPC = 8
BLOCKS = N_PAGES * PAGE // 256
TOPK = 3
ROT = 32
POS0 = N_PAGES * PAGE
SCALE = DK ** -0.5
EPS = 1e-6
BIG = 1e30

SLOTS = 8
SLOT = 4096
C_STATE = 0
C_OUT = C_STATE + 2
C_AIN = C_OUT + 2 + 4
C_K = C_AIN + 4
C_V = C_K + 2 * NS
C_AOUT = C_V + 2 * NS
CHUNKS = C_AOUT + 2
CAP = 128
ROUNDS = -(-T // CAP)
N = 512
PIECE = 2048
GROUPS = FT * P // N
UP_PIECES = 4 * GROUPS
F_PIECE = PIECE // D
PIECES = UP_PIECES + FT // F_PIECE
RAW = 7
F_RAW = 6
F_TILES = PIECE // P
F_ACTS = 4
SPLIT = 3
IN_PIECES = (QKV + H) * KT * P // PIECE


def earlier_fills(slot, dense):
    n = len(range(slot, IN_PIECES, RAW))
    return n if dense else n + (PIECES // F_RAW if slot < F_RAW else 0)


assert PIECES % RAW == 0 and PIECES % SPLIT == 0 and C_AIN % SLOTS == 0
STORES = 6


def fills_per_chunk(n):
    if C_OUT + 2 <= n < C_AIN:
        return 0
    return 16 * (PPC if C_K <= n < C_AOUT else 1)


def full_value(n):
    return sum(fills_per_chunk(m) for m in range(n % SLOTS, n + 1, SLOTS))


CST = {}
_at = 0
for _name, _n in (("ident", P), ("ones", P), ("upper", P), ("causal", P), ("before", 64), ("eps", 2),
                  ("slot_no", CAP), ("sel", 31), ("sel_q", 31), ("eps_qk", 1)):
    CST[_name] = (_at, _n)
    _at += _n
CST_N = _at
PRM = {}
_at = 0
for _name, _n in (("gain", 5 * KT), ("o_gain", 1), ("conv_w", QKV * CONV_W), ("a_log", H), ("dt_bias", H),
                  ("router", KT * NE), ("w_small", KT * 2 * H)):
    PRM[_name] = (_at, _n)
    _at += _n
PRM_N = _at
ROPE_N = ROT + 2 * T


def program(nc, x_in, cst_in, lmask_in, rope_in, prm_in, conv_in, table_in, gdn_in_w, state_in, gdn_out_w,
            ffn_w, att_in_w, k_pages, v_pages, att_out_w, moe_w,
            y_out, convp_out, convs_out, deltap_out, deltas_out, kv_out):
    with ExitStack() as ctx:
        def sb(name, shape, dt=F32):
            return ctx.enter_context(nc.sbuf_tensor(name, shape, dt))

        def sem(name):
            return ctx.enter_context(nc.semaphore(name))

        xT = sb("xT", [P, KT, T])
        cst = sb("cst", [P, CST_N])
        prm = sb("prm", [P, PRM_N])
        conv_prev = sb("conv_prev", [P, QKV, CONV_W - 1, NS])
        raw = sb("raw", [P, 2, CONV_W - 1 + T])
        conv_last = sb("conv_last", [P, QKV, CONV_W - 1])
        conv_new = sb("conv_new", [P, QKV, NS])
        small = sb("small", [P, 768])
        table = sb("table", [1, NS * N_PAGES], I32)
        more = sb("more", [1, 1], I32)
        with nc.sbuf_tensor("hT", [P, KT, T], F32) as hT, nc.sbuf_tensor("ring", [P, SLOTS, SLOT], F32) as ring, \
                nc.sbuf_tensor("scr", [P, 48 * T], F32) as scr:
            pass
        fh_lo = sb("fh_lo", [P, KT, T], F32R)
        raw_w = sb("raw_w", [P, RAW, PIECE])
        w_hi = sb("w_hi", [P, SPLIT, PIECE], F32R)
        w_lo = sb("w_lo", [P, SPLIT, PIECE], F32R)
        with nc.sbuf_tensor("f_hi", [P, FT, T], F32R) as f_hi, nc.sbuf_tensor("f_lo", [P, FT, T], F32R) as f_lo, \
                nc.sbuf_tensor("fh_hi", [P, KT, T], F32R) as fh_hi:
            pass
        gh_hi = f_hi[:, 0:KT, :]
        f_tmp = raw_w[:, F_RAW, 0:F_ACTS * T].rearrange("p (i t) -> p i t", t=T)
        aT_hi = sb("aT_hi", [P, FT, CAP], F32R)
        aT_lo = sb("aT_lo", [P, FT, CAP], F32R)
        xe_hi = sb("xe_hi", [P, KT, CAP], F32R)
        xe_lo = sb("xe_lo", [P, KT, CAP], F32R)
        moe_scr = sb("moe_scr", [P, 7176])
        bank = [ctx.enter_context(nc.psum_tensor(f"bank{i}", [P, 512], F32))[:, :] for i in range(8)]

        def c_(name):
            a, n = CST[name]
            return cst[:, a:a + n]

        def p_(name):
            a, n = PRM[name]
            return prm[:, a:a + n]

        ident, ones, upper, causal = c_("ident"), c_("ones"), c_("upper"), c_("causal")
        before = c_("before").rearrange("p (i j) -> p i j", i=8)
        eps, eps_q = cst[:, CST["eps"][0]:CST["eps"][0] + 1], cst[:, CST["eps"][0] + 1:CST["eps"][0] + 2]
        gain = p_("gain").rearrange("p (l k) -> p l k", k=KT)
        conv_w = p_("conv_w").rearrange("p (c j) -> p c j", j=CONV_W)
        router = p_("router").rearrange("p (k e) -> p k e", e=NE)
        w_small = p_("w_small").rearrange("p (k e) -> p k e", e=2 * H)
        rms = raw[:, 0, CONV_W - 1:]

        def carve(base, at, *dims):
            n = int(np.prod(dims))
            v = base[:, at:at + n]
            if len(dims) == 2:
                v = v.rearrange("p (a b) -> p a b", b=dims[1])
            if len(dims) == 3:
                v = v.rearrange("p (a b c) -> p a b c", b=dims[1], c=dims[2])
            return v

        qkv = carve(scr, 0, QKV, T)
        zT = carve(scr, QKV * T, H, T)
        nrm = carve(scr, (QKV + H) * T, 2 * H, T)
        oT = carve(scr, (QKV + H) * T, H, T)
        osq = carve(scr, (QKV + 2 * H) * T, H, T)
        qk_rows = nrm[0:2 * H, 15, 0:NPR]
        s_sq, s_rt = nrm[:, 2, 0:2 * H * NS], nrm[:, 3, 0:2 * H * NS]
        small_T = zT[0:2 * H, H - 1, :]
        o_rows = qkv[0:H, 0, :]
        core = ring[:, 4:8, :].rearrange("p s n -> p (s n)")
        ktok = carve(core, 0, NI, P)
        vtok = carve(core, 2048, NI, P)
        coefT = carve(core, 4096, NI, P)
        attT = carve(core, 6144, NI, P)
        X = carve(core, 8192, NI, P)
        Z = carve(core, 10240, NI, P)
        Y = carve(core, 12288, NI, P)
        lmask = carve(core, 14336, LEVELS, P)
        decT = carve(core, 15232, 2, GRP * P)
        rhs_w = X[:, 0:8, :]
        u_tok = X[:, 8:16, :]
        S_new = Y[:, 0:8, :]
        S_fin = Y[:, 8:16, :]
        wide = decT[0:64]
        kv_rows = carve(core, 14336, 2, P)[0:64]
        states = ring[:, 0:2, :].rearrange("p s n -> p (s n)").rearrange("p (i v) -> p i v", v=DK)
        sm_at = [0]

        def sm(*dims):
            v = carve(small, sm_at[0], *dims)
            sm_at[0] += int(np.prod(dims))
            return v

        ba = sm(3, 2 * H)
        beta = sm(3, H)
        gdec = sm(3, H)
        t_abs = sm(3, H)
        t_exp = sm(3, H)
        e_alog = sm(H)
        cum = sm(CH, H)
        neg_ecum = sm(CH, H)
        to_end = sm(CH, H)
        e_end = sm(CH, H)
        ge_s = sm(H)
        diag8 = sm(2, 64)
        row_b = sm(2, 64)
        sk = sm(64)
        sq_ = sm(64)
        qk_ = sm(64)
        u_s = sm(64)
        aq = carve(scr, 0, 16, T)
        rope = scr[:, 16 * T:16 * T + ROPE_N]
        rot_p = rope[:, 0:ROT]
        cosT, sinT = rope[0:ROT, ROT:ROT + T], rope[0:ROT, ROT + T:ROT + 2 * T]
        at = 16 * T + ROPE_N
        rot_t = carve(scr, at, T); at += T
        v_tok = carve(scr, at, CH * KVH, P); at += CH * KVH * P
        prob = scr[0:64, at:at + N_PAGES * PAGE]; at += N_PAGES * PAGE
        o_att = carve(scr, at, H, T); at += H * T
        pr_s = carve(scr, at, 2, 384); at += 768
        pr_T = carve(scr, at, 2, 384); at += 768
        a_small = scr[:, at:48 * T]
        pmax, psums, prec = a_small[:, 16:20], a_small[:, 20:24], a_small[:, 24:28]
        hflat = hT[:, :, :].rearrange("p k t -> p (k t)")
        q_wide = hflat[:, 0:NS * KVH * 64].rearrange("p (i r) -> p i r", r=64)
        q_own = hflat.rearrange("p (b k r) -> p b k r", b=NS, k=KVH)[:, :, :, 0:2]
        prodn = hflat[:, NS * KVH * 64:NS * KVH * 64 + 64]
        prob_T = hflat[:, 0:N_PAGES * 64].rearrange("p (g r) -> p g r", r=64)
        st = [32]

        def stat(rows, *dims):
            v = carve(a_small, st[0], *dims)[0:rows]
            st[0] += int(np.prod(dims))
            return v

        st_max, st_sum, pen, biases, sums = (stat(64, BLOCKS) for _ in range(5))
        cmp_b, eq_b = stat(64, BLOCKS, BLOCKS), stat(64, BLOCKS, BLOCKS)
        m_neg, l_new, p_new, r_den = (stat(64, 1) for _ in range(4))
        rd_diag, p_diag = stat(64, 64), stat(64, 64)
        o_new = stat(P, NS, H)
        kv_of_head = stat(8, KVH)
        assert st[0] <= 48 * T - at
        o8 = carve(scr, at - 1536, NS, DK)[0:8]
        o_wide = carve(scr, at - 512, KVH, DK)[0:8]
        rl = sm(3, NE)
        sm_at[0] = 0
        rpos = sm(3, ROUNDS * NE + 1)
        rgate = sm(3, ROUNDS * NE + 1)
        rrank = sm(3, NE)
        counts = sm(NE)
        over = sm(1)
        at = 0
        htok = carve(moe_scr, at, 3, D); at += 3 * D
        pick = carve(moe_scr, at, 3, CAP); at += 3 * CAP
        pick_g = carve(moe_scr, at, 3, CAP); at += 3 * CAP
        spread = moe_scr[0:CAP, at:at + T]; at += T
        s_sil = carve(moe_scr, at, 2, N); at += 2 * N
        s_act = carve(moe_scr, at, 2, N); at += 2 * N
        ye = moe_scr[0:CAP, at:at + D]; at += D
        rcmp = carve(scr, 0, 3 * NE, NE)
        req = carve(scr, 192, 3 * NE, NE)
        rmax = carve(scr, 408, 3)


        ring_full = [sem(f"ring_full{s}") for s in range(SLOTS)]
        x_loaded, prm_loaded, lmask_loaded = sem("x_loaded"), sem("prm_loaded"), sem("lmask_loaded")
        table_loaded = sem("table_loaded")
        stored = sem("stored")
        states_stored = sem("states_stored")
        consts_set = sem("consts_set")
        squares, sum_sq, root, normed = sem("squares"), sem("sum_sq"), sem("root"), sem("normed")
        dve_link, act_link, pool_link = sem("dve_link"), sem("act_link"), sem("pool_link")
        proj, raw_ready, conv_done, z_ready = sem("proj"), sem("raw_ready"), sem("conv_done"), sem("z_ready")
        raw_saved, conv_s_done, silu_done, small_ready = sem("raw_saved"), sem("conv_s_done"), sem("silu_done"), sem("small_ready")
        qk_sq, qk_sum, qk_root, qk_normed = sem("qk_sq"), sem("qk_sum"), sem("qk_root"), sem("qk_normed")
        in_split_hi, in_split_lo = sem("in_split_hi"), sem("in_split_lo")
        qk_rows_set, qk_spread, o_rows_set = sem("qk_rows_set"), sem("qk_spread"), sem("o_rows_set")
        gates_a, gates_e, gates_done = sem("gates_a"), sem("gates_e"), sem("gates_done")
        cum_ps, cum_sb, cum_exp = sem("cum_ps"), sem("cum_sb"), sem("cum_exp")
        rowdec, arg_done, dec_exp, ecum_row, kk_ready, coef_done = (
            sem("rowdec"), sem("arg_done"), sem("dec_exp"), sem("ecum_row"), sem("kk_ready"), sem("coef_done"))
        turned, turned_sb = sem("turned"), sem("turned_sb")
        y_ps, y_sb, x_ps, z_ps, x_sb, z_sb = sem("y_ps"), sem("y_sb"), sem("x_ps"), sem("z_ps"), sem("x_sb"), sem("z_sb")
        kdec_done, q_dec_done = sem("kdec_done"), sem("q_dec_done")
        ks_ps, w_sb, u_ps, u_sb, s_ps, s_sb, o_ps, o_sb = (
            sem("ks_ps"), sem("w_sb"), sem("u_ps"), sem("u_sb"), sem("s_ps"), sem("s_sb"), sem("o_ps"), sem("o_sb"))
        core_done = sem("core_done")
        sdiag, srow_ps, sread_ps, sdecayed, su_done, st_ps, st_sb, sou, sout_ps, snew = (
            sem("sdiag"), sem("srow_ps"), sem("sread_ps"), sem("sdecayed"), sem("su_done"), sem("st_ps"), sem("st_sb"),
            sem("sou"), sem("sout_ps"), sem("snew"))
        osq_done, osum, oroot, o_normed = sem("osq_done"), sem("osum"), sem("oroot"), sem("o_normed")
        outp, out_added = sem("outp"), sem("out_added")
        f_split_hi, f_split_lo, f_used, f_silu, f_act, f_hi_set, f_lo_set, fh_hi_set, fh_lo_set, f_added = (
            sem(n) for n in ("f_split_hi", "f_split_lo", "f_used", "f_silu", "f_act", "f_hi_set", "f_lo_set", "fh_hi_set",
                             "fh_lo_set", "f_added"))
        piece_full = [sem(f"piece_full{i}") for i in range(RAW)]
        split_hi, split_lo, piece_used = sem("split_hi"), sem("split_lo"), sem("piece_used")
        m_silu, m_act, act_turned, aT_hi_set, aT_lo_set, xe_hi_set, xe_lo_set = (
            sem(n) for n in ("m_silu", "m_act", "act_turned", "aT_hi_set", "aT_lo_set", "xe_hi_set", "xe_lo_set"))
        pos_ps, over_set, h_turned, h_tok = sem("pos_ps"), sem("over_set"), sem("h_turned"), sem("h_tok")
        picked, gathered, ye_sb, spread_ps, spread_sb, comb, comb_added = (
            sem("picked"), sem("gathered"), sem("ye_sb"), sem("spread_ps"), sem("spread_sb"), sem("comb"), sem("comb_added"))
        aproj, aproj_sb, rot_ps, roped, v_ps, v_sb = sem("aproj"), sem("aproj_sb"), sem("rot_ps"), sem("roped"), sem("v_ps"), sem("v_sb")
        sc_ps, sc_max, sc_exp, p_sb, pT_ps, pT_sb, po_ps, po_sb = (
            sem("sc_ps"), sem("sc_max"), sem("sc_exp"), sem("p_sb"), sem("pT_ps"), sem("pT_sb"), sem("po_ps"), sem("po_sb"))
        q_wide_set, k_read, prod_done, lnew_ps, bias_done, pexp, diag_done, probT_ps, probT_sb, v_read, o8_done, o8_turned, od_done = (
            sem(n) for n in ("q_wide_set", "k_read", "prod_done", "lnew_ps", "bias_done", "pexp", "diag_done", "probT_ps",
                             "probT_sb", "v_read", "o8_done", "o8_turned", "od_done"))
        aout, aout_added = sem("aout"), sem("aout_added")
        r_ps, r_arg, r_exp, r_gate = sem("r_ps"), sem("r_arg"), sem("r_exp"), sem("r_gate")

        mm = nc.tensor.matmul

        def tile4(n):
            return ring[:, n % SLOTS, :].rearrange("p (c k m) -> p c k m", c=4, k=KT)

        def slot_free(eng, n):
            m = n - SLOTS
            if C_AIN <= n < C_AIN + SLOTS:
                if n - C_AIN < F_RAW // 2:
                    eng.wait_ge(f_split_lo, PIECES - F_RAW + 2 * (n - C_AIN + 1))
                else:
                    eng.wait_ge(f_used, PIECES)
            elif n < C_OUT:
                eng.wait_ge(in_split_lo, IN_PIECES)
            elif n < C_AIN:
                eng.wait_ge(proj, QKV + H)
            elif m < C_K:
                eng.wait_ge(aproj, 4 * (m - C_AIN + 1))
            elif m < C_V:
                eng.wait_ge(k_read, m - C_K + 1)
            elif m < C_AOUT:
                eng.wait_ge(v_read, m - C_V + 1)
            else:
                eng.wait_ge(aout, 4 * (m - C_AOUT + 1))

        def load_pages(eng, n, pages):
            first, cache = (C_K, k_pages) if n < C_V else (C_V, v_pages)
            slot_free(eng, n)
            for page in pages:
                entry = (n - first) * PPC + page
                at_page = eng.value_load(table[0:1, entry:entry + 1], min_val=0, max_val=cache.shape[0] - 1)
                dst = ring[:, n % SLOTS, page * (SLOT // PPC):(page + 1) * (SLOT // PPC)]
                eng.dma_start(dst, cache[bass.ds(at_page, 1)].rearrange("a p n -> p (a n)"))\
                   .then_inc(ring_full[n % SLOTS], 16)

        C_BOTH = C_K + SLOTS

        block = ctx.enter_context(nc.Block())

        @block.sync
        def _(sp):
            def load(n, src, size=SLOT):
                slot_free(sp, n)
                sp.dma_start(ring[:, n % SLOTS, 0:size], src).then_inc(ring_full[n % SLOTS], 16)

            sp.dma_start(xT[:, :, :], x_in).then_inc(x_loaded, 16)
            sp.dma_start(cst[:, :], cst_in).then_inc(prm_loaded, 16)
            sp.dma_start(prm[:, :], prm_in).then_inc(prm_loaded, 16)
            sp.dma_start(conv_prev[:, :, :, :], conv_in).then_inc(prm_loaded, 16)
            for p in range(IN_PIECES):
                if p >= RAW:
                    sp.wait_ge(in_split_lo, p - RAW + 1)
                sp.dma_start(raw_w[:, p % RAW, :], gdn_in_w[p]).then_inc(piece_full[p % RAW], 16)
                if p == 4:
                    sp.dma_start(core[:, 14336:15232], lmask_in).then_inc(lmask_loaded, 16)
            for n in range(2):
                load(C_STATE + n, state_in[n])
            for n in range(2):
                load(C_OUT + n, gdn_out_w[n])
            for p in range(PIECES):
                if p >= F_RAW:
                    sp.wait_ge(f_split_lo, p - F_RAW + 1)
                elif p < 4:
                    sp.wait_ge(states_stored, 16)
                else:
                    sp.wait_ge(outp, 4)
                sp.dma_start(raw_w[:, p % F_RAW, :], ffn_w[p]).then_inc(piece_full[p % F_RAW], 16)
            for n in range(4):
                load(C_AIN + n, att_in_w[n])
            sp.wait_ge(table_loaded, 16)
            for n in range(C_K, C_AOUT):
                load_pages(sp, n, range(0, PPC) if n < C_BOTH else range(0, PPC // 2))
            for n in range(2):
                load(C_AOUT + n, att_out_w[n])

            def load_expert(e, rnd, first=False):
                v = e + NE * rnd
                for p in range(PIECES):
                    if not first or p >= RAW:
                        sp.wait_ge(split_lo, v * PIECES + (p - RAW + 1))
                    else:
                        slot = p * PIECE // SLOT
                        last = max(n for n in range(CHUNKS) if n % SLOTS == slot)
                        sp.wait_ge(v_read, last - C_V + 1)
                    row = moe_w[e * PIECES + p] if first else \
                        moe_w[bass.ds(e * PIECES + p, 1)].rearrange("a p n -> p (a n)")
                    sp.dma_start(raw_w[:, p % RAW, :], row).then_inc(piece_full[p % RAW], 16)

            load_expert(0, 0, first=True)
            with sp.Fori(1, NE) as e:
                load_expert(e, 0)
            sp.wait_ge(over_set, 1)
            over_cap = sp.value_load(more[0:1, 0:1], min_val=0, max_val=1)
            with sp.If(over_cap == 1):
                for rnd in range(1, ROUNDS):
                    with sp.Fori(0, NE) as e:
                        load_expert(e, rnd)
            sp.wait_ge(stored, 16 * STORES)

        @block.tensor
        def _(pe):
            def arrived(n):
                pe.wait_ge(ring_full[n % SLOTS], full_value(n))

            def norm_sums(i, tiles=range(KT)):
                for k in tiles:
                    pe.wait_ge(squares, KT * i + k + 1)
                    last = mm(bank[3][:, 0:T], ones, hT[:, k, :], start=(k == 0), stop=(k == KT - 1))
                    if k == KT - 1:
                        last.then_inc(sum_sq, 1)

            def stationary_mm(out, hi, lo, move_hi, move_lo, first, last):
                mm(out, hi, move_hi, start=first, stop=False)
                mm(out, hi, move_lo, start=False, stop=False)
                return mm(out, lo, move_hi, start=False, stop=last)

            pe.wait_ge(prm_loaded, 48)
            norm_sums(0)

            def qk_row_sums(c):
                sel = c_("sel_q") if c < H else c_("sel")
                pe.wait_ge(qk_sq, c + 1)
                ins = mm(bank[5][0:2 * H, 0:NPR], sel[:, 15 - c:31 - c], nrm[:, c, 0:NPR], start=(c == 0), stop=(c == 2 * H - 1))
                if c == 2 * H - 1:
                    ins.then_inc(qk_sum, 1)

            def qk_spread_row(c):
                pe.wait_ge(qk_rows_set, 1)
                if c >= 2:
                    pe.wait_ge(qk_normed, c - 1)
                mm(bank[6 + c % 2][:, 0:NPR], ident[0:2 * H, c:c + 1].to_broadcast([2 * H, P]), qk_rows,
                   start=True, stop=True).then_inc(qk_spread, 1)

            for k in range(KT):
                pe.wait_ge(normed, k + 1)
                last = mm(bank[4][0:2 * H, 0:T], w_small[:, k, :], hT[:, k, :], start=(k == 0), stop=(k == KT - 1))
            last.then_inc(small_ready, 1)
            for c in range(QKV + H):
                if c == 4:
                    pe.wait_ge(gates_a, 1)
                    for i, (t0, n) in enumerate(TOK_TILES):
                        last = nc.tensor.transpose(bank[4][0:n, 384 + 16 * i:400 + 16 * i], small_T[:, t0:t0 + n],
                                                   ident[0:2 * H, 0:2 * H])
                    last.then_inc(small_ready, 1)
                if c == 12:
                    pe.wait_ge(gates_done, 1)
                    for i in range(CH):
                        mm(bank[4][:, 64 + 8 * i:72 + 8 * i], upper, gdec[:, i, :], start=True, stop=True)
                    mm(bank[4][:, 80:96], ones, gdec[:, 0:2, :].rearrange("p c h -> p (c h)"),
                       start=True, stop=True).then_inc(cum_ps, 1)
                if c % 2 == 0:
                    pe.wait_ge(in_split_lo, c // 2 + 1)
                if c >= 4:
                    if c - 4 < QKV:
                        pe.wait_ge(raw_ready, c - 3)
                    else:
                        pe.wait_ge(z_ready, c - 4 - QKV + 1)
                hi, lo = (w[:, (c // 2) % SPLIT, D * (c % 2):D * (c % 2 + 1)].rearrange("p (k m) -> p k m", m=P)
                          for w in (w_hi, w_lo))
                for k in range(KT):
                    if c == 0:
                        pe.wait_ge(fh_lo_set, k + 1)
                    last = stationary_mm(bank[c % 4][:, 0:T], hi[:, k, :], lo[:, k, :], gh_hi[:, k, :], fh_lo[:, k, :],
                                         k == 0, k == KT - 1)
                last.then_inc(proj, 1)
                if 3 <= c < 3 + 2 * H:
                    qk_row_sums(c - 3)
                if c >= QKV:
                    qk_spread_row(2 * (c - QKV))
                    qk_spread_row(2 * (c - QKV) + 1)
                if c == QKV + 5:
                    pe.wait_ge(qk_sq, 2 * H + 1)
                    pe.wait_ge(qk_root, 1)
                    mm(bank[5][:, 0:2 * H * NS], ones, s_sq, start=True, stop=True).then_inc(qk_sum, 1)
            pe.wait_ge(cum_sb, 1)
            pe.wait_ge(qk_normed, 2 * H + 1)

            def turn(g, src):
                n = 2 * g + src
                if n >= 2:
                    pe.wait_ge(turned_sb, n - 1)
                for j in range(GRP):
                    i = GRP * g + j
                    c, h = i // H, i % H
                    last = nc.tensor.transpose(bank[6 + n % 2][:, P * j:P * (j + 1)],
                                               qkv[:, H * (1 + src) + h, P * c:P * (c + 1)], ident)
                last.then_inc(turned, 1)

            for g in range(NG):
                if g == 0:
                    pe.wait_ge(z_ready, H)
                elif g < 3:
                    pe.wait_ge(arg_done, g)
                else:
                    pe.wait_ge(ecum_row, 1)
                for j in range(GRP):
                    c, h = (GRP * g + j) // H, (GRP * g + j) % H
                    last = mm(bank[0][:, P * j:P * (j + 1)], gdec[:, c, h:h + 1].to_broadcast([P, P]), upper,
                              start=True, stop=True)
                last.then_inc(rowdec, 1)
                if g >= 1:
                    pe.wait_ge(coef_done, g)
                for b, q in ((1, 1), (2, 0)):
                    for j in range(GRP):
                        c, h = (GRP * g + j) // H, (GRP * g + j) % H
                        last = mm(bank[b][:, P * j:P * (j + 1)], qkv[:, H + h, P * c:P * (c + 1)],
                                  qkv[:, q * H + h, P * c:P * (c + 1)], start=True, stop=True)
                last.then_inc(kk_ready, 1)
                turn(g, 0)
                turn(g, 1)
            arrived(C_STATE)
            arrived(C_STATE + 1)
            for h in range(H):
                for b in range(NS):
                    i = h * NS + b
                    last = mm(bank[3][:, 2 * i:2 * i + 2], states[:, i, :], qkv[:, h:h + H + 1:H, NPR + b],
                              start=True, stop=True)
            last.then_inc(sread_ps, 1)
            pe.wait_ge(sdiag, 1)
            for r in range(2):
                mm(bank[5][:, 64 * r:64 * r + 64], ones[0:NS, :], diag8[0:NS, r, :], start=True, stop=True)
            mm(bank[5][:, 128:192], ones, qk_, start=True, stop=True).then_inc(srow_ps, 1)

            for l in range(LEVELS):
                for g in range(NG):
                    if l == 0:
                        pe.wait_ge(coef_done, NG)
                        pe.wait_ge(ecum_row, 2)
                        if g == 3:
                            pe.wait_ge(su_done, 1)
                    else:
                        pe.wait_ge(x_sb, NG * (l - 1) + g + 1)
                    for j in range(GRP):
                        i = GRP * g + j
                        out = bank[g][:, P * j:P * (j + 1)]
                        if l == 0:
                            last = nc.tensor.transpose(out, coefT[:, i, :], ident)
                        else:
                            last = mm(out, coefT[:, i, :], X[:, i, :], start=True, stop=True)
                    last.then_inc(y_ps, 1)
                for g in range(NG):
                    pe.wait_ge(y_sb, NG * l + g + 1)
                    bx, bz = bank[4 + g % 2], bank[6 + g % 2]
                    if l == 0 and g < 2:
                        pe.wait_ge(turned_sb, 2 * NG)
                        pe.wait_ge(su_done, 1)
                    if NG * l + g >= 2:
                        pe.wait_ge(z_sb, NG * l + g - 1)
                    if 0 < l < LEVELS - 1:
                        for j in range(GRP):
                            i = GRP * g + j
                            last = mm(bx[:, P * j:P * (j + 1)], Z[:, i, :], Y[:, i, :], start=True, stop=True)
                        last.then_inc(x_ps, 1)
                    for j in range(GRP):
                        i = GRP * g + j
                        if l == 0:
                            last = nc.tensor.transpose(bz[:, P * j:P * (j + 1)], Y[:, i, :], ident)
                        else:
                            last = mm(bz[:, P * j:P * (j + 1)], Y[:, i, :], Z[:, i, :], start=True, stop=True)
                    last.then_inc(z_ps, 1)
            pe.wait_ge(z_sb, NG * LEVELS)
            for c in range(CH):
                if c == 1:
                    pe.wait_ge(s_sb, 2)
                    for g in range(2):
                        for j in range(GRP):
                            h = GRP * g + j
                            last = mm(bank[g][:, P * j:P * (j + 1)], qkv[:, H + h, P:2 * P], S_new[:, h, :],
                                      start=True, stop=True)
                        last.then_inc(ks_ps, 1)
                for g in range(2):
                    if c == 1:
                        pe.wait_ge(w_sb, g + 1)
                    for j in range(GRP):
                        h = GRP * g + j
                        rhs = vtok[:, h, :] if c == 0 else rhs_w[:, h, :]
                        last = mm(bank[2 + g][:, P * j:P * (j + 1)], Z[:, H * c + h, :], rhs, start=True, stop=True)
                    last.then_inc(u_ps, 1)
                for g in range(2):
                    pe.wait_ge(u_sb, 2 * c + g + 1)
                    if c == 1:
                        pe.wait_ge(s_sb, 2)
                    if c == 0 and g == 0:
                        pe.wait_ge(kdec_done, 1)
                    for j in range(GRP):
                        h = GRP * g + j
                        last = mm(bank[4 + g][:, P * j:P * (j + 1)], ktok[:, H * c + h, :], u_tok[:, h, :],
                                  start=True, stop=True)
                    last.then_inc(s_ps, 1)
                    if c == 1:
                        pe.wait_ge(q_dec_done, 1)
                        pe.wait_ge(o_sb, g + 1)
                    for j in range(GRP):
                        h = GRP * g + j
                        out = bank[6 + g][:, P * j:P * (j + 1)]
                        last = mm(out, u_tok[:, h, :], attT[:, H * c + h, :], start=True, stop=(c == 0))
                        if c == 1:
                            last = mm(out, S_new[:, h, :], qkv[:, h, P:2 * P], start=False, stop=True)
                    last.then_inc(o_ps, 1)
            pe.wait_ge(sou, 1)
            pe.wait_ge(w_sb, 2)
            nc.tensor.transpose(bank[0][0:64, 0:P], u_s, ident)
            nc.tensor.transpose(bank[0][0:64, P:2 * P],
                                sk, ident).then_inc(st_ps, 1)
            for i in range(16):
                pe.wait_ge(st_sb, 2 + i)
                if i < 2:
                    pe.wait_ge(u_sb, 4)
                else:
                    pe.wait_ge(snew, i - 1)
                mm(bank[2 + i % 2], kv_rows[:, 1, :], wide[:, i % 2, :], start=True, stop=True).then_inc(sout_ps, 1)
            for h in range(H):
                pe.wait_ge(osq_done, h + 1)
                last = mm(bank[1][0:H, 0:T], c_("sel")[:, 15 - h:15 - h + H], osq[:, h, :], start=(h == 0), stop=(h == H - 1))
            last.then_inc(osum, 1)
            pe.wait_ge(o_rows_set, 2)
            for h in range(H):
                if h >= 2:
                    pe.wait_ge(o_normed, h - 1)
                mm(bank[h % 2][:, 0:T], ident[0:H, h:h + 1].to_broadcast([H, P]), o_rows, start=True, stop=True)\
                    .then_inc(oroot, 1)

            def out_projection(first, src, src_ready, done, added, norm_after):
                for d in range(KT):
                    if d % 4 == 0:
                        arrived(first + d // 4)
                    if d >= 4:
                        pe.wait_ge(added, d - 3)
                    for h in range(H):
                        if d == 0:
                            src_ready(h)
                        last = mm(bank[4 + d % 4][:, 0:T], tile4(first + d // 4)[:, d % 4, h, :], src[:, h, :],
                                  start=(h == 0), stop=(h == H - 1))
                    last.then_inc(done, 1)
                    if d >= 2:
                        norm_sums(norm_after, [d - 2])
                norm_sums(norm_after, [KT - 2, KT - 1])

            def o_ready(h):
                pe.wait_ge(o_normed, h + 1)
                if h == 0:
                    pe.wait_ge(o_sb, 4)
                    pe.wait_ge(s_sb, 4)

            out_projection(C_OUT, oT, o_ready, outp, out_added, 1)


            def weight_tiles(p):
                pe.wait_ge(f_split_lo, p + 1)
                return [w[:, p % SPLIT, :].rearrange("p (i m) -> p i m", m=P) for w in (w_hi, w_lo)]

            for f in range(FT):
                hi, lo = weight_tiles(f)
                if f >= 2:
                    pe.wait_ge(f_act, f - 1)
                for up in range(2):
                    for k in range(KT):
                        if f == 0 and up == 0:
                            pe.wait_ge(fh_lo_set, KT + k + 1)
                        i = KT * up + k
                        last = stationary_mm(bank[2 * (f % 2) + up][:, 0:T], hi[:, i, :], lo[:, i, :],
                                             fh_hi[:, k, :], fh_lo[:, k, :], k == 0, k == KT - 1)
                last.then_inc(f_used, 1)
            for n in range(KT * FT):
                d, f, i = n // FT, n % FT, n % F_TILES
                if i == 0:
                    hi, lo = weight_tiles(FT + n // F_TILES)
                if d == 0:
                    pe.wait_ge(f_lo_set, f + 1)
                if f == 0 and d >= 3:
                    pe.wait_ge(f_added, d - 2)
                last = stationary_mm(bank[4 + d % 3][:, 0:T], hi[:, i, :], lo[:, i, :], f_hi[:, f, :], f_lo[:, f, :],
                                     f == 0, f == FT - 1)
                if i == F_TILES - 1:
                    last.then_inc(f_used, 1)
                if f == FT - 1 and d >= 2:
                    norm_sums(2, [d - 2])

            norm_sums(2, [KT - 2, KT - 1])

            def rotate(c):
                pe.wait_ge(prm_loaded, 64)
                pe.wait_ge(aproj_sb, c + 1)
                if c >= 2:
                    pe.wait_ge(roped, c - 1)
                mm(bank[4 + c % 2][0:ROT, 0:T], rot_p, aq[:, c, :], start=True, stop=True).then_inc(rot_ps, 1)

            for c in range(16):
                if c % 4 == 0:
                    arrived(C_AIN + c // 4)
                if c >= 4:
                    pe.wait_ge(aproj_sb, c - 3)
                for k in range(KT):
                    if c == 0:
                        pe.wait_ge(normed, 2 * KT + k + 1)
                    last = mm(bank[c % 4][:, 0:T], tile4(C_AIN + c // 4)[:, c % 4, k, :], hT[:, k, :],
                              start=(k == 0), stop=(k == KT - 1))
                last.then_inc(aproj, 1)
                if 1 <= c <= 12:
                    rotate(c - 1)
            pe.wait_ge(aproj_sb, 16)
            for t in range(CH):
                for h in range(KVH):
                    last = nc.tensor.transpose(bank[6 + t][:, P * h:P * (h + 1)], aq[:, 12 + h, P * t:P * (t + 1)], ident)
                last.then_inc(v_ps, 1)
            pe.wait_ge(roped, 12)

            def scores(h):
                if h >= 2:
                    pe.wait_ge(sc_max, h - 1)
                kv = 8 + h // 2
                mm(bank[4 + h % 2][:, 0:P], aq[:, h, 0:P], aq[:, kv, 0:P], start=True, stop=True)
                mm(bank[4 + h % 2][:, P:3 * P], aq[:, h, P:2 * P], aq[:, kv, 0:2 * P],
                   start=True, stop=True).then_inc(sc_ps, 1)

            def turn_probs(h):
                pe.wait_ge(p_sb, h + 1)
                if h == 0:
                    pe.wait_ge(v_sb, 2)
                else:
                    pe.wait_ge(pT_sb, h)
                for j in range(3):
                    last = nc.tensor.transpose(bank[6][:, P * j:P * (j + 1)], pr_s[:, h % 2, P * j:P * (j + 1)], ident)
                last.then_inc(pT_ps, 1)

            def values(h):
                pe.wait_ge(pT_sb, h + 1)
                pe.wait_ge(v_sb, 2)
                if h >= 1:
                    pe.wait_ge(po_sb, h)
                b, kv = bank[7], h // 2
                mm(b[:, 0:P], v_tok[:, kv, :], pr_T[:, h % 2, 0:P], start=True, stop=True)
                mm(b[:, P:2 * P], v_tok[:, kv, :], pr_T[:, h % 2, P:2 * P], start=True, stop=False)
                mm(b[:, P:2 * P], v_tok[:, KVH + kv, :], pr_T[:, h % 2, 2 * P:3 * P],
                   start=False, stop=True).then_inc(po_ps, 1)

            def key_chunk(c):
                n, b = C_K + c, c // 2
                arrived(n)
                keys = ring[:, n % SLOTS, :].rearrange("p (q g h t) -> p q g h t", q=2, g=4, h=KVH)
                for h in range(KVH):
                    for q in range(2):
                        last = mm(bank[2 * (c % 2) + q][0:64, :].rearrange("p (g t) -> p g t", t=PAGE),
                                  q_wide[:, KVH * b + h, :], keys[:, q, :, h, :],
                                  start=(b == 0 and h == 0), stop=(b == NS - 1 and h == KVH - 1), skip_group_check=True)
                last.then_inc(k_read, 1)

            for i in range(H + 2):
                if 1 <= i <= H:
                    turn_probs(i - 1)
                if i >= 2:
                    values(i - 2)
                if i < H:
                    scores(i)
                if i == 0:
                    pe.wait_ge(q_wide_set, 1)
                key_chunk(i)
            for c in range(H + 2, 2 * NS):
                key_chunk(c)
                if c == 2 * NS - 2:
                    pe.wait_ge(prod_done, 1)
                    pe.wait_ge(pT_sb, H)
                    mm(bank[6][0:64, 0:1], prodn, ones[:, 0:1], start=True, stop=True).then_inc(lnew_ps, 1)
            pe.wait_ge(diag_done, 1)
            pe.wait_ge(sc_max, H)
            pe.wait_ge(po_sb, H)
            for g in range(N_PAGES):
                last = mm(bank[4 + g // 8][:, 64 * (g % 8):64 * (g % 8 + 1)], prob[:, PAGE * g:PAGE * (g + 1)], rd_diag,
                          start=True, stop=True)
                if g % 8 == 7:
                    last.then_inc(probT_ps, 1)
            mm(bank[7][:, 0:64], ones[0:64, :], p_diag, start=True, stop=True).then_inc(probT_ps, 1)

            def turn_o(b):
                pe.wait_ge(o8_done, b + 1)
                nc.tensor.transpose(bank[6][:, H * b:H * (b + 1)], o8[:, b, :], ident[0:8, 0:8]).then_inc(o8_turned, 1)

            for c in range(2 * NS):
                n, b = C_V + c, c // 2
                arrived(n)
                if c % 8 == 0:
                    pe.wait_ge(probT_sb, 2)
                if c % 2 == 0 and b >= 4:
                    pe.wait_ge(o8_done, b - 3)
                for g in range(PPC):
                    page = (c % 2) * PPC + g
                    last = mm(bank[b % 4][0:8, :], prob_T[:, page, H * b:H * (b + 1)],
                              ring[:, n % SLOTS, 512 * g:512 * (g + 1)], start=(page == 0), stop=(page == N_PAGES - 1))
                last.then_inc(v_read, 1)
                if c % 2 == 0 and b >= 1:
                    turn_o(b - 1)
            turn_o(NS - 1)

            def att_ready(h):
                if h == 0:
                    pe.wait_ge(po_sb, H)
                    pe.wait_ge(od_done, 1)

            out_projection(C_AOUT, o_att, att_ready, aout, aout_added, 3)
            pe.wait_ge(normed, 4 * KT)
            for i, (t0, n) in enumerate(TOK_TILES):
                for k in range(KT):
                    last = mm(bank[0][0:n, NE * i:NE * i + NE], hT[:, k, t0:t0 + n], router[:, k, :],
                              start=(k == 0), stop=(k == KT - 1))
            last.then_inc(r_ps, 1)
            for i, (t0, n) in enumerate(TOK_TILES):
                for half in range(2):
                    m = 2 * i + half
                    if m >= 2:
                        pe.wait_ge(h_tok, m - 1)
                    for j in range(4):
                        last = nc.tensor.transpose(bank[4 + half][0:n, P * j:P * (j + 1)],
                                                   hT[:, 4 * half + j, t0:t0 + n], ident)
                    last.then_inc(h_turned, 1)
            pe.wait_ge(r_gate, 1)
            for i, (t0, n) in enumerate(TOK_TILES):
                out = bank[0][0:n, 32 + NE * i:32 + NE * (i + 1)]
                for j in range(i):
                    mm(out, ones[:, 0:n], rrank[:, j, :], start=(j == 0), stop=False)
                mm(out, upper[0:n, 0:n], rrank[0:n, i, :], start=(i == 0), stop=True)
            for i, (t0, n) in enumerate(TOK_TILES):
                last = mm(bank[0][0:1, 64:64 + NE], ones[0:n, 0:1], rrank[0:n, i, :], start=(i == 0), stop=(i == 2))
            last.then_inc(pos_ps, 1)
            pe.wait_ge(h_tok, 6)

            def gather(v):
                pe.wait_ge(picked, v + 1)
                for half in range(2):
                    for j in range(4):
                        k = 4 * half + j
                        for i, (t0, n) in enumerate(TOK_TILES):
                            last = mm(bank[6 + half][:, CAP * j:CAP * (j + 1)], htok[0:n, i, P * k:P * (k + 1)],
                                      pick[0:n, i, :], start=(i == 0), stop=(i == 2))
                    last.then_inc(gathered, 1)

            def combine(v, d):
                if d == 0:
                    pe.wait_ge(ye_sb, v * 2 + 2)
                if d >= 2:
                    pe.wait_ge(comb_added, v * KT + (d - 1))
                mm(bank[4 + d % 2][:, 0:T], ye[:, P * d:P * (d + 1)], spread, start=True, stop=True).then_inc(comb, 1)

            def split_mm(out, hi, lo, w_at, first, last):
                (buf, col) = w_at
                move_hi, move_lo = w_hi[:, buf, col:col + N], w_lo[:, buf, col:col + N]
                mm(out, hi, move_hi, start=first, stop=False)
                mm(out, hi, move_lo, start=False, stop=False)
                return mm(out, lo, move_hi, start=False, stop=last)

            def expert(v, first=False):
                for p in range(PIECES):
                    pe.wait_ge(split_lo, v * PIECES + (p + 1))
                    buf = p % SPLIT
                    if p < UP_PIECES:
                        j, up, half = p // 4, (p // 2) % 2, p % 2
                        out = bank[2 * up + j % 2]
                        if p == 0:
                            pe.wait_ge(xe_lo_set, v + 1)
                        if half == 0 and (not first or j >= 2):
                            pe.wait_ge(m_act if up else m_silu, v * GROUPS + (j - 1 if j >= 2 else 0))
                        for i in range(4):
                            k = 4 * half + i
                            last = split_mm(out, xe_hi[:, k, :], xe_lo[:, k, :], (buf, N * i), k == 0, k == KT - 1)
                    else:
                        if p == UP_PIECES:
                            pe.wait_ge(spread_sb, v + 1)
                        for i in range(F_PIECE):
                            f = F_PIECE * (p - UP_PIECES) + i
                            if f % 4 == 0:
                                pe.wait_ge(aT_lo_set, v * GROUPS + (f // 4 + 1))
                            for half in range(2):
                                last = split_mm(bank[4 + half], aT_hi[:, f, :], aT_lo[:, f, :],
                                                (buf, D * i + N * half), f == 0, f == FT - 1)
                    last.then_inc(piece_used, 1)
                    if not first and 5 <= p < 5 + 2 * KT and p % 2 == 1:
                        combine(v - 1, (p - 5) // 2)
                    if p >= 8 and p % 4 == 0 and (p - 8) // 4 < GROUPS:
                        j = (p - 8) // 4
                        pe.wait_ge(m_act, v * GROUPS + (j + 1))
                        if j >= 2:
                            pe.wait_ge(aT_lo_set, v * GROUPS + (j - 1))
                        for i in range(4):
                            last = nc.tensor.transpose(bank[6 + j % 2][:, P * i:P * (i + 1)],
                                                       s_act[:, j % 2, P * i:P * (i + 1)], ident)
                        last.then_inc(act_turned, 1)
                    if p == 24:
                        if not first:
                            pe.wait_ge(comb_added, v * KT)
                        for i, (t0, n) in enumerate(TOK_TILES):
                            last = nc.tensor.transpose(bank[4][0:CAP, t0:t0 + n], pick_g[0:n, i, :], ident[0:n, 0:n])
                        last.then_inc(spread_ps, 1)
                    if p == 38:
                        pe.wait_ge(aT_lo_set, v * GROUPS + GROUPS)
                        gather(v + 1)

            gather(0)
            expert(0, first=True)
            with pe.Fori(1, NE) as e:
                expert(e)
            over_cap = pe.value_load(more[0:1, 0:1], min_val=0, max_val=1)
            with pe.If(over_cap == 0):
                for d in range(KT):
                    combine(NE - 1, d)
            with pe.Else():
                for rnd in range(1, ROUNDS):
                    with pe.Fori(0, NE) as e:
                        expert(e + NE * rnd)
                for d in range(KT):
                    combine(ROUNDS * NE - 1, d)
            norm_sums(4)

        @block.scalar
        def _(act):
            steps = [0]

            def link(ins):
                steps[0] += 1
                ins.then_inc(act_link, 1)
                act.wait_ge(act_link, steps[0])

            A = nc.scalar.activation
            act.dma_start(table[:, :], table_in).then_inc(table_loaded, 16)
            act.wait_ge(prm_loaded, 48)

            def norm_root(i):
                act.wait_ge(sum_sq, i + 1)
                A(rms, bank[3][:, 0:T], ACT.Sqrt, bias=eps, scale=1.0 / D).then_inc(root, 1)

            act.wait_ge(consts_set, 1)
            def split_in(p):
                act.wait_ge(piece_full[p % RAW], 16 * (p // RAW + 1))
                if p >= SPLIT:
                    act.wait_ge(proj, 2 * (p - SPLIT + 1))
                A(w_hi[:, p % SPLIT, :], raw_w[:, p % RAW, :], ACT.Copy).then_inc(in_split_hi, 1)

            norm_root(0)
            for k in range(KT):
                act.wait_ge(normed, k + 1)
                A(gh_hi[:, k, :], hT[:, k, :], ACT.Copy).then_inc(fh_hi_set, 1)
            for p in range(SPLIT):
                split_in(p)
            act.wait_ge(normed, KT)
            for c in range(QKV + 1):
                if c == 7:
                    act.wait_ge(gates_a, 2)
                    A(beta, ba[:, :, 0:H], ACT.Exp, scale=-1.0)
                    A(e_alog, p_("a_log"), ACT.Exp)
                    link(A(t_exp, t_abs, ACT.Exp, scale=-1.0))
                    A(t_exp, t_exp, ACT.Ln, bias=ones[:, 0:1]).then_inc(gates_e, 1)
                if c == 17:
                    act.wait_ge(cum_sb, 1)
                    A(neg_ecum, cum, ACT.Exp)
                    A(e_end, e_end, ACT.Exp)
                    A(ge_s[0:NS], gdec[0:NS, 2, :], ACT.Exp)
                    A(to_end, to_end, ACT.Exp).then_inc(cum_exp, 1)
                if c == 21:
                    act.wait_ge(qk_sum, 1)
                    A(qk_rows, bank[5][0:2 * H, 0:NPR], ACT.Sqrt, bias=c_("eps_qk")[0:2 * H], scale=1.0).then_inc(qk_root, 1)
                if c < QKV:
                    act.wait_ge(proj, c + 1)
                    if c >= 2:
                        act.wait_ge(conv_done, c - 1)
                        act.wait_ge(raw_saved, c - 1)
                    A(raw[:, c % 2, CONV_W - 1:], bank[c % 4][:, 0:T], ACT.Copy).then_inc(raw_ready, 1)
                if c >= 1:
                    act.wait_ge(conv_done, c)
                    A(qkv[:, c - 1, 0:NPR], qkv[:, c - 1, 0:NPR], ACT.Silu).then_inc(silu_done, 1)
                if c % 2 == 1 and (c + 5) // 2 < IN_PIECES:
                    split_in((c + 5) // 2)
            act.wait_ge(conv_s_done, 1)
            A(qkv[:, :, NPR:T], qkv[:, :, NPR:T], ACT.Silu).then_inc(silu_done, 1)
            for h in range(H):
                act.wait_ge(proj, QKV + h + 1)
                A(zT[:, h, :], bank[h % 4][:, 0:T], ACT.Silu).then_inc(z_ready, 1)
                if h == 1:
                    split_in(IN_PIECES - 1)
                if h == 6:
                    act.wait_ge(qk_sum, 2)
                    A(s_rt[:, 0:H * NS], bank[5][:, 0:H * NS], ACT.Sqrt, bias=eps_q, scale=float(DK))
                    A(s_rt[:, H * NS:], bank[5][:, H * NS:2 * H * NS], ACT.Sqrt, bias=eps, scale=1.0).then_inc(qk_root, 1)

            def untuck(g):
                for src, dst in ((0, ktok), (1, vtok)):
                    n = 2 * g + src
                    act.wait_ge(turned, n + 1)
                    A(dst[:, GRP * g:GRP * (g + 1), :].rearrange("p i n -> p (i n)"), bank[6 + n % 2][:, :],
                      ACT.Copy).then_inc(turned_sb, 1)

            for g in range(NG):
                act.wait_ge(arg_done, g + 1)
                if g >= CH:
                    A(Y[:, GRP * (g - 2):GRP * (g - 1), :].rearrange("p i n -> p (i n)"), bank[0][:, :],
                      ACT.Exp).then_inc(ecum_row, 1)
                A(decT[:, g % 2, :], decT[:, g % 2, :], ACT.Exp).then_inc(dec_exp, 1)
                untuck(g)
            for c in range(CH):
                for g in range(2):
                    act.wait_ge(o_ps, 2 * c + g + 1)
                    if c == 0 and g == 0:
                        act.wait_ge(qk_normed, 2 * H + 1)
                    A(oT[:, GRP * g:GRP * (g + 1), P * c:P * (c + 1)],
                      bank[6 + g][:, :].rearrange("p (h t) -> p h t", t=P), ACT.Copy).then_inc(o_sb, 1)
            act.wait_ge(osum, 1)
            A(o_rows, bank[1][0:H, 0:T], ACT.Sqrt, bias=eps[0:H], scale=1.0 / DK).then_inc(o_rows_set, 1)
            def split_f(p):
                act.wait_ge(piece_full[p % F_RAW], 16 * (earlier_fills(p % F_RAW, True) + p // F_RAW + 1))
                if p >= SPLIT:
                    act.wait_ge(f_used, p - SPLIT + 1)
                A(w_hi[:, p % SPLIT, :], raw_w[:, p % F_RAW, :], ACT.Copy).then_inc(f_split_hi, 1)

            act.wait_ge(outp, KT)
            act.wait_ge(core_done, 1)
            split_f(0)
            norm_root(1)

            def silu_f(f):
                act.wait_ge(f_used, f + 1)
                if f >= F_ACTS:
                    act.wait_ge(f_lo_set, f - F_ACTS + 1)
                A(f_tmp[:, f % F_ACTS, :], bank[2 * (f % 2)][:, 0:T], ACT.Silu).then_inc(f_silu, 1)

            def hi_f(f):
                act.wait_ge(f_act, f + 1)
                A(f_hi[:, f, :], f_tmp[:, f % F_ACTS, :], ACT.Copy).then_inc(f_hi_set, 1)

            for k in range(KT):
                act.wait_ge(normed, KT + k + 1)
                A(fh_hi[:, k, :], hT[:, k, :], ACT.Copy).then_inc(fh_hi_set, 1)
            for p in range(1, SPLIT):
                split_f(p)
            for p in range(SPLIT, PIECES):
                if p < FT:
                    split_f(p)
                if 0 <= p - 4 < FT:
                    hi_f(p - 4)
                if 0 <= p - 3 < FT:
                    silu_f(p - 3)
                if p >= FT:
                    split_f(p)
            norm_root(2)
            for c in range(16):
                act.wait_ge(aproj, c + 1)
                if c == 0:
                    act.dma_start(rope, rope_in).then_inc(prm_loaded, 16)
                A(aq[:, c, :], bank[c % 4][:, 0:T], ACT.Copy).then_inc(aproj_sb, 1)
            for t in range(CH):
                act.wait_ge(v_ps, t + 1)
                A(v_tok[:, KVH * t:KVH * (t + 1), :].rearrange("p i n -> p (i n)"), bank[6 + t][:, :],
                  ACT.Copy).then_inc(v_sb, 1)

            def p_exp(h):
                act.wait_ge(sc_max, h + 1)
                i, m = h % 2, 2 * (h % 2)
                A(pr_s[:, i, 0:P], pr_s[:, i, 0:P], ACT.Exp, bias=pmax[:, m:m + 1], accum_out=psums[:, m:m + 1])
                A(pr_s[:, i, P:3 * P], pr_s[:, i, P:3 * P], ACT.Exp, bias=pmax[:, m + 1:m + 2],
                  accum_out=psums[:, m + 1:m + 2]).then_inc(sc_exp, 1)

            def p_turned(h):
                act.wait_ge(pT_ps, h + 1)
                if h >= 2:
                    act.wait_ge(po_ps, h - 1)
                A(pr_T[:, h % 2, :], bank[6][:, 0:3 * P], ACT.Copy).then_inc(pT_sb, 1)

            def p_out(h):
                act.wait_ge(po_ps, h + 1)
                A(o_att[:, h, 0:NPR], bank[7][:, 0:NPR], ACT.Copy).then_inc(po_sb, 1)

            for i in range(H + 2):
                if 1 <= i <= H:
                    p_turned(i - 1)
                if i >= 2:
                    p_out(i - 2)
                if i < H:
                    p_exp(i)
                if i >= 1:
                    load_pages(act, C_BOTH + i - 1, range(PPC // 2, PPC))
            for n in range(C_BOTH + H + 1, C_V + SLOTS):
                load_pages(act, n, range(PPC // 2, PPC))
            act.wait_ge(bias_done, 1)
            for n in range(BLOCKS):
                A(prob[:, 256 * n:256 * (n + 1)], bank[n // 2][0:64, 256 * (n % 2):256 * (n % 2 + 1)], ACT.Exp,
                  bias=biases[:, n:n + 1], scale=SCALE, accum_out=sums[:, n:n + 1])
            A(p_new, l_new, ACT.Exp, bias=m_neg, scale=SCALE).then_inc(pexp, 1)
            for i in range(2):
                act.wait_ge(probT_ps, i + 1)
                A(prob_T[:, 8 * i:8 * (i + 1), :].rearrange("p g r -> p (g r)"), bank[4 + i][:, :], ACT.Copy)\
                    .then_inc(probT_sb, 1)
            for n in range(C_V + SLOTS, C_AOUT):
                load_pages(act, n, range(PPC // 2, PPC))
            def split_piece(v, p, first=False):
                act.wait_ge(piece_full[p % RAW], v * (16 * PIECES // RAW) + 16 * (earlier_fills(p % RAW, False) + p // RAW + 1))
                if not first or p >= SPLIT:
                    act.wait_ge(piece_used, v * PIECES + (p - SPLIT + 1))
                A(w_hi[:, p % SPLIT, :], raw_w[:, p % RAW, :], ACT.Copy).then_inc(split_hi, 1)

            act.wait_ge(aout, KT)
            split_piece(0, 0, first=True)
            norm_root(3)
            for p in range(1, SPLIT):
                split_piece(0, p, first=True)
            act.wait_ge(stored, 16 * 5)
            for i, (t0, n) in enumerate(TOK_TILES):
                for half in range(2):
                    m = 2 * i + half
                    act.wait_ge(h_turned, m + 1)
                    A(htok[0:n, i, 512 * half:512 * (half + 1)], bank[4 + half][0:n, :], ACT.Copy).then_inc(h_tok, 1)
                    if m == 2:
                        act.wait_ge(r_arg, 1)
                        A(rgate[:, :, 0:NE], rgate[:, :, 0:NE], ACT.Exp).then_inc(r_exp, 1)

            def take_gathered(v):
                for half in range(2):
                    act.wait_ge(gathered, v * 2 + (half + 1))
                    A(xe_hi[:, 4 * half:4 * half + 4, :].rearrange("p k n -> p (k n)"), bank[6 + half][:, :], ACT.Copy)\
                        .then_inc(xe_hi_set, 1)

            def take_y(v):
                act.wait_ge(piece_used, v * PIECES + PIECES)
                for half in range(2):
                    A(ye[:, N * half:N * (half + 1)], bank[4 + half][:, :], ACT.Copy).then_inc(ye_sb, 1)

            def expert(v, first=False):
                for p in range(PIECES):
                    if not first or p >= SPLIT:
                        split_piece(v, p, first)
                    if p == 2 and not first:
                        take_y(v - 1)
                    if p % 4 == 0 and 1 <= p // 4 <= GROUPS:
                        j = p // 4 - 1
                        act.wait_ge(piece_used, v * PIECES + (4 * j + 2))
                        if not first or j >= 2:
                            act.wait_ge(m_act, v * GROUPS + (j - 1 if j >= 2 else 0))
                        A(s_sil[:, j % 2, :], bank[j % 2][:, :], ACT.Silu).then_inc(m_silu, 1)
                    if p % 4 == 0 and 3 <= p // 4 < 3 + GROUPS:
                        j = p // 4 - 3
                        act.wait_ge(act_turned, v * GROUPS + (j + 1))
                        A(aT_hi[:, 4 * j:4 * j + 4, :].rearrange("p f n -> p (f n)"), bank[6 + j % 2][:, :], ACT.Copy)\
                            .then_inc(aT_hi_set, 1)
                    if p == UP_PIECES:
                        act.wait_ge(spread_ps, v + 1)
                        A(spread, bank[4][0:CAP, 0:T], ACT.Copy).then_inc(spread_sb, 1)
                    if p == PIECES - 1:
                        take_gathered(v + 1)

            take_gathered(0)
            expert(0, first=True)
            with act.Fori(1, NE) as e:
                expert(e)
            over_cap = act.value_load(more[0:1, 0:1], min_val=0, max_val=1)
            with act.If(over_cap == 0):
                take_y(NE - 1)
            with act.Else():
                for rnd in range(1, ROUNDS):
                    with act.Fori(0, NE) as e:
                        expert(e + NE * rnd)
                take_y(ROUNDS * NE - 1)
            norm_root(4)

        @block.gpsimd
        def _(pool):
            steps = [0]

            def link(ins):
                steps[0] += 1
                ins.then_inc(pool_link, 1)
                pool.wait_ge(pool_link, steps[0])

            G = nc.gpsimd
            link(G.memset(raw[:, :, :], 0.0))
            link(G.memset(small[:, :], 0.0))
            G.memset(small[:, 766:767], 0.0).then_inc(consts_set, 1)
            for c in range(QKV):
                pool.wait_ge(raw_ready, c + 1)
                G.tensor_copy(conv_last[:, c, :], raw[:, c % 2, NPR:NPR + CONV_W - 1])
                G.tensor_copy(conv_new[:, c, :], raw[:, c % 2, NPR + CONV_W - 1:]).then_inc(raw_saved, 1)
            pool.wait_ge(raw_saved, QKV)
            pool.wait_ge(prm_loaded, 48)
            dst = qkv[:, :, NPR:T]
            tmp = nrm[:, 0, 0:QKV * NS].rearrange("p (c b) -> p c b", b=NS)
            wide_w = lambda j: conv_w[:, :, j:j + 1].to_broadcast([P, QKV, NS])
            link(G.tensor_tensor(dst, conv_prev[:, :, 0, :], wide_w(0), ALU.mult))
            for j in range(1, CONV_W):
                src = conv_prev[:, :, j, :] if j < CONV_W - 1 else conv_new[:, :, :]
                link(G.tensor_tensor(tmp, src, wide_w(j), ALU.mult))
                if j < CONV_W - 1:
                    link(G.tensor_tensor(dst, dst, tmp, ALU.add))
                else:
                    G.tensor_tensor(dst, dst, tmp, ALU.add).then_inc(conv_s_done, 1)
            pool.dma_start(convp_out, conv_last[:, :, :]).then_inc(stored, 16)
            pool.dma_start(convs_out[:, :, 0:CONV_W - 2, :], conv_prev[:, :, 1:, :]).then_inc(stored, 16)
            pool.dma_start(convs_out[:, :, CONV_W - 2, :], conv_new[:, :, :]).then_inc(stored, 16)
            pool.wait_ge(sread_ps, 1)
            pool.wait_ge(su_done, 1)
            for i in range(8):
                s = states[:, 8 * i:8 * i + 8, :]
                G.tensor_tensor(s, s, row_b[:, 1, 8 * i:8 * i + 8].unsqueeze(2).to_broadcast([P, 8, DK]),
                                ALU.mult).then_inc(sdecayed, 1)
            pool.wait_ge(st_sb, 1)
            for i in range(16):
                if i >= 2:
                    pool.wait_ge(sout_ps, i - 1)
                G.tensor_tensor(wide[:, i % 2, :].rearrange("p (a v) -> p a v", a=4),
                                kv_rows[:, 0, :].unsqueeze(1).to_broadcast([64, 4, DK]),
                                ident[0:64, 4 * i:4 * i + 4].unsqueeze(2).to_broadcast([64, 4, DK]),
                                ALU.mult).then_inc(st_sb, 1)
            pool.wait_ge(snew, 16)
            pool.dma_start(deltas_out, states[:, :, :]).then_inc(states_stored, 16)
            pool.wait_ge(s_sb, 4)
            pool.wait_ge(o_sb, 4)
            pool.dma_start(deltap_out, S_fin).then_inc(stored, 16)
            pool.wait_ge(stored, 64)
            pool.wait_ge(states_stored, 16)
            G.memset(small[:, 766:767], 0.0).then_inc(core_done, 1)
            pool.wait_ge(roped, 12)
            pool.wait_ge(aproj_sb, 16)
            pool.dma_start(kv_out, aq[:, 8:16, :]).then_inc(stored, 16)
            pool.wait_ge(normed, 5 * KT)
            pool.dma_start(y_out, hT[:, :, :]).then_inc(stored, 16)

        @block.vector
        def _(dve):
            steps = [0]

            def link(ins):
                steps[0] += 1
                ins.then_inc(dve_link, 1)
                dve.wait_ge(dve_link, steps[0])

            V = nc.vector

            def square_x(d, added, count):
                dve.wait_ge(added, count)
                V.tensor_tensor(hT[:, d, :], xT[:, d, :], xT[:, d, :], ALU.mult).then_inc(squares, 1)

            def norm(i, beside=lambda k: None):
                dve.wait_ge(root, i + 1)
                link(V.reciprocal(rms, rms))
                for k in range(KT):
                    V.scalar_tensor_tensor(out=hT[:, k, :], in0=xT[:, k, :], scalar=gain[:, i, k:k + 1], in1=rms,
                                           op0=ALU.mult, op1=ALU.mult).then_inc(normed, 1)
                    beside(k)

            dve.wait_ge(x_loaded, 16)
            dve.wait_ge(prm_loaded, 48)
            dve.wait_ge(consts_set, 1)
            for d in range(KT):
                square_x(d, x_loaded, 16)
            norm(0)

            def rest_of_input(k, norms):
                hi = gh_hi if norms == 0 else fh_hi
                dve.wait_ge(fh_hi_set, KT * norms + k + 1)
                V.tensor_tensor(fh_lo[:, k, :], hT[:, k, :], hi[:, k, :].bitcast(F32), ALU.subtract).then_inc(fh_lo_set, 1)

            def rest_of_in(p):
                dve.wait_ge(in_split_hi, p + 1)
                V.tensor_tensor(w_lo[:, p % SPLIT, :], raw_w[:, p % RAW, :], w_hi[:, p % SPLIT, :].bitcast(F32),
                                ALU.subtract).then_inc(in_split_lo, 1)

            dve.wait_ge(small_ready, 1)
            V.tensor_copy(small_T, bank[4][0:2 * H, 0:T]).then_inc(gates_a, 1)
            for k in range(KT):
                rest_of_input(k, 0)
            for p in range(SPLIT):
                rest_of_in(p)

            def gate_args():
                dve.wait_ge(small_ready, 2)
                V.tensor_copy(ba[:, 0:2, :], bank[4][:, 384:416].rearrange("p (i n) -> p i n", i=2))
                link(V.tensor_copy(ba[0:NS, 2, :], bank[4][0:NS, 416:432]))
                link(V.tensor_tensor(xg, xg, p_("dt_bias").unsqueeze(1).to_broadcast([P, 3, H]), ALU.add))
                V.scalar_tensor_tensor(out=t_abs, in0=xg, scalar=-1.0, in1=xg, op0=ALU.mult, op1=ALU.max).then_inc(gates_a, 1)

            def gates():
                dve.wait_ge(gates_e, 1)
                link(V.tensor_scalar(beta, beta, 1.0, None, ALU.add))
                V.reciprocal(beta, beta)
                link(V.scalar_tensor_tensor(out=gdec, in0=xg, scalar=0.0, in1=t_exp, op0=ALU.max, op1=ALU.add))
                link(V.scalar_tensor_tensor(out=gdec, in0=gdec, scalar=-1.0, in1=e_alog.unsqueeze(1).to_broadcast([P, 3, H]),
                                            op0=ALU.mult, op1=ALU.mult))
                V.tensor_copy(small[:, 767:768], small[:, 766:767]).then_inc(gates_done, 1)

            def take_cum():
                dve.wait_ge(cum_ps, 1)
                V.tensor_copy(cum, bank[4][:, 64:80].rearrange("p (c h) -> p c h", c=2))
                link(V.tensor_copy(e_end, bank[4][:, 80:96].rearrange("p (c h) -> p c h", c=2)))
                V.tensor_tensor(to_end, e_end, cum, ALU.subtract).then_inc(cum_sb, 1)

            def square(c):
                dve.wait_ge(silu_done, c + 1)
                V.tensor_tensor(nrm[:, c, 0:NPR], qkv[:, c, 0:NPR], qkv[:, c, 0:NPR], ALU.mult).then_inc(qk_sq, 1)

            xg = ba[:, :, H:2 * H]
            for c in range(QKV):
                if 2 <= c < 2 + 2 * H:
                    square(c - 2)
                if c == 7:
                    gate_args()
                if c == 8:
                    gates()
                if c == 15:
                    take_cum()
                if c == 22:
                    dve.wait_ge(qk_root, 1)
                    V.reciprocal(qk_rows, qk_rows).then_inc(qk_rows_set, 1)
                dve.wait_ge(raw_ready, c + 1)
                r, dst = raw[:, c % 2, :], qkv[:, c, 0:NPR]
                link(V.tensor_scalar(dst, r[:, 0:NPR], conv_w[:, c, 0:1], None, ALU.mult))
                for j in range(1, CONV_W):
                    ins = V.scalar_tensor_tensor(out=dst, in0=r[:, j:j + NPR], scalar=conv_w[:, c, j:j + 1], in1=dst,
                                                 op0=ALU.mult, op1=ALU.add)
                    if j < CONV_W - 1:
                        link(ins)
                    else:
                        ins.then_inc(conv_done, 1)
                if c % 2 == 1 and (c + 5) // 2 < IN_PIECES:
                    rest_of_in((c + 5) // 2)
            for c in range(2 * H):
                dve.wait_ge(qk_spread, c + 1)
                dve.wait_ge(silu_done, QKV)
                V.tensor_tensor(qkv[:, c, 0:NPR], qkv[:, c, 0:NPR], bank[6 + c % 2][:, 0:NPR], ALU.mult).then_inc(qk_normed, 1)
                if c == 1:
                    rest_of_in(IN_PIECES - 1)
                if c == 5:
                    dve.wait_ge(silu_done, QKV + 1)
                    s_qk = qkv[:, 0:2 * H, NPR:T]
                    V.tensor_tensor(s_sq.rearrange("p (c b) -> p c b", b=NS), s_qk, s_qk, ALU.mult).then_inc(qk_sq, 1)
            dve.wait_ge(qk_root, 2)
            link(V.reciprocal(s_rt, s_rt))
            V.tensor_tensor(s_qk, s_qk, s_rt.rearrange("p (c b) -> p c b", b=NS), ALU.mult).then_inc(qk_normed, 1)
            dve.wait_ge(qk_normed, 2 * H + 1)
            V.tensor_tensor(qk_.rearrange("p (h b) -> p h b", b=NS), qkv[:, 0:H, NPR:T], qkv[:, H:2 * H, NPR:T], ALU.mult)
            dve.wait_ge(cum_exp, 1)
            link(V.tensor_scalar(neg_ecum, neg_ecum, -1.0, None, ALU.mult))
            id8 = ident[0:NS, 0:NS].unsqueeze(1).to_broadcast([NS, H, NS])
            for r, src in ((0, beta[0:NS, 2, :]), (1, ge_s[0:NS, :])):
                ins = V.tensor_tensor(diag8[0:NS, r, :].rearrange("p (h b) -> p h b", b=NS),
                                      src.unsqueeze(2).to_broadcast([NS, H, NS]), id8, ALU.mult)
            ins.then_inc(sdiag, 1)
            for g in range(NG):
                dve.wait_ge(rowdec, g + 1)
                if g == 0:
                    dve.wait_ge(lmask_loaded, 16)
                for j in range(GRP):
                    c, h = (GRP * g + j) // H, (GRP * g + j) % H
                    ins = V.tensor_scalar(decT[:, g % 2, P * j:P * (j + 1)], bank[0][:, P * j:P * (j + 1)],
                                          cum[:, c, h:h + 1], 0.0, ALU.subtract, ALU.min)
                ins.then_inc(arg_done, 1)
                dve.wait_ge(dec_exp, g + 1)
                dve.wait_ge(kk_ready, g + 1)
                dm = decT[:, g % 2, :].rearrange("p (i n) -> p i n", i=GRP)
                link(V.tensor_tensor(dm, dm, upper.unsqueeze(1).to_broadcast([P, GRP, P]), ALU.mult))
                V.tensor_tensor(attT[:, GRP * g:GRP * (g + 1), :].rearrange("p i n -> p (i n)"), bank[2][:, :],
                                decT[:, g % 2, :], ALU.mult)
                for j in range(GRP):
                    i = GRP * g + j
                    ins = V.scalar_tensor_tensor(out=coefT[:, i, :], in0=bank[1][:, P * j:P * (j + 1)],
                                                 scalar=beta[:, i // H, i % H:i % H + 1],
                                                 in1=decT[:, g % 2, P * j:P * (j + 1)], op0=ALU.mult, op1=ALU.mult)
                ins.then_inc(coef_done, 1)
            dve.wait_ge(ecum_row, 2)
            V.tensor_tensor(qkv[:, 0:H, P:2 * P], qkv[:, 0:H, P:2 * P], Y[:, 0:H, :], ALU.mult).then_inc(q_dec_done, 1)
            dve.wait_ge(srow_ps, 1)
            dve.wait_ge(sread_ps, 1)
            V.tensor_copy(row_b.rearrange("p r n -> p (r n)"), bank[5][:, 0:128])
            link(V.tensor_copy(qk_, bank[5][:, 128:192]))
            read = bank[3][:, 0:128].rearrange("p (i r) -> p r i", r=2)
            link(V.tensor_tensor(sk, read[:, 1, :], row_b[:, 1, :], ALU.mult))
            V.tensor_tensor(sq_, read[:, 0, :], row_b[:, 1, :], ALU.mult).then_inc(su_done, 1)
            hb = lambda v: v.rearrange("p (h b) -> p h b", b=NS)
            link(V.tensor_tensor(hb(u_s), qkv[:, 2 * H:3 * H, NPR:T], hb(sk), ALU.subtract))
            link(V.tensor_tensor(u_s, u_s, row_b[:, 0, :], ALU.mult))
            V.tensor_copy(hb(sk), qkv[:, H:2 * H, NPR:T])
            link(V.tensor_tensor(qk_, qk_, u_s, ALU.mult))
            V.tensor_tensor(oT[:, :, NPR:T], hb(sq_), hb(qk_), ALU.add).then_inc(sou, 1)
            for l in range(LEVELS):
                if l == 3:
                    dve.wait_ge(turned_sb, 2 * NG)
                    for i in range(NI):
                        ins = V.tensor_scalar(ktok[:, i, :], ktok[:, i, :], to_end[:, i // H, i % H:i % H + 1], None, ALU.mult)
                    ins.then_inc(kdec_done, 1)
                for g in range(NG):
                    gi = slice(GRP * g, GRP * (g + 1))
                    dve.wait_ge(y_ps, NG * l + g + 1)
                    if l == 0 and g == 0:
                        dve.wait_ge(q_dec_done, 1)
                    V.tensor_tensor(Y[:, gi, :], bank[g][:, :].rearrange("p (i n) -> p i n", i=GRP),
                                    lmask[:, l:l + 1, :].to_broadcast([P, GRP, P]), ALU.mult).then_inc(y_sb, 1)
                for g in range(NG):
                    gi = slice(GRP * g, GRP * (g + 1))
                    fl = lambda v: v[:, gi, :].rearrange("p i n -> p (i n)")
                    if l == 0:
                        idw = ident.unsqueeze(1).to_broadcast([P, GRP, P])
                        dve.wait_ge(y_sb, g + 1)
                        V.tensor_tensor(X[:, gi, :], idw, Y[:, gi, :], ALU.subtract).then_inc(x_sb, 1)
                        dve.wait_ge(z_ps, g + 1)
                        V.tensor_tensor(Z[:, gi, :], idw, bank[6 + g % 2][:, :].rearrange("p (i n) -> p i n", i=GRP),
                                        ALU.subtract).then_inc(z_sb, 1)
                    else:
                        if l < LEVELS - 1:
                            dve.wait_ge(x_ps, NG * (l - 1) + g + 1)
                            V.tensor_tensor(fl(X), fl(X), bank[4 + g % 2][:, :], ALU.subtract).then_inc(x_sb, 1)
                        dve.wait_ge(z_ps, NG * l + g + 1)
                        V.tensor_tensor(fl(Z), fl(Z), bank[6 + g % 2][:, :], ALU.subtract).then_inc(z_sb, 1)
            for c in range(CH):
                if c == 1:
                    for g in range(2):
                        dve.wait_ge(ks_ps, g + 1)
                        for j in range(GRP):
                            h = GRP * g + j
                            ins = V.scalar_tensor_tensor(out=rhs_w[:, h, :], in0=bank[g][:, P * j:P * (j + 1)],
                                                         scalar=neg_ecum[:, 1, h:h + 1], in1=vtok[:, H + h, :],
                                                         op0=ALU.mult, op1=ALU.add)
                        ins.then_inc(w_sb, 1)
                for g in range(2):
                    dve.wait_ge(u_ps, 2 * c + g + 1)
                    if c == 1:
                        dve.wait_ge(o_ps, g + 1)
                    for j in range(GRP):
                        h = GRP * g + j
                        ins = V.tensor_scalar(u_tok[:, h, :], bank[2 + g][:, P * j:P * (j + 1)],
                                              beta[:, c, h:h + 1], None, ALU.mult)
                    ins.then_inc(u_sb, 1)
                for g in range(2):
                    dve.wait_ge(s_ps, 2 * c + g + 1)
                    if c == 0:
                        V.tensor_copy(S_new[:, GRP * g:GRP * (g + 1), :].rearrange("p i n -> p (i n)"),
                                      bank[4 + g][:, :]).then_inc(s_sb, 1)
                    else:
                        dve.wait_ge(s_sb, 2)
                        for j in range(GRP):
                            h = GRP * g + j
                            ins = V.scalar_tensor_tensor(out=S_fin[:, h, :], in0=S_new[:, h, :],
                                                         scalar=e_end[:, 1, h:h + 1], in1=bank[4 + g][:, P * j:P * (j + 1)],
                                                         op0=ALU.mult, op1=ALU.add)
                        ins.then_inc(s_sb, 1)
            dve.wait_ge(st_ps, 1)
            V.tensor_copy(kv_rows.rearrange("p r n -> p (r n)"), bank[0][0:64, 0:2 * P]).then_inc(st_sb, 1)
            for h in range(H):
                if h == 0:
                    dve.wait_ge(o_sb, 4)
                    dve.wait_ge(sou, 1)
                V.tensor_tensor(osq[:, h, :], oT[:, h, :], oT[:, h, :], ALU.mult).then_inc(osq_done, 1)
            for i in range(16):
                dve.wait_ge(sout_ps, i + 1)
                dve.wait_ge(sdecayed, i // 2 + 1)
                s = states[:, 4 * i:4 * i + 4, :].rearrange("p i n -> p (i n)")
                V.tensor_tensor(s, s, bank[2 + i % 2][:, :], ALU.add).then_inc(snew, 1)
            dve.wait_ge(osum, 1)
            link(V.scalar_tensor_tensor(out=oT, in0=oT, scalar=p_("o_gain"), in1=zT, op0=ALU.mult, op1=ALU.mult))
            dve.wait_ge(o_rows_set, 1)
            V.reciprocal(o_rows, o_rows).then_inc(o_rows_set, 1)
            for h in range(H):
                dve.wait_ge(oroot, h + 1)
                V.tensor_tensor(oT[:, h, :], oT[:, h, :], bank[h % 2][:, 0:T], ALU.mult).then_inc(o_normed, 1)

            def add_out(done, added):
                for d in range(KT + 1):
                    if d < KT:
                        dve.wait_ge(done, d + 1)
                        V.tensor_tensor(xT[:, d, :], xT[:, d, :], bank[4 + d % 4][:, 0:T], ALU.add).then_inc(added, 1)
                    if d >= 1:
                        square_x(d - 1, added, d)

            add_out(outp, out_added)
            def rest_of_piece(p):
                dve.wait_ge(f_split_hi, p + 1)
                V.tensor_tensor(w_lo[:, p % SPLIT, :], raw_w[:, p % F_RAW, :], w_hi[:, p % SPLIT, :].bitcast(F32),
                                ALU.subtract).then_inc(f_split_lo, 1)

            rest_of_piece(0)
            norm(1, lambda k: rest_of_input(k - 2, 1) if k >= 2 else None)
            rest_of_input(KT - 2, 1)
            rest_of_input(KT - 1, 1)

            def gated(f):
                dve.wait_ge(f_silu, f + 1)
                dve.wait_ge(f_used, f + 1)
                a = f_tmp[:, f % F_ACTS, :]
                V.tensor_tensor(a, a, bank[2 * (f % 2) + 1][:, 0:T], ALU.mult).then_inc(f_act, 1)

            def rest_of_act(f):
                dve.wait_ge(f_hi_set, f + 1)
                V.tensor_tensor(f_lo[:, f, :], f_tmp[:, f % F_ACTS, :], f_hi[:, f, :].bitcast(F32), ALU.subtract)\
                    .then_inc(f_lo_set, 1)

            def add_f(d):
                dve.wait_ge(f_used, FT + (FT * (d + 1) - 1) // F_TILES + 1)
                V.tensor_tensor(xT[:, d, :], xT[:, d, :], bank[4 + d % 3][:, 0:T], ALU.add).then_inc(f_added, 1)

            for p in range(1, SPLIT):
                rest_of_piece(p)
            added = 0
            for p in range(SPLIT, PIECES):
                if p < FT:
                    rest_of_piece(p)
                if 0 <= p - 4 < FT:
                    rest_of_act(p - 4)
                if 0 <= p - 3 < FT:
                    gated(p - 3)
                if p >= FT:
                    rest_of_piece(p)
                while added < KT and FT + (FT * (added + 1) - 1) // F_TILES <= p - SPLIT:
                    add_f(added)
                    if added >= 1:
                        square_x(added - 1, f_added, added)
                    added += 1
            for d in range(added, KT + 1):
                if d < KT:
                    add_f(d)
                square_x(d - 1, f_added, d)
            norm(2)
            dve.wait_ge(prm_loaded, 64)
            for c in range(12):
                a = aq[0:ROT, c, :]
                dve.wait_ge(rot_ps, c + 1)
                if c >= 1:
                    dve.wait_ge(roped, c)
                V.tensor_tensor(rot_t[0:ROT, :], bank[4 + c % 2][0:ROT, 0:T], sinT, ALU.mult)
                link(V.tensor_tensor(a, a, cosT, ALU.mult))
                V.tensor_tensor(a, a, rot_t[0:ROT, :], ALU.add).then_inc(roped, 1)
            dve.wait_ge(roped, 12)

            def p_max(h):
                dve.wait_ge(sc_ps, h + 1)
                if h >= 2:
                    dve.wait_ge(pT_ps, h - 1)
                i, m = h % 2, 2 * (h % 2)
                b = bank[4 + h % 2]
                V.scalar_tensor_tensor(out=pr_s[:, i, 0:P], in0=b[:, 0:P], scalar=SCALE, in1=causal, op0=ALU.mult, op1=ALU.add)
                V.tensor_scalar(pr_s[:, i, P:2 * P], b[:, P:2 * P], SCALE, None, ALU.mult)
                link(V.scalar_tensor_tensor(out=pr_s[:, i, 2 * P:3 * P], in0=b[:, 2 * P:3 * P], scalar=SCALE, in1=causal,
                                            op0=ALU.mult, op1=ALU.add))
                V.tensor_reduce(pmax[:, m:m + 1], pr_s[:, i, 0:P], AX, ALU.max)
                link(V.tensor_reduce(pmax[:, m + 1:m + 2], pr_s[:, i, P:3 * P], AX, ALU.max))
                V.tensor_scalar(pmax[:, m:m + 2], pmax[:, m:m + 2], -1.0, None, ALU.mult).then_inc(sc_max, 1)

            def p_scale(h):
                i, m = h % 2, 2 * (h % 2)
                dve.wait_ge(sc_exp, h + 1)
                link(V.reciprocal(prec[:, m:m + 2], psums[:, m:m + 2]))
                V.tensor_scalar(pr_s[:, i, 0:P], pr_s[:, i, 0:P], prec[:, m:m + 1], None, ALU.mult)
                V.tensor_scalar(pr_s[:, i, P:3 * P], pr_s[:, i, P:3 * P], prec[:, m + 1:m + 2], None, ALU.mult)\
                    .then_inc(p_sb, 1)

            for i in range(H + 1):
                if i == 0:
                    dve.wait_ge(aproj, 16)
                    link(V.memset(hflat, 0.0))
                    V.tensor_copy(q_own.rearrange("p b k r -> p k r b"),
                                  aq[:, 0:H, NPR:T].rearrange("p (k r) b -> p k r b", r=2)).then_inc(q_wide_set, 1)
                    V.tensor_tensor(prodn.rearrange("p (b k r) -> p k r b", k=KVH, r=2),
                                    aq[:, 0:H, NPR:T].rearrange("p (k r) b -> p k r b", r=2),
                                    aq[:, 8:12, NPR:T].unsqueeze(2).to_broadcast([P, KVH, 2, NS]), ALU.mult)\
                        .then_inc(prod_done, 1)
                if i >= 1:
                    p_scale(i - 1)
                if i < H:
                    p_max(i)
            dve.wait_ge(lnew_ps, 1)
            V.tensor_copy(l_new, bank[6][0:64, 0:1])
            V.tensor_reduce(kv_of_head, ident[0:8, 0:8].rearrange("p (k r) -> p k r", r=2), AX, ALU.add)
            for q in range(4):
                dve.wait_ge(k_read, 2 * NS - 1 + q // 2)
                t = bank[q][0:64, :].rearrange("p (n t) -> p n t", n=2)
                V.tensor_reduce(st_max[:, 2 * q:2 * q + 2], t, AX, ALU.max)
                ins = V.tensor_reduce(st_sum[:, 2 * q:2 * q + 2], t, AX, ALU.add)
            link(ins)
            other, own = st_sum.unsqueeze(1).to_broadcast([64, 8, 8]), st_sum.unsqueeze(2).to_broadcast([64, 8, 8])
            V.tensor_tensor(cmp_b, other, own, ALU.is_gt)
            link(V.tensor_tensor(eq_b, other, own, ALU.is_equal))
            link(V.tensor_tensor(eq_b, eq_b, before[0:64], ALU.mult))
            link(V.tensor_tensor(cmp_b, cmp_b, eq_b, ALU.add))
            link(V.tensor_reduce(pen, cmp_b, AX, ALU.add))
            link(V.tensor_scalar(pen, pen, float(TOPK) - 0.5, -BIG, ALU.is_gt, ALU.mult))
            link(V.tensor_tensor(st_max, st_max, pen, ALU.add))
            link(V.tensor_reduce(m_neg, st_max, AX, ALU.max))
            link(V.tensor_scalar(m_neg, m_neg, l_new, -SCALE, ALU.max, ALU.mult))
            V.tensor_scalar(biases, pen, m_neg, None, ALU.add).then_inc(bias_done, 1)
            dve.wait_ge(pexp, 1)
            link(V.tensor_reduce(r_den, sums, AX, ALU.add))
            link(V.tensor_tensor(r_den, r_den, p_new, ALU.add))
            link(V.reciprocal(r_den, r_den))
            link(V.tensor_scalar(rd_diag, ident[0:64, 0:64], r_den, None, ALU.mult))
            V.tensor_scalar(p_diag, rd_diag, p_new, None, ALU.mult).then_inc(diag_done, 1)
            dve.wait_ge(probT_ps, 3)
            V.tensor_tensor(o_new.rearrange("p b (k r) -> p k r b", r=2),
                            bank[7][:, 0:64].rearrange("p (b k r) -> p k r b", b=NS, r=2),
                            aq[:, 12:16, NPR:T].unsqueeze(2).to_broadcast([P, KVH, 2, NS]), ALU.mult)
            dve.wait_ge(po_ps, H)
            for b in range(NS):
                dve.wait_ge(v_read, 2 * (b + 1))
                if b >= 1:
                    dve.wait_ge(o8_done, b)
                link(V.tensor_tensor(o_wide, bank[b % 4][0:8, :].rearrange("p (k d) -> p k d", k=KVH),
                                     kv_of_head.unsqueeze(2).to_broadcast([8, KVH, DK]), ALU.mult))
                V.tensor_reduce(o8[:, b, :], o_wide.rearrange("p k d -> p d k"), AX, ALU.add).then_inc(o8_done, 1)
            dve.wait_ge(o8_turned, NS)
            V.tensor_tensor(o_att[:, :, NPR:T], bank[6][:, 0:64].rearrange("p (b h) -> p h b", h=H),
                            o_new.rearrange("p b h -> p h b"), ALU.add).then_inc(od_done, 1)
            add_out(aout, aout_added)

            def rest_of_weights(v, p):
                dve.wait_ge(split_hi, v * PIECES + (p + 1))
                V.tensor_tensor(w_lo[:, p % SPLIT, :], raw_w[:, p % RAW, :], w_hi[:, p % SPLIT, :].bitcast(F32),
                                ALU.subtract).then_inc(split_lo, 1)

            rest_of_weights(0, 0)
            norm(3)
            rest_of_weights(0, 1)
            dve.wait_ge(r_ps, 1)
            V.tensor_copy(rl[:, 0:2, :], bank[0][:, 0:16].rearrange("p (i e) -> p i e", i=2))
            link(V.tensor_copy(rl[0:NS, 2, :], bank[0][0:NS, 16:24]))
            r4 = lambda v: v.rearrange("p (t i) j -> p t i j", t=3)
            other, own = rl.unsqueeze(2).to_broadcast([P, 3, NE, NE]), rl.unsqueeze(3).to_broadcast([P, 3, NE, NE])
            V.tensor_tensor(r4(rcmp), other, own, ALU.is_gt)
            link(V.tensor_tensor(r4(req), other, own, ALU.is_equal))
            link(V.tensor_tensor(r4(req), r4(req), before.unsqueeze(1).to_broadcast([P, 3, NE, NE]), ALU.mult))
            link(V.tensor_tensor(rcmp, rcmp, req, ALU.add))
            link(V.tensor_reduce(rrank.rearrange("p t e -> p (t e)"), rcmp, AX, ALU.add))
            V.tensor_scalar(rrank, rrank, 1.5, None, ALU.is_lt)
            link(V.tensor_reduce(rmax, rl, AX, ALU.max))
            V.tensor_tensor(rgate[:, :, 0:NE], rl, rmax.unsqueeze(2).to_broadcast([P, 3, NE]), ALU.subtract).then_inc(r_arg, 1)
            rest_of_weights(0, 2)
            dve.wait_ge(r_exp, 1)
            rg = rgate[:, :, 0:NE]
            link(V.tensor_tensor(rg, rg, rrank, ALU.mult))
            link(V.tensor_reduce(rmax, rg, AX, ALU.add))
            link(V.reciprocal(rmax, rmax))
            V.tensor_tensor(rg, rg, rmax.unsqueeze(2).to_broadcast([P, 3, NE]), ALU.mult).then_inc(r_gate, 1)
            dve.wait_ge(pos_ps, 1)
            link(V.memset(rpos, -1.0))
            V.tensor_tensor(rpos[:, 0:2, 0:NE], bank[0][:, 32:32 + 2 * NE].rearrange("p (i e) -> p i e", i=2), rrank[:, 0:2, :],
                            ALU.mult)
            V.tensor_tensor(rpos[0:NS, 2, 0:NE], bank[0][0:NS, 32 + 2 * NE:32 + 3 * NE], rrank[0:NS, 2, :], ALU.mult)
            link(V.tensor_copy(counts[0:1, :], bank[0][0:1, 64:64 + NE]))
            link(V.tensor_scalar(rpos[:, :, 0:NE], rpos[:, :, 0:NE], -1.0, None, ALU.add))
            for rnd in range(1, ROUNDS):
                V.tensor_scalar(rpos[:, :, NE * rnd:NE * (rnd + 1)], rpos[:, :, 0:NE], -float(rnd * CAP), None, ALU.add)
                V.tensor_copy(rgate[:, :, NE * rnd:NE * (rnd + 1)], rg)
            V.memset(rgate[:, :, NE * ROUNDS:], 0.0)
            link(V.tensor_reduce(over[0:1, :], counts[0:1, :], AX, ALU.max))
            V.tensor_scalar(more[:, :], over[0:1, :], CAP + 0.5, None, ALU.is_gt).then_inc(over_set, 1)
            dve.wait_ge(over_set, 1)
            dve.wait_ge(stored, 16 * 5)

            def pick_tokens(v):
                at_v = slice(v, v + 1) if isinstance(v, int) else bass.ds(v, 1)
                for i, (t0, n) in enumerate(TOK_TILES):
                    V.tensor_scalar(pick_g[0:n, i, :], c_("slot_no")[0:n], rpos[0:n, i, at_v], rgate[0:n, i, at_v],
                                    ALU.is_equal, ALU.mult)
                    last = V.tensor_scalar(pick[0:n, i, :], c_("slot_no")[0:n], rpos[0:n, i, at_v], None, ALU.is_equal)
                last.then_inc(picked, 1)

            def rest_of_gathered(v):
                for half in range(2):
                    dve.wait_ge(xe_hi_set, v * 2 + (half + 1))
                    part = slice(4 * half, 4 * half + 4)
                    last = V.tensor_tensor(xe_lo[:, part, :].rearrange("p k n -> p (k n)"), bank[6 + half][:, :],
                                           xe_hi[:, part, :].rearrange("p k n -> p (k n)").bitcast(F32), ALU.subtract)
                last.then_inc(xe_lo_set, 1)

            def add_combined(v, d):
                dve.wait_ge(comb, v * KT + (d + 1))
                V.tensor_tensor(xT[:, d, :], xT[:, d, :], bank[4 + d % 2][:, 0:T], ALU.add).then_inc(comb_added, 1)

            def expert(v, first=False):
                for p in range(PIECES):
                    if not first or p >= SPLIT:
                        rest_of_weights(v, p)
                    if not first and 9 <= p < 9 + 2 * KT and p % 2 == 1:
                        add_combined(v - 1, (p - 9) // 2)
                    if p >= 6 and (p - 6) % 4 == 0 and (p - 6) // 4 < GROUPS:
                        j = (p - 6) // 4
                        dve.wait_ge(m_silu, v * GROUPS + (j + 1))
                        dve.wait_ge(piece_used, v * PIECES + (4 * j + 4))
                        if not first or j >= 2:
                            dve.wait_ge(act_turned, v * GROUPS + (j - 1 if j >= 2 else 0))
                        V.tensor_tensor(s_act[:, j % 2, :], s_sil[:, j % 2, :], bank[2 + j % 2][:, :], ALU.mult)\
                            .then_inc(m_act, 1)
                    if p % 4 == 0 and 3 <= p // 4 < 3 + GROUPS:
                        j = p // 4 - 3
                        dve.wait_ge(aT_hi_set, v * GROUPS + (j + 1))
                        part = slice(4 * j, 4 * j + 4)
                        V.tensor_tensor(aT_lo[:, part, :].rearrange("p f n -> p (f n)"), bank[6 + j % 2][:, :],
                                        aT_hi[:, part, :].rearrange("p f n -> p (f n)").bitcast(F32), ALU.subtract)\
                            .then_inc(aT_lo_set, 1)
                    if p == UP_PIECES:
                        dve.wait_ge(spread_ps, v + 1)
                        dve.wait_ge(gathered, v * 2 + 2)
                        pick_tokens(v + 1)
                    if p == PIECES - 1:
                        rest_of_gathered(v + 1)

            pick_tokens(0)
            rest_of_gathered(0)
            expert(0, first=True)
            with dve.Fori(1, NE) as e:
                expert(e)
            over_cap = dve.value_load(more[0:1, 0:1], min_val=0, max_val=1)
            with dve.If(over_cap == 0):
                for d in range(KT + 1):
                    if d < KT:
                        add_combined(NE - 1, d)
                    if d >= 1:
                        square_x(d - 1, comb_added, (NE - 1) * KT + d)
            with dve.Else():
                for rnd in range(1, ROUNDS):
                    with dve.Fori(0, NE) as e:
                        expert(e + NE * rnd)
                for d in range(KT + 1):
                    if d < KT:
                        add_combined(ROUNDS * NE - 1, d)
                    if d >= 1:
                        square_x(d - 1, comb_added, (ROUNDS * NE - 1) * KT + d)
            norm(4)


def _constants():
    r = np.arange(P)
    c = {
        "ident": np.eye(P), "ones": np.ones((P, P)), "upper": r[:, None] <= r[None, :],
        "causal": np.where(r[None, :] <= r[:, None], 0.0, -BIG),
        "before": np.tile((np.arange(8)[None, :] < np.arange(8)[:, None]).reshape(1, 64), (P, 1)),
        "eps": np.tile(np.array([[EPS, EPS * DK]]), (P, 1)), "slot_no": np.tile(np.arange(CAP)[None], (P, 1)),
        "sel": np.tile(np.arange(31)[None] == 15, (P, 1)), "sel_q": np.tile((np.arange(31)[None] == 15) * DK, (P, 1)),
        "eps_qk": np.where(r[:, None] < H, EPS * DK, EPS),
    }
    cst = np.concatenate([np.asarray(c[n], np.float32) for n in CST], axis=1)
    masks = []
    for level in range(LEVELS):
        s = 1 << level
        same = (r[:, None] // (2 * s)) == (r[None, :] // (2 * s))
        masks.append(same & ((r[:, None] // s) % 2 == 1) & ((r[None, :] // s) % 2 == 0))
    lmask = np.stack(masks, axis=1).reshape(P, LEVELS * P).astype(np.float32)
    half = ROT // 2
    rot = np.zeros((P, ROT), np.float32)
    rot[np.arange(half) + half, np.arange(half)] = -1.0
    rot[np.arange(half), np.arange(half) + half] = 1.0
    inv = np.power(np.float32(500000.0), -np.arange(half, dtype=np.float32) * np.float32(2.0 / ROT))
    pos = np.concatenate([np.arange(NPR), np.full(NS, POS0)]).astype(np.float32)
    ang = np.tile((pos[None, :] * inv[:, None]).astype(np.float32), (2, 1))
    rope = np.zeros((P, ROPE_N), np.float32)
    rope[:, :ROT] = rot
    rope[:ROT, ROT:ROT + T] = np.cos(ang)
    rope[:ROT, ROT + T:] = np.sin(ang)
    return cst, lmask, rope


def kernel(**inputs):
    import numpy as _np
    import concourse.bacc as _bacc
    from concourse import mybir as _mybir
    from concourse.bass_utils import run_bass_kernel_spmd as _run

    a = {k: _np.asarray(v) for k, v in inputs.items()}
    cont = _np.ascontiguousarray

    def columns(w, per_chunk):
        k, n = w.shape
        t = w.reshape(k // P, P, n // (P * per_chunk), per_chunk, P).transpose(2, 1, 3, 0, 4)
        return cont(t.reshape(t.shape[0], P, -1))

    def gate_up(g, u):
        parts = [w.reshape(KT, P, FT, P).transpose(2, 1, 0, 3) for w in (g, u)]
        return _np.stack(parts, axis=2).reshape(FT, P, PIECE)

    def down(w):
        tiles = w.reshape(FT, P, KT, P).transpose(2, 0, 1, 3).reshape(-1, F_TILES, P, P)
        return tiles.transpose(0, 2, 1, 3).reshape(-1, P, PIECE)

    def experts(g, u, w):
        wide = _np.stack([m.reshape(NE, 2, KT // 2, P, GROUPS, N).transpose(0, 4, 1, 3, 2, 5) for m in (g, u)], axis=2)
        tall = w.reshape(NE, FT // F_PIECE, F_PIECE, P, D).transpose(0, 1, 3, 2, 4)
        return _np.concatenate([wide.reshape(NE, UP_PIECES, P, PIECE), tall.reshape(NE, -1, P, PIECE)], axis=1)\
            .reshape(NE * PIECES, P, PIECE)

    x = _np.concatenate([a["x_prompt"][0], a["x_sample"][:, 0]], axis=0)
    cst, lmask, rope = _constants()
    gains = _np.stack([a["norm_mix"][0], a["norm_ffn"][0], a["norm_mix"][1], a["norm_ffn"][1], a["norm_final"]])
    w_in = a["gdn_w_in"][0]
    n_wide = (QKV + H) * P
    prm = {
        "gain": gains.reshape(5, KT, P).transpose(2, 0, 1), "o_gain": a["gdn_o_norm"][0][:, None],
        "conv_w": a["gdn_conv_w"][0].reshape(CONV_W, QKV, P).transpose(2, 1, 0),
        "a_log": _np.tile(a["gdn_a_log"][0][None], (P, 1)), "dt_bias": _np.tile(a["gdn_dt_bias"][0][None], (P, 1)),
        "router": a["moe_router"][0].reshape(KT, P, NE).transpose(1, 0, 2),
        "w_small": w_in[:, n_wide:].reshape(KT, P, 2 * H).transpose(1, 0, 2),
    }
    given = {
        "x": x.reshape(T, KT, P).transpose(2, 1, 0),
        "cst": cst, "lmask": lmask, "rope": rope,
        "prm": _np.concatenate([prm[n].reshape(P, -1) for n in PRM], axis=1),
        "conv": a["state_conv"][0].reshape(NS, CONV_W - 1, QKV, P).transpose(3, 2, 1, 0),
        "table": a["page_table"].reshape(1, -1),
        "gdn_in": columns(w_in[:, :n_wide], 2),
        "state": a["state_delta"][0].transpose(2, 1, 0, 3).reshape(DK, 2, SLOT).transpose(1, 0, 2),
        "gdn_out": columns(a["gdn_w_out"][0], 4),
        "ffn_w": _np.concatenate([gate_up(a["ffn_w_gate"], a["ffn_w_up"]), down(a["ffn_w_down"])]),
        "att_in": columns(a["att_w_in"][0], 4),
        "k_pages": a["cache_k"][0].transpose(0, 3, 2, 1).reshape(-1, P, KVH * PAGE),
        "v_pages": a["cache_v"][0].reshape(-1, PAGE, KVH * DK),
        "att_out": columns(a["att_w_out"][0], 4),
        "moe": experts(a["moe_w_gate"][0], a["moe_w_up"][0], a["moe_w_down"][0]),
    }
    outs = {"y": (P, KT, T), "convp": (P, QKV, CONV_W - 1), "convs": (P, QKV, CONV_W - 1, NS),
            "deltap": (P, H, DK), "deltas": (P, H * NS, DK), "kv": (P, 2 * KVH, T)}

    nc = _bacc.Bacc("TRN2", target_bir_lowering=False, num_devices=1)
    arrays, args = {}, []
    for name, v in given.items():
        arrays[f"in_{name}"] = cont(v)
        args.append(nc.dram_tensor(f"in_{name}", v.shape, _mybir.dt.from_np(v.dtype), kind="ExternalInput").ap())
    for name, shape in outs.items():
        args.append(nc.dram_tensor(f"out_{name}", shape, F32, kind="ExternalOutput").ap())
    program(nc, *args)
    r = _run(nc, [arrays], core_ids=[0]).results[0]
    y = r["out_y"].transpose(2, 1, 0).reshape(T, D)
    kv = r["out_kv"].transpose(2, 1, 0)
    convs = r["out_convs"].transpose(3, 2, 1, 0).reshape(1, NS, CONV_W - 1, QKV * P)
    deltas = r["out_deltas"].reshape(DK, H, NS, DK).transpose(2, 1, 0, 3)[None]
    return (y[None, :NPR], y[NPR:, None],
            r["out_convp"].transpose(2, 1, 0).reshape(1, 1, CONV_W - 1, QKV * P),
            r["out_deltap"].transpose(1, 0, 2)[None, None],
            kv[None, None, :NPR, :KVH], kv[None, None, :NPR, KVH:],
            convs, deltas, kv[None, NPR:, None, :KVH], kv[None, NPR:, None, KVH:])
```
